# Optimizing a Trainium2 kernel written in Bass

```python
import math
import jax
import jax.numpy as jnp
from jax import lax
import numpy as np

D_MODEL = 1024
BATCH = 1
SEQ = 512
DEPTH = 2

GRID_W = 64
CTX_LEN = 256
EPS = 1e-6
ROPE_THETA = 10000.0
N_BRANCHES = 4
BRANCH_WIDTH = D_MODEL // 2
D_FF = 4 * D_MODEL

SSM_HEAD_DIM = 64
SSM_HEADS = BRANCH_WIDTH // SSM_HEAD_DIM
SSM_D_INNER = SSM_HEADS * SSM_HEAD_DIM
SSM_GROUPS = 2
SSM_HPG = SSM_HEADS // SSM_GROUPS
SSM_STATE = 128
SSM_CONV = 5
SSM_CHUNK = 128
SSM_XBC = SSM_D_INNER + 2 * SSM_GROUPS * SSM_STATE

SC_WIDTH = BRANCH_WIDTH
SC_CONV = 3

MLA_HEADS = 8
MLA_NOPE = 64
MLA_ROPE = 32
MLA_V = BRANCH_WIDTH // MLA_HEADS
MLA_Q_RANK = 384
MLA_KV_RANK = 256
ATTN_BLOCK = 128

FNET_GROUPS = 4
FNET_GROUP_DIM = BRANCH_WIDTH // FNET_GROUPS

IN_SIZES = (SSM_D_INNER, SSM_XBC, 2 * SSM_HEADS, 3 * SC_WIDTH, MLA_Q_RANK, MLA_KV_RANK, MLA_ROPE, BRANCH_WIDTH, N_BRANCHES * D_MODEL)
IN_SPLITS = tuple(int(v) for v in np.cumsum(IN_SIZES)[:-1])
D_IN = int(sum(IN_SIZES))

kernel_name = 'hybrid_ssd_conv_mla_fourier_dit_block'

def rmsnorm(x, g):
    xf = x.astype(jnp.float32)
    y = xf * lax.rsqrt(jnp.mean(xf * xf, axis=-1, keepdims=True) + EPS)
    return (y * g.astype(jnp.float32)).astype(x.dtype)

def modulate(h, shift, scale):
    return h * (1 + scale) + shift

def dwconv(u, w):
    pad = (w.shape[0] - 1) // 2
    return lax.conv_general_dilated(u, w[:, None, :].astype(u.dtype), window_strides=(1,), padding=[(pad, pad)], dimension_numbers=('NWC', 'WIO', 'NWC'), feature_group_count=u.shape[-1])

def axial_rope(n_tokens):
    rows = n_tokens // GRID_W
    row = jnp.repeat(jnp.arange(rows, dtype=jnp.float32), GRID_W)
    col = jnp.tile(jnp.arange(GRID_W, dtype=jnp.float32), rows)
    n_freq = MLA_ROPE // 4
    inv = ROPE_THETA ** (-jnp.arange(n_freq, dtype=jnp.float32) / n_freq)
    ang = jnp.stack([row[:, None] * inv, col[:, None] * inv], axis=1)
    return jnp.cos(ang), jnp.sin(ang)

def rope2d(x, cos, sin):
    xs = x.astype(jnp.float32).reshape(x.shape[:-1] + (2, 2, MLA_ROPE // 4))
    x1, x2 = xs[..., 0, :], xs[..., 1, :]
    out = jnp.stack([x1 * cos - x2 * sin, x1 * sin + x2 * cos], axis=-2)
    return out.reshape(x.shape).astype(x.dtype)

def ssd_scan(x, dt, a, b, c, h0, want_y):
    f32 = jnp.float32
    bsz, n = x.shape[:2]
    nc, q = n // SSM_CHUNK, SSM_CHUNK
    xdt = (x.astype(f32) * dt[..., None]).reshape(bsz, nc, q, SSM_GROUPS, SSM_HPG, SSM_HEAD_DIM)
    bm = b.astype(f32).reshape(bsz, nc, q, SSM_GROUPS, SSM_STATE)
    cm = c.astype(f32).reshape(bsz, nc, q, SSM_GROUPS, SSM_STATE)
    la = (dt * a).reshape(bsz, nc, q, SSM_GROUPS, SSM_HPG)
    cum = jnp.cumsum(la, axis=2)
    states = jnp.einsum('bcjgn,bcjgr,bcjgrp->bcgrpn', bm, jnp.exp(cum[:, :, -1:] - cum), xdt)
    chunk_decay = jnp.exp(cum[:, :, -1])

    def step(h, inp):
        s, d = inp
        return h * d[..., None, None] + s, h

    h_final, h_prev = lax.scan(step, h0.reshape(bsz, SSM_GROUPS, SSM_HPG, SSM_HEAD_DIM, SSM_STATE), (jnp.moveaxis(states, 1, 0), jnp.moveaxis(chunk_decay, 1, 0)))
    h_final = h_final.reshape(bsz, SSM_HEADS, SSM_HEAD_DIM, SSM_STATE)
    if not want_y:
        return None, h_final
    h_prev = jnp.moveaxis(h_prev, 0, 1)
    lower = jnp.tril(jnp.ones((q, q), dtype=bool))[:, :, None, None]
    seg = jnp.exp(jnp.where(lower, cum[:, :, :, None] - cum[:, :, None, :], -jnp.inf))
    cb = jnp.einsum('bcign,bcjgn->bcijg', cm, bm)
    y_diag = jnp.einsum('bcijg,bcijgr,bcjgrp->bcigrp', cb, seg, xdt)
    y_off = jnp.einsum('bcign,bcigr,bcgrpn->bcigrp', cm, jnp.exp(cum), h_prev)
    return (y_diag + y_off).reshape(bsz, n, SSM_HEADS, SSM_HEAD_DIM), h_final

def ssd_stream(z, xbc, dt_raw, h_init, conv_w, conv_b, a_log, dt_bias, d_skip, norm_g, want_y):
    f32 = jnp.float32
    bsz, n = z.shape[:2]
    xbc = jax.nn.silu(dwconv(xbc, conv_w) + conv_b.astype(xbc.dtype))
    xs, bmat, cmat = jnp.split(xbc, [SSM_D_INNER, SSM_D_INNER + SSM_GROUPS * SSM_STATE], axis=-1)
    xs = xs.reshape(bsz, n, SSM_HEADS, SSM_HEAD_DIM)
    bmat = bmat.reshape(bsz, n, SSM_GROUPS, SSM_STATE)
    cmat = cmat.reshape(bsz, n, SSM_GROUPS, SSM_STATE)
    a = -jnp.exp(a_log.astype(f32))
    dt = jax.nn.softplus(dt_raw.astype(f32).reshape(bsz, n, 2, SSM_HEADS) + dt_bias.astype(f32))
    flip = lambda t: jnp.flip(t, axis=1)
    y_f, h_f = ssd_scan(xs, dt[:, :, 0], a[0], bmat, cmat, h_init[0], want_y)
    y_b, h_b = ssd_scan(flip(xs), flip(dt[:, :, 1]), a[1], flip(bmat), flip(cmat), h_init[1], want_y)
    if not want_y:
        return None, (h_f, h_b)
    y = y_f + flip(y_b) + d_skip.astype(f32)[:, None] * xs.astype(f32)
    y = y.reshape(bsz, n, SSM_D_INNER) * jax.nn.silu(z.astype(f32))
    y = rmsnorm(y.reshape(bsz, n, SSM_GROUPS, SSM_D_INNER // SSM_GROUPS), norm_g.reshape(SSM_GROUPS, -1))
    return y.reshape(bsz, n, SSM_D_INNER).astype(z.dtype), (h_f, h_b)

def short_conv(u, conv_w):
    bg, cg, xin = jnp.split(u, 3, axis=-1)
    return bg * dwconv(cg * xin, conv_w)

def mla_q(q_a, qa_g, w_qb, cos, sin):
    bsz, n = q_a.shape[:2]
    q = (rmsnorm(q_a, qa_g) @ w_qb).reshape(bsz, n, MLA_HEADS, MLA_NOPE + MLA_ROPE)
    q_nope, q_rope = q[..., :MLA_NOPE], q[..., MLA_NOPE:]
    if cos is not None:
        q_rope = rope2d(q_rope, cos[:, None], sin[:, None])
    return q_nope, q_rope

def mla_kv(kv_a, k_r, kva_g, w_kvb, cos, sin):
    bsz, n = kv_a.shape[:2]
    kv = (rmsnorm(kv_a, kva_g) @ w_kvb).reshape(bsz, n, MLA_HEADS, MLA_NOPE + MLA_V)
    k_rope = k_r if cos is None else rope2d(k_r, cos, sin)
    return kv[..., :MLA_NOPE], k_rope, kv[..., MLA_NOPE:]

def block_attention(q_nope, q_rope, k_nope, k_rope, v):
    bsz, lq = q_nope.shape[:2]
    nb = lq // ATTN_BLOCK
    scale = (MLA_NOPE + MLA_ROPE) ** -0.5

    def one_block(qs):
        qn, qr = qs
        s = jnp.einsum('bqhd,bkhd->bhqk', qn, k_nope, preferred_element_type=jnp.float32) + jnp.einsum('bqhr,bkr->bhqk', qr, k_rope, preferred_element_type=jnp.float32)
        p = jax.nn.softmax(s * scale, axis=-1)
        return jnp.einsum('bhqk,bkhd->bqhd', p.astype(v.dtype), v)

    blocks = lambda t: jnp.moveaxis(t.reshape((bsz, nb, ATTN_BLOCK) + t.shape[2:]), 1, 0)
    o = lax.map(one_block, (blocks(q_nope), blocks(q_rope)))
    return jnp.moveaxis(o, 0, 1).reshape(bsz, lq, MLA_HEADS * MLA_V)

def fourier_mix(u):
    bsz, n = u.shape[:2]
    g = u.astype(jnp.float32).reshape(bsz, n, FNET_GROUPS, FNET_GROUP_DIM)
    return jnp.fft.fft2(g, axes=(1, 3), norm='ortho').real.reshape(bsz, n, BRANCH_WIDTH).astype(u.dtype)

def merge_branches(branches, gate_logits, w_branch, w_out):
    bsz, n = gate_logits.shape[:2]
    gates = jax.nn.sigmoid(gate_logits.astype(jnp.float32)).astype(gate_logits.dtype).reshape(bsz, n, N_BRANCHES, D_MODEL)
    merged = gates[:, :, 0] * (branches[0] @ w_branch[0])
    for k in range(1, N_BRANCHES):
        merged = merged + gates[:, :, k] * (branches[k] @ w_branch[k])
    return merged @ w_out

def hybrid_mixer(h_ctx, h_lat, cos, sin, w_in, ssm_conv_w, ssm_conv_b, ssm_a_log, ssm_dt_bias, ssm_d, ssm_norm_g, sc_conv_w, mla_qa_g, mla_wqb, mla_kva_g, mla_wkvb, w_branch, w_out, need_ctx):
    zc, xbcc, dtc, scc, qac, kvac, krc, fnc, gtc = jnp.split(h_ctx @ w_in, IN_SPLITS, axis=-1)
    zl, xbcl, dtl, scl, qal, kval, krl, fnl, gtl = jnp.split(h_lat @ w_in, IN_SPLITS, axis=-1)
    h0 = jnp.zeros((h_ctx.shape[0], SSM_HEADS, SSM_HEAD_DIM, SSM_STATE), jnp.float32)
    y_ssm_c, ctx_states = ssd_stream(zc, xbcc, dtc, (h0, h0), ssm_conv_w, ssm_conv_b, ssm_a_log, ssm_dt_bias, ssm_d, ssm_norm_g, need_ctx)
    y_ssm_l, _ = ssd_stream(zl, xbcl, dtl, ctx_states, ssm_conv_w, ssm_conv_b, ssm_a_log, ssm_dt_bias, ssm_d, ssm_norm_g, True)
    kn_c, kr_c, v_c = mla_kv(kvac, krc, mla_kva_g, mla_wkvb, None, None)
    kn_l, kr_l, v_l = mla_kv(kval, krl, mla_kva_g, mla_wkvb, cos, sin)
    qn_l, qr_l = mla_q(qal, mla_qa_g, mla_wqb, cos, sin)
    att_l = block_attention(qn_l, qr_l, jnp.concatenate([kn_c, kn_l], axis=1), jnp.concatenate([kr_c, kr_l], axis=1), jnp.concatenate([v_c, v_l], axis=1))
    out_l = merge_branches((y_ssm_l, short_conv(scl, sc_conv_w), att_l, fourier_mix(fnl)), gtl, w_branch, w_out)
    if not need_ctx:
        return None, out_l
    qn_c, qr_c = mla_q(qac, mla_qa_g, mla_wqb, None, None)
    att_c = block_attention(qn_c, qr_c, kn_c, kr_c, v_c)
    out_c = merge_branches((y_ssm_c, short_conv(scc, sc_conv_w), att_c, fourier_mix(fnc)), gtc, w_branch, w_out)
    return out_c, out_l

def sq_relu_mlp(h, w1, w2):
    return jnp.square(jax.nn.relu(h @ w1)) @ w2

def setup_inputs(seed: int = 0) -> dict:
    key = jax.random.key(seed)
    ks = jax.random.split(key, 32)
    f32 = jnp.float32

    def nrm(k, shape, std):
        return jax.random.normal(k, shape, f32) * std

    def gain(k, shape):
        return 1.0 + 0.02 * jax.random.normal(k, shape, f32)

    dt0 = jnp.exp(jax.random.uniform(ks[10], (DEPTH, 2, SSM_HEADS), f32, math.log(1e-3), math.log(1e-1)))
    return {
        'x': nrm(ks[0], (BATCH, SEQ, D_MODEL), 1.0),
        'c': nrm(ks[1], (BATCH, D_MODEL), 1.0),
        'ctx': nrm(ks[2], (BATCH, CTX_LEN, D_MODEL), 1.0),
        'c_ctx': nrm(ks[3], (D_MODEL,), 1.0),
        'ada_w': nrm(ks[4], (DEPTH, D_MODEL, 6 * D_MODEL), 0.25 * D_MODEL ** -0.5),
        'ada_b': nrm(ks[5], (DEPTH, 6 * D_MODEL), 0.01),
        'norm1_g': gain(ks[6], (DEPTH, D_MODEL)),
        'norm2_g': gain(ks[7], (DEPTH, D_MODEL)),
        'w_in': nrm(ks[8], (DEPTH, D_MODEL, D_IN), D_MODEL ** -0.5),
        'ssm_conv_w': nrm(ks[9], (DEPTH, SSM_CONV, SSM_XBC), SSM_CONV ** -0.5),
        'ssm_conv_b': nrm(ks[11], (DEPTH, SSM_XBC), 0.01),
        'ssm_a_log': jnp.log(jax.random.uniform(ks[12], (DEPTH, 2, SSM_HEADS), f32, 1.0, 16.0)),
        'ssm_dt_bias': dt0 + jnp.log(-jnp.expm1(-dt0)),
        'ssm_d': 1.0 + nrm(ks[13], (DEPTH, SSM_HEADS), 0.1),
        'ssm_norm_g': gain(ks[14], (DEPTH, SSM_D_INNER)),
        'sc_conv_w': nrm(ks[15], (DEPTH, SC_CONV, SC_WIDTH), SC_CONV ** -0.5),
        'mla_qa_g': gain(ks[16], (DEPTH, MLA_Q_RANK)),
        'mla_wqb': nrm(ks[17], (DEPTH, MLA_Q_RANK, MLA_HEADS * (MLA_NOPE + MLA_ROPE)), MLA_Q_RANK ** -0.5),
        'mla_kva_g': gain(ks[18], (DEPTH, MLA_KV_RANK)),
        'mla_wkvb': nrm(ks[19], (DEPTH, MLA_KV_RANK, MLA_HEADS * (MLA_NOPE + MLA_V)), MLA_KV_RANK ** -0.5),
        'w_branch': nrm(ks[20], (DEPTH, N_BRANCHES, BRANCH_WIDTH, D_MODEL), BRANCH_WIDTH ** -0.5),
        'w_out': nrm(ks[21], (DEPTH, D_MODEL, D_MODEL), D_MODEL ** -0.5),
        'mlp_w1': nrm(ks[22], (DEPTH, D_MODEL, D_FF), D_MODEL ** -0.5),
        'mlp_w2': nrm(ks[23], (DEPTH, D_FF, D_MODEL), D_FF ** -0.5),
        'final_norm_g': gain(ks[24], (D_MODEL,)),
    }

def reference(x, c, ctx, c_ctx, ada_w, ada_b, norm1_g, norm2_g, w_in, ssm_conv_w, ssm_conv_b, ssm_a_log, ssm_dt_bias, ssm_d, ssm_norm_g, sc_conv_w, mla_qa_g, mla_wqb, mla_kva_g, mla_wkvb, w_branch, w_out, mlp_w1, mlp_w2, final_norm_g):
    cos, sin = axial_rope(x.shape[1])
    x_lat, x_ctx = x, ctx
    for i in range(DEPTH):
        need_ctx = i < DEPTH - 1
        mod_lat = (jax.nn.silu(c) @ ada_w[i] + ada_b[i])[:, None, :]
        mod_ctx = jax.nn.silu(c_ctx) @ ada_w[i] + ada_b[i]
        sh1, sc1, g1, sh2, sc2, g2 = jnp.split(mod_lat, 6, axis=-1)
        csh1, csc1, cg1, csh2, csc2, cg2 = jnp.split(mod_ctx, 6, axis=-1)
        h_lat = modulate(rmsnorm(x_lat, norm1_g[i]), sh1, sc1)
        h_ctx = modulate(rmsnorm(x_ctx, norm1_g[i]), csh1, csc1)
        o_ctx, o_lat = hybrid_mixer(h_ctx, h_lat, cos, sin, w_in[i], ssm_conv_w[i], ssm_conv_b[i], ssm_a_log[i], ssm_dt_bias[i], ssm_d[i], ssm_norm_g[i], sc_conv_w[i], mla_qa_g[i], mla_wqb[i], mla_kva_g[i], mla_wkvb[i], w_branch[i], w_out[i], need_ctx)
        x_lat = x_lat + g1 * o_lat
        x_lat = x_lat + g2 * sq_relu_mlp(modulate(rmsnorm(x_lat, norm2_g[i]), sh2, sc2), mlp_w1[i], mlp_w2[i])
        if need_ctx:
            x_ctx = x_ctx + cg1 * o_ctx
            x_ctx = x_ctx + cg2 * sq_relu_mlp(modulate(rmsnorm(x_ctx, norm2_g[i]), csh2, csc2), mlp_w1[i], mlp_w2[i])
    return rmsnorm(x_lat, final_norm_g)


_drawn_inputs = setup_inputs


def setup_inputs(seed=0):
    import zlib

    import numpy as np

    out = dict(_drawn_inputs(seed))
    spreads = {}
    factors = {'ctx': 8.0,
     'c_ctx': 8.0,
     'norm1_g': 8.0,
     'norm2_g': 45.574,
     'ssm_conv_b': 200.0,
     'ssm_d': 200.0,
     'ssm_norm_g': 200.0,
     'mla_qa_g': 22.73,
     'mla_wqb': 6.424,
     'mla_kva_g': 23.702,
     'mla_wkvb': 3.393,
     'final_norm_g': 23.427,
     'ssm_a_log': 8.0,
     'ssm_dt_bias': 7.128}
    for name, (base, spread) in spreads.items():
        noise = np.random.default_rng([zlib.crc32(name.encode()), seed]).standard_normal(out[name].shape)
        drawn = base * np.exp(spread * noise) if base else spread * noise
        out[name] = jnp.asarray(drawn.astype(out[name].dtype))
    for name, factor in factors.items():
        out[name] = (out[name] * factor).astype(out[name].dtype)
    return out
```

```python
from contextlib import ExitStack

import numpy as np

import concourse.bass as bass
from concourse import mybir

P = 128
D = 1024
CTX = 256
LAT = 512
TOK = CTX + LAT
NT = TOK // P
GRID_W = 64
DEPTH = 2
DFF = 4 * D
EPS = 1e-6
BW = D // 2
KD = D // P
KB = BW // P
HEADS = 8
SSM_HD = 64
STATE = 128
NOPE, ROPE, VD = 64, 32, 64
QR, KVR = 384, 256
QH = NOPE + ROPE
SCALE = float(QH) ** -0.5
Z0 = 0
XBC0 = Z0 + BW
DT0 = XBC0 + 1024
SC0 = DT0 + 16
QA0 = SC0 + 3 * BW
KVA0 = QA0 + QR
KR0 = KVA0 + KVR
FN0 = KR0 + ROPE
GT0 = FN0 + BW
WT = 1024
NRAW = 3
NSLOT = 4
HALF = 512
T0 = HALF - CTX

F32 = mybir.dt.float32
F32R = mybir.dt.float32r
ALU = mybir.AluOpType
ACT = mybir.ActivationFunctionType
AX = mybir.AxisListType

SUM_BLOCK = 16
ROWS = NT * 8
C_ID, C_U, C_L, C_KEEP, C_ROT, C_SEL, C_CHAN = 0, 128, 256, 384, 512, 640, 642
C_COS = C_CHAN + 256
C_SIN = C_COS + TOK
C_ALL = C_SIN + TOK
R_CW, R_CB, R_N1, R_N2, R_SN, R_SW, R_QG, R_KG, R_FG, R_C, R_CC, R_END = 0, 40, 48, 56, 64, 68, 80, 83, 85, 93, 101, 109


def constant_tables():
    t = np.zeros((P, C_ALL), np.float32)
    i = np.arange(P)
    t[:, C_ID:C_ID + P] = np.eye(P)
    t[:, C_U:C_U + P] = i[:, None] <= i[None, :]
    t[:, C_L:C_L + P] = i[:, None] >= i[None, :]
    t[:, C_KEEP:C_KEEP + P] = i[None, :] % SUM_BLOCK != 0
    nf = ROPE // 4
    for half in range(2):
        for f in range(nf):
            a = NOPE + 2 * nf * half + f
            t[a + nf, C_ROT + a] = -1.0
            t[a, C_ROT + a + nf] = 1.0
    for r in range(4):
        t[r, C_SEL + r % 2] = 1.0
    w = 2 * np.pi * np.outer(i, i) / P
    t[:, C_CHAN:C_CHAN + P] = np.cos(w)
    t[:, C_CHAN + P:C_CHAN + 2 * P] = np.sin(w)
    tok = np.arange(LAT)
    inv = 10000.0 ** (-np.arange(nf) / nf)
    for half, pos in enumerate((tok // GRID_W, tok % GRID_W)):
        ang = inv[:, None] * pos[None, :]
        for part in range(2):
            a = NOPE + 2 * nf * half + nf * part
            t[a:a + nf, C_COS + CTX:C_COS + TOK] = np.cos(ang)
            t[a:a + nf, C_SIN + CTX:C_SIN + TOK] = np.sin(ang)
    t[NOPE:QH, C_COS:C_COS + CTX] = 1.0
    j = np.arange(LAT)
    w = 2 * np.pi * ((j[:, None] * j[None, :]) % LAT) / LAT
    dft = np.stack([np.cos(w), -np.sin(w)]).astype(np.float32)
    return t, dft


class Counts:

    def __init__(self, nc, ctx, known):
        self.nc, self.ctx, self.known, self.now, self.sems = nc, ctx, known or {}, {}, {}
        self.table, self.last = {}, None

    def sem(self, name):
        if name not in self.sems:
            self.sems[name] = self.ctx.enter_context(self.nc.semaphore(name))
            self.now[name] = 0
        return self.sems[name]

    def does(self, name, key=None, by=1):
        sem = self.sem(name)
        self.now[name] += by
        self.table[name, key] = self.now[name]
        self.last = sem, self.now[name]
        return sem, by

    def when(self, name, key):
        at = self.table.get((name, key)) or self.known.get((name, key))
        assert at or not self.known, (name, key)
        return self.sem(name), at or 1

    def mine(self):
        return self.last


def backbone(nc, A, out, known):
    ctx = ExitStack()
    with ctx:
        counts = Counts(nc, ctx, known)
        when, does, last_ = counts.when, counts.does, counts.mine

        def sb(name, shape, dt=F32, scope=ctx):
            return scope.enter_context(nc.sbuf_tensor(name, shape, dt))

        cst = sb("cst", [P, C_ALL])
        par = sb("par", [P, DEPTH, P])
        adab = sb("adab", [P, DEPTH, 48])
        mods = sb("mods", [P, DEPTH, 48, 2])
        gsc = sb("gsc", [P, 8, 2])
        heads_bc = sb("heads_bc", [P, DEPTH, 40])
        ones = sb("ones", [P, 4, P])
        epsc = sb("epsc", [P, 1])
        sel_r = sb("sel_r", [P, 2], F32R)
        s_hi = sb("s_hi", [P, KD, P], F32R)
        raw = sb("raw", [P, NRAW, WT])
        w_hi = sb("w_hi", [P, 2, WT], F32R)
        w_lo = sb("w_lo", [P, 2, WT], F32R)
        h_hi = sb("h_hi", [P, KD, TOK], F32R)
        h_lo = sb("h_lo", [P, KD, TOK], F32R)
        rstd = sb("rstd", [P, TOK])
        sdev = sb("sdev", [P, TOK])
        rmax = sb("rmax", [P, 2])
        rsum = sb("rsum", [P, 2])
        rrec = sb("rrec", [P, 2])
        psum = [ctx.enter_context(nc.psum_tensor(f"slot{i}", [P, 2 * HALF], F32)) for i in range(NSLOT)]

        with ExitStack() as m:
            br_hi = sb("br_hi", [P, KB, TOK], F32R, m)
            br_lo = sb("br_lo", [P, KB, TOK], F32R, m)
            with ExitStack() as q:
                kT = sb("kT", [P, HEADS, TOK], F32, q)
                vt = sb("vt", [P, NT, BW], F32, q)
                qT = sb("qT", [P, HEADS, TOK], F32, q)
                with ExitStack() as r:
                    ln_hi = sb("ln_hi", [P, 3, TOK], F32R, r)
                    ln_lo = sb("ln_lo", [P, 3, TOK], F32R, r)
                with ExitStack() as r:
                    pT = sb("pT", [P, NT, TOK], F32, r)
            sigm = sb("sigm", [P, 2, TOK], F32, m)
            gated = sb("gated", [P, TOK], F32, m)
            merged = sb("merged", [P, KD, TOK], F32, m)
            with ExitStack() as q:
                cgs = sb("cgs", [P, 2, TOK], F32, q)
                cgx = sb("cgx", [P, 2, TOK], F32, q)
                cvo = sb("cvo", [P, 2, TOK], F32, q)
            with ExitStack() as q:
                dft = sb("dft", [P, 2, 4, LAT], F32, q)
                ch_hi = sb("ch_hi", [P, 256], F32R, q)
                ch_lo = sb("ch_lo", [P, 256], F32R, q)
                fn_hi = sb("fn_hi", [P, TOK], F32R, q)
                fn_lo = sb("fn_lo", [P, TOK], F32R, q)
                fy = sb("fy", [P, NT, 256], F32, q)
            with ExitStack() as q:
                dts = sb("dts", [P, 6, 2, NT, 8], F32, q)
                ex = sb("ex", [P, 3, 2, NT, 8], F32, q)
                dterm = sb("dterm", [P, 2, NT, 8], F32, q)
                laR = sb("laR", [P, P], F32, q)
                cumR = sb("cumR", [P, P], F32, q)
                blkR = sb("blkR", [P, 8], F32, q)
                exin = sb("exin", [P, 3, 2, NT, 8], F32, q)
                xs_tok = sb("xs_tok", [P, NT, BW], F32, q)
                b_tok = sb("b_tok", [P, NT, 256], F32, q)
                y_tok = sb("y_tok", [P, NT, BW], F32, q)
                with ExitStack() as r:
                    bc = sb("bc", [P, 4, TOK], F32, r)
                with ExitStack() as r:
                    zs = sb("zs", [P, KB, TOK], F32, r)
        with ExitStack() as m:
            with ExitStack() as q:
                lraw = sb("lraw", [P, 5, TOK], F32, q)
                sql = sb("sql", [P, 3, TOK], F32, q)
            with ExitStack() as q:
                diff = sb("diff", [P, 8, P], F32, q)
                seg = sb("seg", [P, 8, P], F32, q)
                cbm = sb("cbm", [P, 2, 2, P], F32, q)
                xd = sb("xd", [P, BW], F32, q)
                xr = sb("xr", [P, BW], F32, q)
                st = sb("st", [P, 2, BW], F32, q)
                yo = sb("yo", [P, BW], F32, q)
                decayed = sb("decayed", [P, BW], F32, q)
        with ExitStack() as m:
            x = sb("x", [P, KD, TOK], F32, m)
            with ExitStack() as q:
                sqx = sb("sqx", [P, KD, TOK], F32, q)
                row_hi = sb("row_hi", [4, 2, 256], F32R, q)
                row_lo = sb("row_lo", [4, 2, 256], F32R, q)
                zeros = sb("zeros", [P, WT], F32, q)
                silc = sb("silc", [P, 2, 8], F32, q)
                parr = sb("parr", [P, DEPTH + 1, P], F32, q)
            with ExitStack() as q:
                xin = sb("xin", [P, 2, D], F32, q)
            with ExitStack() as q:
                f_hi = sb("f_hi", [P, KD, TOK], F32R, q)
                f_lo = sb("f_lo", [P, KD, TOK], F32R, q)
                act_r = sb("act_r", [P, 2, TOK], F32, q)
            with ExitStack() as q:
                yout = sb("yout", [P, 2, D], F32, q)
                xf = sb("xf", [P, KD, TOK], F32, q)
        y_sq = xs_tok[:, :, :].rearrange("p t c -> p (t c)").rearrange("p (k t) -> p k t", k=KB)
        act_f = [rstd, sdev]
        probs = [rstd, sdev]
        cacc = [gated, rstd]
        conv = sigm[:, 0, :]
        dtT = y_tok[:, :, :].rearrange("p t c -> p (t c)")[0:32, 0:TOK]

        x_spill = nc.dram_tensor("x_spill", (P, KD * TOK), F32, kind="Internal").ap()

        tiles, tile_of = [], {}

        def tile(key, src, k0, kt, c0, cols, pitch=0):
            tile_of[key] = len(tiles)
            tiles.append((src[k0 * P:(k0 + kt) * P, c0:c0 + cols].rearrange("(k p) c -> p k c", p=P), kt, cols,
                          pitch or cols))

        def merge_tiles(L, k, branch):
            for j in range(4):
                for f in (2 * j, 2 * j + 1):
                    tile((L, "gate", k, f), A["w_in"][L], 0, KD, GT0 + D * branch + P * f, P)
                tile((L, "proj", k, j), A["w_branch"][L, branch], 0, KB, 256 * j, 256)

        for L in range(DEPTH):
            win = A["w_in"][L]
            for j in range(24):
                for half in range(2):
                    tile((L, "ada", j, half), A["ada_w"][L], 4 * half, 4, 256 * j, 256)
            for f in range(2):
                tile((L, "kva", f), win, 0, KD, KVA0 + P * f, P)
            tile((L, "kr"), win, 0, KD, KR0 - NOPE, P)
            for f in range(3):
                tile((L, "qa", f), win, 0, KD, QA0 + P * f, P)
            for i in range(2):
                tile((L, "wkv", i), A["mla_wkvb"][L], 0, 2, 512 * i, 512)
            for i in range(3):
                tile((L, "wq", i), A["mla_wqb"][L], 0, 3, 3 * QH * i, min(320, HEADS * QH - 3 * QH * i), 320)
            merge_tiles(L, 0, 2)
            for f in range(KB):
                tile((L, "cg", f), win, 0, KD, SC0 + BW + P * f, P)
                tile((L, "xin", f), win, 0, KD, SC0 + 2 * BW + P * f, P)
                tile((L, "bg", f), win, 0, KD, SC0 + P * f, P)
            merge_tiles(L, 1, 1)
            for f in range(KB):
                tile((L, "fn", f), win, 0, KD, FN0 + P * f, P)
            merge_tiles(L, 2, 3)
            tile((L, "dt"), win, 0, KD, DT0, P)
            for f in range(KD):
                tile((L, "xbc", f), win, 0, KD, XBC0 + P * f, P)
            for f in range(KB):
                tile((L, "z", f), win, 0, KD, Z0 + P * f, P)
            merge_tiles(L, 3, 0)
            for f in range(KD):
                tile((L, "out", f), A["w_out"][L], 0, KD, P * f, P)
            for c in range(4):
                for f in range(KD):
                    tile((L, "w1", c, f), A["mlp_w1"][L], 0, KD, D * c + P * f, P)
                for f in range(KD):
                    tile((L, "w2", c, f), A["mlp_w2"][L], KD * c, KD, P * f, P)
        ada_tiles = {s for key, s in tile_of.items() if key[1] == "ada"}

        def lo_sem(s):
            return "w_lo_by_dve" if s in ada_tiles else "w_lo_by_pool"

        ALL = [(T0, 0, CTX), (HALF, CTX, LAT)]
        LATS = ALL[1:]

        def spans(L):
            return ALL if L < DEPTH - 1 else LATS

        def first(L):
            return 0 if L < DEPTH - 1 else CTX

        def kinds(a):
            return ([(0, CTX, 1)] if a == 0 else []) + [(CTX, TOK, 0)]

        order, last_use = {}, {}

        def slot(key):
            return psum[order[key] % NSLOT][:, :]

        def cols(key, a, p0=0, p1=P):
            return slot(key)[p0:p1, T0 + a:T0 + TOK]

        slot_full = counts.sem("slot_full")
        slot_read = [counts.sem(f"slot{i}_read") for i in range(NSLOT)]

        def full(key):
            return slot_full, order[key] + 1

        def frees(key):
            counts.last = slot_read[order[key] % NSLOT], order[key] // NSLOT + 1
            return slot_read[order[key] % NSLOT], 1

        def read(key):
            return slot_read[order[key] % NSLOT], order[key] // NSLOT + 1

        block = ctx.enter_context(nc.Block())

        def att_items(L):
            return [(h, qt) for h in range(HEADS) for qt in range(first(L) // P, NT)]

        def ssd_items(L):
            return [(d, c, c * P >= first(L), n > 0, n < NT - 1)
                    for d, chunks in enumerate(((0, 1, 2, 3, 4, 5), (1, 0, 5, 4, 3, 2))) for n, c in enumerate(chunks)]

        def fourier_parts(L):
            parts = [(0, 2, 0, CTX, 2, (CTX * P) ** -0.5), (2, 4, CTX, LAT, 1, (LAT * P) ** -0.5)]
            return parts[first(L) // CTX:]

        @block.tensor
        def _(pe):
            ident = cst[:, C_ID:C_ID + P]

            def take(key):
                order[key] = len(order)
                if order[key] >= NSLOT:
                    pe.wait_ge(slot_read[order[key] % NSLOT], order[key] // NSLOT)
                return slot(key)

            def weights(wkey, key):
                s = tile_of[wkey]
                pe.wait_ge(*when(lo_sem(s), s))
                last_use[s] = order[key]
                _, kt, _, pitch = tiles[s]
                return [w[:, s % 2, 0:kt * pitch].rearrange("p (k c) -> p k c", k=kt) for w in (w_hi, w_lo)]

            def product(key, wkey, kts, col, a_hi, a_lo, sp, ready=None):
                o = take(key)
                wh, wl = weights(wkey, key)
                for k in range(kts):
                    if ready:
                        ready(k)
                    for n, (w, a) in enumerate(((wh, a_hi), (wh, a_lo), (wl, a_hi))):
                        for c0, t0, nt in sp:
                            last = pe.matmul(o[:, c0:c0 + nt], w[:, k, col:col + P], a[:, k, t0:t0 + nt],
                                             start=(k == 0 and n == 0), stop=(k == kts - 1 and n == 2))
                last.then_inc(slot_full, 1)

            def mean_square(key, src, k0, k1, mat, sp, name, tag):
                o = take(key)
                for k in range(k0, k1):
                    pe.wait_ge(*when(name, (tag, k)))
                    for c0, t0, nt in sp:
                        last = pe.matmul(o[:, c0:c0 + nt], ones[:, mat, :], src[:, k, t0:t0 + nt],
                                         start=(k == k0), stop=(k == k1 - 1))
                last.then_inc(slot_full, 1)

            def turn(key, blocks, to=P):
                o = take(key)
                for n, b in enumerate(blocks):
                    last = pe.transpose(o[:, n * to:(n + 1) * to], b, ident if to == P else cst[0:to, C_ID:C_ID + to])
                last.then_inc(slot_full, 1)

            def ada_rows(L, j):
                if (L, j) == (0, 0):
                    pe.wait_ge(*when("cond_split", 0))
                o = take((L, "ada", j))
                for half in range(2):
                    wh, wl = weights((L, "ada", j, half), (L, "ada", j))
                    for k in range(4):
                        for n, w in enumerate((wh, wl)):
                            last = pe.matmul(o[:, 0:256], s_hi[:, 4 * half + k, :], w[:, k, :],
                                             start=(half == 0 and k == 0 and n == 0),
                                             stop=(half == 1 and k == 3 and n == 1))
                last.then_inc(slot_full, 1)

            def ada_turn(L, j):
                pe.wait_ge(*read((L, "ada", j)))
                o = take((L, "adaT", j))
                for i in range(2):
                    for n, r in enumerate((row_hi, row_lo)):
                        last = pe.matmul(o[:, 2 * i:2 * i + 2], r[0:4, j % 2, i * P:(i + 1) * P], sel_r[0:4, :],
                                         start=(n == 0), stop=(n == 1))
                last.then_inc(slot_full, 1)

            def rotated(key, src, h, sp):
                o = take(key)
                for c0, t0, nt in sp:
                    last = pe.matmul(o[:, c0:c0 + nt], cst[NOPE:QH, C_ROT:C_ROT + P], src[NOPE:QH, h, t0:t0 + nt],
                                     start=True, stop=True)
                last.then_inc(slot_full, 1)

            def latent(L):
                sp = spans(L)
                for f in range(2):
                    product((L, "kva", f), (L, "kva", f), KD, 0, h_hi, h_lo, ALL,
                            (lambda k: pe.wait_ge(*when("h_lo", (L, 1, k)))) if f == 0 else None)
                product((L, "kr"), (L, "kr"), KD, 0, h_hi, h_lo, ALL)
                for f in range(3):
                    product((L, "qa", f), (L, "qa", f), KD, 0, h_hi, h_lo, sp)
                mean_square((L, "kvms"), sql, 0, 2, 3, ALL, "kv_squared", L)
                pe.wait_ge(*when("kr_copied", L))
                rotated((L, "krot"), kT, 0, ALL)
                for i in range(2):
                    for h in range(4 * i, 4 * i + 4):
                        product((L, "k", h), (L, "wkv", i), 2, P * (h % 4), ln_hi, ln_lo, ALL,
                                (lambda k: pe.wait_ge(*when("kvn_lo", (L, k)))) if h == 0 else None)
                    for tp in range(NT // 2):
                        o = take((L, "v", i, tp))
                        wh, wl = [w.rearrange("p k (h c) -> p k h c", h=4)
                                  for w in weights((L, "wkv", i), (L, "v", i, tp))]
                        for u in range(2):
                            t = 2 * tp + u
                            for k in range(2):
                                for n, (a, w) in enumerate(((ln_hi, wh), (ln_hi, wl), (ln_lo, wh))):
                                    last = pe.matmul(o[:, HALF * u:HALF * u + 256], a[:, k, t * P:(t + 1) * P],
                                                     w[:, k, :, NOPE:NOPE + VD], start=(k == 0 and n == 0),
                                                     stop=(k == 1 and n == 2))
                        last.then_inc(slot_full, 1)
                mean_square((L, "qms"), sql, 0, 3, 2, sp, "q_squared", L)
                for h in range(HEADS + 1):
                    if h < HEADS:
                        product((L, "q", h), (L, "wq", h // 3), 3, QH * (h % 3), ln_hi, ln_lo, sp,
                                (lambda k: pe.wait_ge(*when("qn_lo", (L, k)))) if h == 0 else None)
                    if h >= 1:
                        pe.wait_ge(*when("q_copied", (L, h - 1)))
                        rotated((L, "qrot", h - 1), qT, h - 1, sp)

            def attention(L):
                items = att_items(L)

                def scores(h, qt):
                    if (h, qt) == items[0]:
                        pe.wait_ge(*when("k_rotated", L))
                    if qt == items[0][1]:
                        pe.wait_ge(*when("q_rotated", (L, h)))
                        pe.wait_ge(*read((L, "k", h)))
                    o = take((L, "s", h, qt))
                    for c0, t0, nt in ALL[:1] if qt < 2 else ALL:
                        last = pe.matmul(o[:, c0:c0 + nt], qT[0:QH, h, qt * P:(qt + 1) * P],
                                         kT[0:QH, h, t0:t0 + nt], start=True, stop=True)
                    last.then_inc(slot_full, 1)

                def values(h):
                    o = take((L, "o", h))
                    for qt in range(items[0][1], NT):
                        pe.wait_ge(*read((L, "pT", h, qt)))
                    lo = (h % 2) * VD
                    for c0, q0, nq in spans(L):
                        kts = NT if q0 else 2
                        for k in range(kts):
                            if h == 0:
                                pe.wait_ge(*read((L, "v", 0, k // 2)))
                            if h == 4:
                                pe.wait_ge(*read((L, "v", 1, k // 2)))
                            last = pe.matmul(o[lo:lo + VD, c0:c0 + nq], vt[:, k, h * VD:(h + 1) * VD],
                                             pT[:, k, q0:q0 + nq], start=(k == 0), stop=(k == kts - 1))
                    last.then_inc(slot_full, 1)

                for n in range(len(items) + 2):
                    if n < len(items):
                        scores(*items[n])
                    if n >= 2:
                        h, qt = items[n - 2]
                        pe.wait_ge(*when("probs", (L, h, qt)))
                        turn((L, "pT", h, qt), [probs[n % 2][:, k * P:(k + 1) * P] for k in range(2 if qt < 2 else NT)])
                        if qt == NT - 1:
                            values(h)

            def branch_ready(L, k, i):
                if k == 0:
                    pe.wait_ge(*read((L, "o", 2 * i)))
                    pe.wait_ge(*read((L, "o", 2 * i + 1)))
                elif k == 2:
                    pe.wait_ge(*read((L, "fo", i)))
                else:
                    pe.wait_ge(*when("branch_lo", (L, k, i)))

            def merge(L, k):
                sp = spans(L)
                for j in range(4):
                    for f in (2 * j, 2 * j + 1):
                        product((L, "gate", k, f), (L, "gate", k, f), KD, 0, h_hi, h_lo, sp)
                    for f in (2 * j, 2 * j + 1):
                        product((L, "proj", k, f), (L, "proj", k, j), KB, P * (f % 2), br_hi, br_lo, sp,
                                (lambda i: branch_ready(L, k, i)) if f == 0 else None)

            def short_conv(L):
                for f in range(KB):
                    for what in ("cg", "xin", "bg"):
                        product((L, what, f), (L, what, f), KD, 0, h_hi, h_lo, spans(L))

            def fourier(L):
                pairs = range(first(L) // CTX, NT // 2)
                product((L, "fn", 0), (L, "fn", 0), KD, 0, h_hi, h_lo, spans(L))
                pe.wait_ge(*when("channel_dft", L))
                for g in range(4):
                    pe.wait_ge(*read((L, "fn", g)))
                    for tp in pairs:
                        o = take((L, "fy", g, tp))
                        for u in range(2):
                            t = 2 * tp + u
                            for n, (a, b) in enumerate(((fn_hi, ch_hi), (fn_hi, ch_lo), (fn_lo, ch_hi))):
                                last = pe.matmul(o[:, HALF * u:HALF * u + 256], a[:, t * P:(t + 1) * P], b[:, :],
                                                 start=(n == 0), stop=(n == 2))
                        last.then_inc(slot_full, 1)
                    if g < 3:
                        product((L, "fn", g + 1), (L, "fn", g + 1), KD, 0, h_hi, h_lo, spans(L))
                    else:
                        pe.wait_ge(*when("dft_loaded", L))
                    if g == 0:
                        pe.wait_ge(*when("dft_loaded", L))
                    for tp in pairs:
                        pe.wait_ge(*read((L, "fy", g, tp)))
                    o = take((L, "fo", g))
                    for tile0, n_t, t0, nt, step, _ in fourier_parts(L):
                        for j in range(n_t):
                            for part in range(2):
                                last = pe.matmul(o[:, T0 + t0:T0 + t0 + nt], fy[:, tile0 + j, part * P:(part + 1) * P],
                                                 dft[:, part, j, 0:LAT:step], start=(j == 0 and part == 0),
                                                 stop=(j == n_t - 1 and part == 1))
                    last.then_inc(slot_full, 1)

            def ssd(L):
                product((L, "dt"), (L, "dt"), KD, 0, h_hi, h_lo, ALL)
                for f in range(KD):
                    product((L, "xbc", f), (L, "xbc", f), KD, 0, h_hi, h_lo, ALL)
                    if f == 0:
                        pe.wait_ge(*read((L, "dt")))
                        turn((L, "dtT"), [dtT[0:32, t * P:(t + 1) * P] for t in range(NT)], 32)
                    if 1 <= f <= 6:
                        pe.wait_ge(*when("conv_silu", (L, f - 1)))
                        src = conv if f - 1 < 4 else bc[:, f - 5, :]
                        turn((L, "xT", f - 1), [src[:, t * P:(t + 1) * P] for t in range(NT)])
                pe.wait_ge(*when("la", L))
                o = take((L, "laT"))
                la = dts[:, 3, :, :, :].rearrange("p d t h -> p d (t h)")
                for d in range(2):
                    last = pe.matmul(o[64 * d:64 * d + ROWS, 0:P], la[:, d, :], ident, start=True, stop=True)
                last.then_inc(slot_full, 1)
                pe.wait_ge(*when("cum_rows", L))
                o = take((L, "cum"))
                for d in range(2):
                    last = pe.matmul(o[:, HALF * d:HALF * d + ROWS], cumR[64 * d:64 * d + ROWS, :],
                                     cst[64 * d:64 * d + ROWS, C_ID + 64 * d:C_ID + 64 * d + ROWS],
                                     start=True, stop=True)
                last.then_inc(slot_full, 1)
                pe.wait_ge(*read((L, "cum")))
                o = take((L, "tot"))
                for d, end in enumerate((P - 1, 0)):
                    last = pe.matmul(o[:, ROWS * d:ROWS * d + ROWS],
                                     cst[:, C_ID + end:C_ID + end + 1].to_broadcast([P, P]),
                                     exin[:, 0, d, :, :].rearrange("p t h -> p (t h)"), start=True, stop=True)
                last.then_inc(slot_full, 1)
                items = ssd_items(L)

                def within(n):
                    d, c, want, has, gives = items[n]
                    tk = slice(c * P, (c + 1) * P)
                    if want:
                        o = take((L, "cb", d, c))
                        pe.wait_ge(*when("conv_silu", (L, 7)))
                        for g in range(2):
                            last = pe.matmul(o[:, g * P:(g + 1) * P], bc[:, g, tk], bc[:, 2 + g, tk],
                                             start=True, stop=True)
                        last.then_inc(slot_full, 1)
                        o = take((L, "seg", d, c))
                        rows = slice(64 * d, 64 * d + ROWS)
                        for h in range(8):
                            r = C_ID + 64 * d + 8 * c + h
                            last = pe.matmul(o[:, h * P:(h + 1) * P], cst[rows, r:r + 1].to_broadcast([ROWS, P]),
                                             cumR[rows, :], start=True, stop=True)
                        last.then_inc(slot_full, 1)
                    if gives:
                        pe.wait_ge(*when("xr", (L, d, c)))
                        o = take((L, "state", d, c))
                        for g in range(2):
                            last = pe.matmul(o[:, g * 256:(g + 1) * 256], b_tok[:, c, g * P:(g + 1) * P],
                                             xr[:, g * 256:(g + 1) * 256], start=True, stop=True)
                        last.then_inc(slot_full, 1)

                def outputs(n):
                    d, c, want, has, gives = items[n]
                    if not want:
                        return
                    tk = slice(c * P, (c + 1) * P)
                    o = take((L, "y", d, c))
                    if has:
                        pe.wait_ge(*read((L, "state") + items[n - 1][0:2]))
                        for g in range(2):
                            pe.matmul(o[:, HALF + g * 256:HALF + (g + 1) * 256], bc[:, 2 + g, tk],
                                      st[:, (n - 1) % 2, g * 256:(g + 1) * 256], start=True, stop=True)
                    pe.wait_ge(*when("seg_masked", (L, d, c)))
                    for h in range(8):
                        last = pe.matmul(o[:, h * 64:(h + 1) * 64], seg[:, h, :], xd[:, h * 64:(h + 1) * 64],
                                         start=True, stop=True)
                    last.then_inc(slot_full, 1)

                pe.wait_ge(*read((L, "xT", 5)))
                within(0)
                for n in range(len(items)):
                    if n + 1 < len(items):
                        within(n + 1)
                    outputs(n)
                for f in range(KB):
                    product((L, "z", f), (L, "z", f), KD, 0, h_hi, h_lo, spans(L))
                pe.wait_ge(*read((L, "y") + items[-1][0:2]))
                for c in range(first(L) // P, NT):
                    turn((L, "yT", c), [y_tok[:, c, f * P:(f + 1) * P] for f in range(KB)])
                for g in range(2):
                    mean_square((L, "yms", g), y_sq, 2 * g, 2 * g + 2, 3, spans(L), "y_squared", L)

            pe.wait_ge(*when("loaded", "params"))
            turn("params", [parr[:, i, :] for i in range(DEPTH + 1)])
            for t in range(NT):
                pe.wait_ge(*when(f"x_in{t % 2}", t))
                turn(("x", t), [xin[:, t % 2, k * P:(k + 1) * P] for k in range(KD)])
            for L in range(DEPTH):
                for j in range(25):
                    if j < 24:
                        ada_rows(L, j)
                    if j >= 1:
                        ada_turn(L, j - 1)
                mean_square((L, "ms", 1), sqx, 0, KD, 1, ALL, "x_squared", (L, 1))
                latent(L)
                attention(L)
                merge(L, 0)
                short_conv(L)
                merge(L, 1)
                fourier(L)
                merge(L, 2)
                ssd(L)
                merge(L, 3)
                for f in range(KD):
                    product((L, "out", f), (L, "out", f), KD, 0, h_hi, h_lo, spans(L),
                            (lambda k: pe.wait_ge(*when("merged_lo", (L, k)))) if f == 0 else None)
                mean_square((L, "ms", 2), sqx, 0, KD, 1, spans(L), "x_squared", (L, 2))
                for c in range(4):
                    for f in range(KD):
                        product((L, "w1", c, f), (L, "w1", c, f), KD, 0, h_hi, h_lo, spans(L),
                                (lambda k: pe.wait_ge(*when("h_lo", (L, 2, k)))) if c == f == 0 else None)
                    for f in range(KD):
                        product((L, "w2", c, f), (L, "w2", c, f), KD, 0, f_hi, f_lo, spans(L),
                                (lambda k: pe.wait_ge(*when("f_lo", (L, c, k)))) if f == 0 else None)
            mean_square((DEPTH, "ms", 1), sqx, 0, KD, 1, LATS, "x_squared", (DEPTH, 1))
            pe.wait_ge(*when("x_scaled", KD - 1))
            for t in range(CTX // P, NT):
                turn(("y", t), [xf[:, k, t * P:(t + 1) * P] for k in range(KD)])

        @block.sync
        def _(sp_):
            for s, (src, kt, ncol, pitch) in enumerate(tiles):
                if s >= NRAW:
                    sp_.wait_ge(*when(lo_sem(s - NRAW), s - NRAW))
                dst = raw[:, s % NRAW, 0:kt * pitch].rearrange("p (k c) -> p k c", k=kt)[:, :, 0:ncol]
                sp_.dma_start(dst, src).then_inc(counts.sem(f"raw{s % NRAW}_loaded"), 16)

        @block.gpsimd
        def _(pool):
            for s in range(len(tiles)):
                if s not in ada_tiles:
                    pool.wait_ge(*when("w_hi", s))
                    pool.tensor_tensor(w_lo[:, s % 2, :], raw[:, s % NRAW, :], w_hi[:, s % 2, :].bitcast(F32),
                                            ALU.subtract).then_inc(*does("w_lo_by_pool", s))

        @block.scalar
        def _(act):
            A_ = nc.scalar.activation
            fed = [0]

            def round_weights(limit):
                while fed[0] < len(tiles) and (fed[0] < 2 or last_use[fed[0] - 2] <= limit):
                    s = fed[0]
                    act.wait_ge(counts.sem(f"raw{s % NRAW}_loaded"), 16 * (s // NRAW + 1))
                    if s >= 2:
                        act.wait_ge(counts.sem("slot_full"), last_use[s - 2] + 1)
                    A_(w_hi[:, s % 2, :], raw[:, s % NRAW, :], ACT.Copy).then_inc(*does("w_hi", s))
                    fed[0] += 1

            act.dma_start(cst[:, :], A["tables"]).then_inc(*does("loaded", "tables", 16))
            act.wait_ge(*when("cleared", 0))
            for L in range(DEPTH):
                vec = "(t c) -> t c"
                for r0, src, n in ((R_CW, A["ssm_conv_w"][L].rearrange("k (t c) -> (k t) c", c=P), 40),
                                   (R_CB, A["ssm_conv_b"][L].rearrange(vec, c=P), 8),
                                   (R_N1, A["norm1_g"][L].rearrange(vec, c=P), 8),
                                   (R_N2, A["norm2_g"][L].rearrange(vec, c=P), 8),
                                   (R_SN, A["ssm_norm_g"][L].rearrange(vec, c=P), 4),
                                   (R_SW, A["sc_conv_w"][L].rearrange("k (t c) -> (k t) c", c=P), 12),
                                   (R_QG, A["mla_qa_g"][L].rearrange(vec, c=P), 3),
                                   (R_KG, A["mla_kva_g"][L].rearrange(vec, c=P), 2),
                                   (R_FG, A["final_norm_g"].rearrange(vec, c=P), 8),
                                   (R_C, A["c"][0].rearrange(vec, c=P), 8),
                                   (R_CC, A["c_ctx"].rearrange(vec, c=P), 8)):
                    act.dma_start(parr[r0:r0 + n, L, :], src).then_inc(*does("loaded", (L, r0), 16))
                act.dma_start(parr[48 * L:48 * L + 48, DEPTH, :], A["ada_b"][L].rearrange(vec, c=P)).then_inc(*does("loaded", (L, "ada"), 16))
                for o, src, n in ((0, A["ssm_a_log"][L].rearrange("a b -> (a b)"), 16),
                                  (16, A["ssm_dt_bias"][L].rearrange("a b -> (a b)"), 16), (32, A["ssm_d"][L], 8)):
                    act.dma_start(heads_bc[:, L, o:o + n], src.partition_broadcast(P)).then_inc(*does("loaded", (L, "h", o), 16))
            counts.table["loaded", "params"] = counts.now["loaded"]
            for t in range(NT):
                if t >= 2:
                    act.wait_ge(*full(("x", t - 2)))
                act.dma_start(xin[:, t % 2, :], A["ctx"][0, t * P:(t + 1) * P, :] if t < 2 else A["x"][0, (t - 2) * P:(t - 1) * P, :]).then_inc(*does(f"x_in{t % 2}", t, 16))
            act.wait_ge(*read("params"))
            A_(silc[:, 0, :], par[:, 0, R_C:R_C + 8], ACT.Silu)
            A_(silc[:, 1, :], par[:, 0, R_CC:R_CC + 8], ACT.Silu).then_inc(*does("silu_c", 0))
            round_weights(-1)

            def norm(L, which, a):
                for k in range(KD):
                    if which == 2:
                        round_weights(order[(L, "out", k)] - 1)
                        act.wait_ge(*read((L, "out", k)))
                    elif L:
                        if k == 0:
                            round_weights(order[L - 1, "w2", 3, KD - 1] - 1)
                            act.wait_ge(*full((L - 1, "w2", 3, KD - 1)))
                        round_weights(order[(L - 1, "w2", 3, k)] - 1)
                        act.wait_ge(*read((L - 1, "w2", 3, k)))
                    elif k == 0:
                        for t in range(NT):
                            round_weights(order[("x", t)] - 1)
                            act.wait_ge(*read(("x", t)))
                    A_(sqx[:, k, a:TOK], x[:, k, a:TOK], ACT.Square).then_inc(*does("x_squared", ((L, which), k)))
                key = (L, "ms", which)
                round_weights(order[key] - 1)
                act.wait_ge(*full(key))
                A_(sdev[:, a:TOK], cols(key, a), ACT.Sqrt, bias=epsc[:, :]).then_inc(*frees(key))
                if L < DEPTH:
                    for k in range(KD):
                        act.wait_ge(*when("h", (L, which, k)))
                        A_(h_hi[:, k, a:TOK], sqx[:, k, a:TOK], ACT.Copy).then_inc(*does("h_hi", (L, which, k)))

            def latent(L):
                a = first(L)
                act.wait_ge(*when("x_stored", L))
                for f in range(2):
                    key = (L, "kva", f)
                    round_weights(order[key] - 1)
                    act.wait_ge(*full(key))
                    A_(sql[:, f, :], cols(key, 0), ACT.Square).then_inc(*does("kv_squared", (L, f)))
                    A_(lraw[:, f, :], cols(key, 0), ACT.Copy).then_inc(*frees(key))
                key = (L, "kr")
                round_weights(order[key] - 1)
                act.wait_ge(*full(key))
                A_(kT[NOPE:QH, 0, :], cols(key, 0, NOPE, QH), ACT.Copy).then_inc(*does("kr_copied", L))
                A_(kT[NOPE:QH, 1, :], cols(key, 0, NOPE, QH), ACT.Copy).then_inc(*frees(key))
                for f in range(3):
                    key = (L, "qa", f)
                    round_weights(order[key] - 1)
                    act.wait_ge(*full(key))
                    A_(lraw[:, 2 + f, a:TOK], cols(key, a), ACT.Copy).then_inc(*frees(key))
                key = (L, "kvms")
                round_weights(order[key] - 1)
                act.wait_ge(*full(key))
                A_(sdev[:, :], cols(key, 0), ACT.Sqrt, bias=epsc[:, :]).then_inc(*frees(key))
                act.wait_ge(*read((L, "qa", 2)))
                for f in range(3):
                    A_(sql[:, f, a:TOK], lraw[:, 2 + f, a:TOK], ACT.Square).then_inc(*does("q_squared", (L, f)))
                for f in range(2):
                    act.wait_ge(*when("kvn", (L, f)))
                    A_(ln_hi[:, f, :], lraw[:, f, :], ACT.Copy).then_inc(*does("kvn_hi", (L, f)))
                for h in range(HEADS):
                    key = (L, "k", h)
                    round_weights(order[key] - 1)
                    act.wait_ge(*full(key))
                    A_(kT[0:NOPE, h, :], cols(key, 0, 0, NOPE), ACT.Copy).then_inc(*frees(key))
                key = (L, "qms")
                round_weights(order[key] - 1)
                act.wait_ge(*full(key))
                A_(sdev[:, a:TOK], cols(key, a), ACT.Sqrt, bias=epsc[:, :]).then_inc(*frees(key))
                for f in range(3):
                    act.wait_ge(*when("qn", (L, f)))
                    A_(ln_hi[:, f, a:TOK], lraw[:, 2 + f, a:TOK], ACT.Copy).then_inc(*does("qn_hi", (L, f)))
                for h in range(HEADS):
                    key = (L, "q", h)
                    round_weights(order[key] - 1)
                    act.wait_ge(*full(key))
                    A_(qT[0:QH, h, a:TOK], cols(key, a, 0, QH), ACT.Copy, scale=SCALE).then_inc(*does("q_copied", (L, h)))

            def attention(L):
                items = att_items(L)
                for n in range(len(items) + 2):
                    if n < len(items):
                        h, qt = items[n]
                        key = (L, "s", h, qt)
                        end = CTX if qt < 2 else TOK
                        act.wait_ge(*when("row_max", (L, h, qt)))
                        if n >= 2:
                            act.wait_ge(*full((L, "pT") + items[n - 2]))
                        A_(probs[n % 2][:, 0:end], slot(key)[:, T0:T0 + end], ACT.Exp, bias=rmax[:, n % 2:n % 2 + 1],
                                accum_out=rsum[:, n % 2:n % 2 + 1]).then_inc(*frees(key))
                    if n >= 2:
                        h, qt = items[n - 2]
                        key = (L, "pT", h, qt)
                        act.wait_ge(*full(key))
                        nk = 2 if qt < 2 else NT
                        A_(pT[:, 0:nk, qt * P:(qt + 1) * P],
                                slot(key)[:, 0:nk * P].rearrange("p (k q) -> p k q", k=nk), ACT.Copy).then_inc(*frees(key))
                        if qt == NT - 1:
                            lo = (h % 2) * VD
                            round_weights(order[L, "o", h] - 1)
                            act.wait_ge(*full((L, "o", h)))
                            A_(br_hi[lo:lo + VD, h // 2, first(L):TOK],
                                    cols((L, "o", h), first(L), lo, lo + VD), ACT.Copy).then_inc(*does("values_hi", (L, h)))

            def branch_hi(L, k, f, src):
                A_(br_hi[:, f, first(L):TOK], src[:, first(L):TOK], ACT.Copy).then_inc(*does("branch_hi", (L, k, f)))

            def merge(L, k):
                a = first(L)
                for f in range(KD):
                    key = (L, "gate", k, f)
                    round_weights(order[key] - 1)
                    act.wait_ge(*full(key))
                    if f >= 2:
                        round_weights(order[(L, "proj", k, f - 2)] - 1)
                        act.wait_ge(*read((L, "proj", k, f - 2)))
                    elif k:
                        round_weights(order[(L, "proj", k - 1, f + 6)] - 1)
                        act.wait_ge(*read((L, "proj", k - 1, f + 6)))
                    A_(sigm[:, f % 2, a:TOK], cols(key, a), ACT.Sigmoid).then_inc(*frees(key))

            def short_conv(L):
                a = first(L)
                for f in range(KB + 1):
                    if f < KB:
                        key = (L, "cg", f)
                        round_weights(order[key] - 1)
                        act.wait_ge(*full(key))
                        if f >= 2:
                            round_weights(order[(L, "xin", f - 2)] - 1)
                            act.wait_ge(*read((L, "xin", f - 2)))
                        A_(cgs[:, f % 2, a:TOK], cols(key, a), ACT.Copy).then_inc(*frees(key))
                    if f >= 1:
                        round_weights(order[(L, "bg", f - 1)] - 1)
                        act.wait_ge(*read((L, "bg", f - 1)))
                        branch_hi(L, 1, f - 1, cvo[:, (f - 1) % 2, :])

            def fourier(L):
                a = first(L)
                round_weights(order[L, "proj", 1, KD - 1])
                act.wait_ge(*full((L, "proj", 1, KD - 1)))
                act.dma_start(dft.rearrange("p a j t -> p a (j t)"), A["dft"].rearrange("a (j p) t -> p a j t", p=P).rearrange("p a j t -> p a j t")).then_inc(*does("dft_loaded", L, 16))
                A_(ch_hi[:, :], cst[:, C_CHAN:C_CHAN + 256], ACT.Copy).then_inc(*does("channel_hi", L))

                def out_hi(g):
                    key = (L, "fo", g)
                    round_weights(order[key] - 1)
                    act.wait_ge(*full(key))
                    for _, _, t0, nt, _, scale in fourier_parts(L):
                        ins = A_(br_hi[:, g, t0:t0 + nt], slot(key)[:, T0 + t0:T0 + t0 + nt], ACT.Copy, scale=scale)
                    ins.then_inc(*does("fourier_hi", (L, g)))

                for g in range(4):
                    if g == 0:
                        round_weights(order[L, "fn", 0] - 1)
                        act.wait_ge(*full((L, "fn", 0)))
                    A_(fn_hi[:, a:TOK], cols((L, "fn", g), a), ACT.Copy).then_inc(*does("fn_hi", (L, g)))
                    if g >= 1:
                        out_hi(g - 1)
                    for tp in range(a // CTX, NT // 2):
                        key = (L, "fy", g, tp)
                        round_weights(order[key] - 1)
                        act.wait_ge(*full(key))
                        A_(fy[:, 2 * tp:2 * tp + 2, :],
                                slot(key).rearrange("p (a b) -> p a b", b=HALF)[:, :, 0:256], ACT.Copy).then_inc(*frees(key))
                    if g < 3:
                        round_weights(order[L, "fn", g + 1] - 1)
                        act.wait_ge(*full((L, "fn", g + 1)))
                out_hi(3)

            def ssd(L):
                a = first(L)
                key = (L, "dt")
                round_weights(order[key] - 1)
                act.wait_ge(*full(key))
                A_(dtT, cols(key, 0, 0, 32), ACT.Copy).then_inc(*frees(key))
                for f in range(KD):
                    if 1 <= f <= 4:
                        round_weights(order[L, "xT", f - 1] - 1)
                        act.wait_ge(*full((L, "xT", f - 1)))
                    round_weights(order[(L, "xbc", f)] - 1)
                    act.wait_ge(*read((L, "xbc", f)))
                    A_(conv if f < 4 else bc[:, f - 4, :], cacc[f % 2][:, :], ACT.Silu).then_inc(*does("conv_silu", (L, f)))
                act.wait_ge(*when("dt_abs", L))
                A_(dts[:, 1, :, :, :], dts[:, 1, :, :, :], ACT.Exp, scale=-1.0).then_inc(*does("dt_exp", L))
                A_(heads_bc[:, L, 0:16], heads_bc[:, L, 0:16], ACT.Exp).then_inc(*does("rates", L))
                act.wait_ge(*when("dt_one", L))
                A_(dts[:, 4, :, :, :], dts[:, 2, :, :, :], ACT.Ln).then_inc(*does("dt_ln", L))
                round_weights(order[(L, "tot")] - 1)
                act.wait_ge(*read((L, "tot")))
                A_(ex[:, :, :, :, :].rearrange("p a d t h -> p (a d t h)"),
                        exin[:, :, :, :, :].rearrange("p a d t h -> p (a d t h)"), ACT.Exp).then_inc(*does("decays", L))
                prev = None
                for d, c, want, has, gives in ssd_items(L):
                    if want:
                        round_weights(order[L, "seg", d, c] - 1)
                        act.wait_ge(*when("diff", (L, d, c)))
                        if prev:
                            act.wait_ge(*full((L, "y") + prev))
                        A_(seg.rearrange("p h i -> p (h i)"), diff.rearrange("p h i -> p (h i)"), ACT.Exp).then_inc(*does("seg_exp", (L, d, c)))
                        prev = (d, c)
                for f in range(KB):
                    key = (L, "z", f)
                    round_weights(order[key] - 1)
                    act.wait_ge(*full(key))
                    A_(zs[:, f, a:TOK], cols(key, a), ACT.Silu).then_inc(*frees(key))
                round_weights(order[(L, "yT", NT - 1)] - 1)
                act.wait_ge(*read((L, "yT", NT - 1)))
                for f in range(KB):
                    A_(y_sq[:, f, a:TOK], zs[:, f, a:TOK], ACT.Square).then_inc(*does("y_squared", (L, f)))
                for g in range(2):
                    key = (L, "yms", g)
                    round_weights(order[key] - 1)
                    act.wait_ge(*full(key))
                    A_(sdev[:, a:TOK], cols(key, a), ACT.Sqrt, bias=epsc[:, :]).then_inc(*frees(key))
                    for f in range(2 * g, 2 * g + 2):
                        act.wait_ge(*when("branch", (L, 3, f)))
                        branch_hi(L, 3, f, zs[:, f, :])

            for L in range(DEPTH):
                a = first(L)
                for j in range(24):
                    key = (L, "ada", j)
                    round_weights(order[key] - 1)
                    act.wait_ge(*full(key))
                    if j >= 2:
                        act.wait_ge(*full((L, "adaT", j - 2)))
                    A_(row_hi[0:4, j % 2, :], slot(key)[0:4, 0:256], ACT.Copy).then_inc(*does("row_hi", (L, j)))
                    round_weights(order[key])
                norm(L, 1, 0)
                act.dma_start(x_spill, x.rearrange("p k t -> p (k t)")).then_inc(*does("x_stored", L, 16))
                latent(L)
                attention(L)
                merge(L, 0)
                short_conv(L)
                merge(L, 1)
                fourier(L)
                merge(L, 2)
                ssd(L)
                merge(L, 3)
                round_weights(order[L, "proj", 3, KD - 1] - 1)
                act.wait_ge(*full((L, "proj", 3, KD - 1)))
                act.dma_start(x.rearrange("p k t -> p (k t)"), x_spill).then_inc(*does("x_back", L, 16))
                for k in range(KD):
                    act.wait_ge(*when("merged", (L, 3, k)))
                    A_(h_hi[:, k, a:TOK], merged[:, k, a:TOK], ACT.Copy).then_inc(*does("merged_hi", (L, k)))
                norm(L, 2, a)
                for n in range(4 * KD):
                    c, f = divmod(n, KD)
                    key = (L, "w1", c, f)
                    round_weights(order[key] - 1)
                    act.wait_ge(*full(key))
                    if n >= 2:
                        act.wait_ge(*read((L, "w1") + divmod(n - 2, KD)))
                    A_(act_r[:, n % 2, a:TOK], cols(key, a), ACT.Relu).then_inc(*does("relu", (L, n)))
                    for m in [n - 1] * (f > 0) + [n] * (f == KD - 1):
                        round_weights(order[(L, "w1") + divmod(m, KD)] - 1)
                        act.wait_ge(*read((L, "w1") + divmod(m, KD)))
                        A_(f_hi[:, m % KD, a:TOK], act_f[m % 2][:, a:TOK], ACT.Copy).then_inc(*does("f_hi", (L, m)))
            norm(DEPTH, 1, CTX)
            for t in range(CTX // P, NT):
                key = ("y", t)
                round_weights(order[key] - 1)
                act.wait_ge(*full(key))
                if t >= 4:
                    act.wait_ge(*when(f"y_out{t % 2}", t - 2))
                A_(yout[:, t % 2, :], slot(key), ACT.Copy).then_inc(*frees(key))
                act.wait_ge(*read(key))
                act.dma_start(out[0, t * P - CTX:(t + 1) * P - CTX, :], yout[:, t % 2, :]).then_inc(*does(f"y_out{t % 2}", t, 16))
            for t in (NT - 2, NT - 1):
                act.wait_ge(*when(f"y_out{t % 2}", t))

        @block.vector
        def _(dve):
            def mul(o, a, b):
                return dve.tensor_tensor(o, a, b, ALU.mult)

            def lo(o, whole, hi):
                return dve.tensor_tensor(o, whole, hi.bitcast(F32), ALU.subtract)

            def fma(o, a, s, b, op0=ALU.mult, op1=ALU.add):
                return dve.scalar_tensor_tensor(o, a, s, b, op0, op1)

            dve.memset(parr[:, :, :], 0.0)
            dve.memset(epsc[:, :], EPS).then_inc(*does("cleared", 0))
            for i, v in enumerate((1.0, 1.0 / D, 1.0 / QR, 1.0 / KVR)):
                dve.memset(ones[:, i, :], v).then_inc(*does("dve_step"))
                dve.wait_ge(*last_())
            dve.memset(zeros[:, :], 0.0).then_inc(*does("dve_step"))
            dve.wait_ge(*last_())
            dve.tensor_copy(s_hi.rearrange("p k c -> p (k c)"), zeros[:, :]).then_inc(*does("dve_step"))
            dve.wait_ge(*last_())
            dve.wait_ge(*full("params"))
            dve.tensor_copy(sel_r[:, :], cst[:, C_SEL:C_SEL + 2]).then_inc(*does("dve_step"))
            dve.wait_ge(*last_())
            dve.tensor_copy(adab.rearrange("p l f -> p (l f)"), slot("params")[:, DEPTH * P:DEPTH * P + 96]).then_inc(*does("dve_step"))
            dve.wait_ge(*last_())
            dve.tensor_copy(par.rearrange("p l f -> p (l f)"), slot("params")[:, 0:DEPTH * P]).then_inc(*frees("params"))
            for t in range(NT):
                key = ("x", t)
                dve.wait_ge(*full(key))
                dve.tensor_copy(x[:, :, t * P:(t + 1) * P], slot(key).rearrange("p (k t) -> p k t", k=KD)).then_inc(*frees(key))
            dve.wait_ge(*when("silu_c", 0))
            cond = silc.rearrange("p v k -> p k v")
            dve.tensor_copy(s_hi[:, :, 0:2], cond).then_inc(*does("dve_step"))
            dve.wait_ge(*last_())
            lo(s_hi[:, :, 2:4], cond, s_hi[:, :, 0:2]).then_inc(*does("cond_split", 0))

            def ada(L):
                for j in range(25):
                    dve.wait_ge(*last_())
                    if j < 24:
                        for half in range(2):
                            s = tile_of[L, "ada", j, half]
                            dve.wait_ge(*when("w_hi", s))
                            lo(w_lo[:, s % 2, :], raw[:, s % NRAW, :], w_hi[:, s % 2, :]).then_inc(*does("w_lo_by_dve", s))
                        key = (L, "ada", j)
                        dve.wait_ge(*when("row_hi", (L, j)))
                        lo(row_lo[0:4, j % 2, :], slot(key)[0:4, 0:256], row_hi[0:4, j % 2, :]).then_inc(*frees(key))
                    if j >= 1:
                        key = (L, "adaT", j - 1)
                        f = 2 * (j - 1)
                        dve.wait_ge(*full(key))
                        dve.tensor_tensor(mods[:, L, f:f + 2, :],
                                               slot(key)[:, 0:4].rearrange("p (f v) -> p f v", v=2),
                                               adab[:, L, f:f + 2].unsqueeze(2).to_broadcast([P, 2, 2]), ALU.add).then_inc(*frees(key))
                dve.wait_ge(*read((L, "adaT", 23)))

            def norm(L, which, a):
                key = (L, "ms", which)
                if L < DEPTH:
                    sh0, sc0, g0 = ((0, 8, R_N1), (24, 32, R_N2))[which - 1]
                    fma(gsc[:, :, :], mods[:, L, sc0:sc0 + 8, :], 1.0,
                             par[:, L, g0:g0 + 8].unsqueeze(2).to_broadcast([P, 8, 2]), ALU.add, ALU.mult).then_inc(*does("dve_step"))
                    dve.wait_ge(*last_())
                dve.wait_ge(*read(key))
                dve.reciprocal(rstd[:, a:TOK], sdev[:, a:TOK]).then_inc(*does("dve_step"))
                dve.wait_ge(*last_())
                if L == DEPTH:
                    for k in range(KD):
                        fma(xf[:, k, a:TOK], x[:, k, a:TOK], par[:, 0, R_FG + k:R_FG + k + 1], rstd[:, a:TOK],
                                 ALU.mult, ALU.mult).then_inc(*does("x_scaled", k))
                    return
                for k in range(KD + 1):
                    dve.wait_ge(*last_())
                    if k < KD:
                        mul(sqx[:, k, a:TOK], x[:, k, a:TOK], rstd[:, a:TOK]).then_inc(*does("dve_step"))
                        dve.wait_ge(*last_())
                        for b, e, v in kinds(a):
                            ins = dve.tensor_scalar(sqx[:, k, b:e], sqx[:, k, b:e], gsc[:, k, v:v + 1],
                                                    mods[:, L, sh0 + k, v:v + 1], ALU.mult, ALU.add)
                            if e == TOK:
                                ins.then_inc(*does("h", (L, which, k)))
                            else:
                                ins.then_inc(*does("dve_step"))
                                dve.wait_ge(*last_())
                    if k:
                        dve.wait_ge(*when("h_hi", (L, which, k - 1)))
                        lo(h_lo[:, k - 1, a:TOK], sqx[:, k - 1, a:TOK], h_hi[:, k - 1, a:TOK]).then_inc(*does("h_lo", (L, which, k - 1)))

            def latent_norm(L, key, tiles_, g0, a, name):
                dve.wait_ge(*last_())
                dve.wait_ge(*read(key))
                dve.reciprocal(rstd[:, a:TOK], sdev[:, a:TOK]).then_inc(*does("dve_step"))
                dve.wait_ge(*last_())
                for f, src in enumerate(tiles_):
                    fma(lraw[:, src, a:TOK], lraw[:, src, a:TOK], par[:, L, g0 + f:g0 + f + 1], rstd[:, a:TOK],
                             ALU.mult, ALU.mult).then_inc(*does(name + "n", (L, f)))
                for f, src in enumerate(tiles_):
                    dve.wait_ge(*when(name + "n_hi", (L, f)))
                    lo(ln_lo[:, f, a:TOK], lraw[:, src, a:TOK], ln_hi[:, f, a:TOK]).then_inc(*does(name + "n_lo", (L, f)))

            def latent(L):
                a = first(L)
                cos, sin = cst[NOPE:QH, C_COS:C_COS + TOK], cst[NOPE:QH, C_SIN:C_SIN + TOK]
                latent_norm(L, (L, "kvms"), (0, 1), R_KG, 0, "kv")
                key = (L, "krot")
                dve.wait_ge(*full(key))
                dve.wait_ge(*read((L, "kr")))
                mul(kT[NOPE:QH, 2, :], cols(key, 0, NOPE, QH), sin).then_inc(*frees(key))
                mul(kT[NOPE:QH, 1, :], kT[NOPE:QH, 1, :], cos).then_inc(*does("dve_step"))
                dve.wait_ge(*last_())
                dve.tensor_tensor(kT[NOPE:QH, 3, :], kT[NOPE:QH, 1, :], kT[NOPE:QH, 2, :], ALU.add).then_inc(*does("dve_step"))
                dve.wait_ge(*last_())
                for h0, h1 in ((0, 3), (4, HEADS)):
                    ins = dve.tensor_copy(kT[NOPE:QH, h0:h1, :],
                                          kT[NOPE:QH, 3:4, :].to_broadcast([ROPE, h1 - h0, TOK]))
                    ins.then_inc(*does("k_rotated", L))
                for i in range(2):
                    for tp in range(NT // 2):
                        key = (L, "v", i, tp)
                        dve.wait_ge(*full(key))
                        dve.tensor_copy(vt[:, 2 * tp:2 * tp + 2, 256 * i:256 * i + 256],
                                             slot(key).rearrange("p (a b) -> p a b", b=HALF)[:, :, 0:256]).then_inc(*frees(key))
                latent_norm(L, (L, "qms"), (2, 3, 4), R_QG, a, "q")
                for h in range(HEADS):
                    dve.wait_ge(*last_())
                    dve.wait_ge(*when("q_copied", (L, h)))
                    ins = dve.tensor_copy(rrec[0:1, 0:1], slot((L, "q", h))[0:1, 0:1])
                    ins.then_inc(*frees((L, "q", h)))
                    key = (L, "qrot", h)
                    dve.wait_ge(*full(key))
                    mul(lraw[NOPE:QH, 0, a:TOK], cols(key, a, NOPE, QH), sin[:, a:TOK]).then_inc(*frees(key))
                    mul(qT[NOPE:QH, h, a:TOK], qT[NOPE:QH, h, a:TOK], cos[:, a:TOK]).then_inc(*does("dve_step"))
                    dve.wait_ge(*last_())
                    dve.tensor_tensor(qT[NOPE:QH, h, a:TOK], qT[NOPE:QH, h, a:TOK], lraw[NOPE:QH, 0, a:TOK],
                                           ALU.add).then_inc(*does("q_rotated", (L, h)))

            def attention(L):
                items = att_items(L)
                for n in range(len(items) + 3):
                    dve.wait_ge(*last_())
                    if n < len(items):
                        h, qt = items[n]
                        key = (L, "s", h, qt)
                        end = CTX if qt < 2 else TOK
                        dve.wait_ge(*full(key))
                        if n >= 2:
                            dve.wait_ge(*read((L, "s") + items[n - 2]))
                        dve.reduce_max(rmax[:, n % 2:n % 2 + 1], slot(key)[:, T0:T0 + end], AX.X, negate=True).then_inc(*does("row_max", (L, h, qt)))
                    if 1 <= n <= len(items):
                        h, qt = items[n - 1]
                        i = (n - 1) % 2
                        end = CTX if qt < 2 else TOK
                        dve.wait_ge(*read((L, "s", h, qt)))
                        dve.reciprocal(rrec[:, i:i + 1], rsum[:, i:i + 1]).then_inc(*does("dve_step"))
                        dve.wait_ge(*last_())
                        dve.tensor_scalar(probs[i][:, 0:end], probs[i][:, 0:end], rrec[:, i:i + 1], None, ALU.mult).then_inc(*does("probs", (L, h, qt)))
                    if n >= 3 and items[n - 3][1] == NT - 1:
                        h = items[n - 3][0]
                        p = (h % 2) * VD
                        dve.wait_ge(*when("values_hi", (L, h)))
                        lo(br_lo[p:p + VD, h // 2, first(L):TOK], cols((L, "o", h), first(L), p, p + VD),
                                br_hi[p:p + VD, h // 2, first(L):TOK]).then_inc(*frees((L, "o", h)))

            def branch_lo(L, k, f, src):
                a = first(L)
                dve.wait_ge(*when("branch_hi", (L, k, f)))
                lo(br_lo[:, f, a:TOK], src[:, a:TOK], br_hi[:, f, a:TOK]).then_inc(*does("branch_lo", (L, k, f)))

            def merge(L, k):
                a = first(L)
                for f in range(KD):
                    key = (L, "proj", k, f)
                    dve.wait_ge(*last_())
                    dve.wait_ge(*full(key))
                    dve.wait_ge(*read((L, "gate", k, f)))
                    if k == 0:
                        mul(merged[:, f, a:TOK], cols(key, a), sigm[:, f % 2, a:TOK]).then_inc(*frees(key))
                    else:
                        mul(gated[:, a:TOK], cols(key, a), sigm[:, f % 2, a:TOK]).then_inc(*frees(key))
                        dve.wait_ge(*read(key))
                        dve.tensor_tensor(merged[:, f, a:TOK], merged[:, f, a:TOK], gated[:, a:TOK], ALU.add).then_inc(*does("merged", (L, k, f)))

            def convolve(o, src, taps, width, bias, a, signal):
                mid = width // 2
                steps = []
                if bias is None:
                    dve.tensor_scalar(o[:, a:TOK], src(a, TOK), taps(mid), None, ALU.mult).then_inc(*does("dve_step"))
                    dve.wait_ge(*last_())
                else:
                    dve.tensor_scalar(o[:, a:TOK], src(a, TOK), taps(mid), bias, ALU.mult, ALU.add).then_inc(*does("dve_step"))
                    dve.wait_ge(*last_())
                for k in [k for k in range(width) if k != mid]:
                    s = k - mid
                    for b, e, _ in kinds(a):
                        steps.append((b + max(0, -s), e - max(0, s), s, k))
                for n, (b, e, s, k) in enumerate(steps):
                    ins = fma(o[:, b:e], src(b + s, e + s), taps(k), o[:, b:e])
                    if n < len(steps) - 1:
                        ins.then_inc(*does("dve_step"))
                        dve.wait_ge(*last_())
                ins.then_inc(*signal())

            def short_conv(L):
                a = first(L)
                for f in range(KB):
                    key = (L, "xin", f)
                    dve.wait_ge(*last_())
                    dve.wait_ge(*full(key))
                    dve.wait_ge(*read((L, "cg", f)))
                    g, o = cgx[:, f % 2, :], cvo[:, f % 2, :]
                    mul(g[:, a:TOK], cols(key, a), cgs[:, f % 2, a:TOK]).then_inc(*frees(key))
                    dve.wait_ge(*read(key))
                    convolve(o, lambda b, e: g[:, b:e], lambda k: par[:, L, R_SW + 4 * k + f:R_SW + 4 * k + f + 1], 3,
                             None, a, lambda: does("dve_step"))
                    dve.wait_ge(*last_())
                    key = (L, "bg", f)
                    dve.wait_ge(*full(key))
                    mul(o[:, a:TOK], cols(key, a), o[:, a:TOK]).then_inc(*frees(key))
                    branch_lo(L, 1, f, o)

            def fourier(L):
                a = first(L)
                dve.wait_ge(*when("channel_hi", L))
                lo(ch_lo[:, :], cst[:, C_CHAN:C_CHAN + 256], ch_hi[:, :]).then_inc(*does("channel_dft", L))
                for g in range(5):
                    dve.wait_ge(*last_())
                    if g < 4:
                        key = (L, "fn", g)
                        dve.wait_ge(*when("fn_hi", (L, g)))
                        lo(fn_lo[:, a:TOK], cols(key, a), fn_hi[:, a:TOK]).then_inc(*frees(key))
                    if g >= 1:
                        key = (L, "fo", g - 1)
                        dve.wait_ge(*when("fourier_hi", (L, g - 1)))
                        parts = fourier_parts(L)
                        for n, (_, _, t0, nt, _, scale) in enumerate(parts):
                            ins = fma(br_lo[:, g - 1, t0:t0 + nt], slot(key)[:, T0 + t0:T0 + t0 + nt], scale,
                                      br_hi[:, g - 1, t0:t0 + nt].bitcast(F32), ALU.mult, ALU.subtract)
                            if n < len(parts) - 1:
                                ins.then_inc(*does("dve_step"))
                                dve.wait_ge(*last_())
                        ins.then_inc(*frees(key))

            def steps(L):
                key = (L, "dtT")
                dve.wait_ge(*last_())
                dve.wait_ge(*full(key))
                raw_ = slot(key)[:, 0:32 * NT].rearrange("p (t c) -> p t c", c=32)
                for d in range(2):
                    bias = heads_bc[:, L, 16 + 8 * d:24 + 8 * d].unsqueeze(1).to_broadcast([P, NT, 8])
                    ins = dve.tensor_tensor(dts[:, 0, d, :, :], raw_[:, :, 8 * d:8 * d + 8], bias, ALU.add)
                    if d == 0:
                        ins.then_inc(*does("dve_step"))
                        dve.wait_ge(*last_())
                ins.then_inc(*frees(key))
                dve.wait_ge(*read(key))
                v = [dts[:, i, :, :, :].rearrange("p d t h -> p (d t h)") for i in range(6)]
                fma(v[1], v[0], -1.0, v[0], ALU.mult, ALU.max).then_inc(*does("dt_abs", L))

            def steps_end(L):
                v = [dts[:, i, :, :, :].rearrange("p d t h -> p (d t h)") for i in range(6)]
                dve.wait_ge(*when("dt_exp", L))
                dve.tensor_scalar(v[2], v[1], 1.0, None, ALU.add).then_inc(*does("dt_one", L))
                dve.wait_ge(*when("dt_one", L))
                dve.tensor_scalar(v[3], v[2], -1.0, None, ALU.add).then_inc(*does("dve_step"))
                dve.wait_ge(*last_())
                dve.tensor_scalar(v[5], v[3], 0.0, None, ALU.is_equal).then_inc(*does("dve_step"))
                dve.wait_ge(*last_())
                dve.wait_ge(*when("dt_ln", L))
                dve.tensor_tensor(v[4], v[4], v[5], ALU.add).then_inc(*does("dve_step"))
                dve.wait_ge(*last_())
                mul(v[4], v[4], v[1]).then_inc(*does("dve_step"))
                dve.wait_ge(*last_())
                dve.tensor_tensor(v[3], v[3], v[5], ALU.add).then_inc(*does("dve_step"))
                dve.wait_ge(*last_())
                dve.reciprocal(v[2], v[3]).then_inc(*does("dve_step"))
                dve.wait_ge(*last_())
                mul(v[4], v[4], v[2]).then_inc(*does("dve_step"))
                dve.wait_ge(*last_())
                fma(v[0], v[0], 0.0, v[4], ALU.max, ALU.add).then_inc(*does("dve_step"))
                dve.wait_ge(*last_())
                for d in range(2):
                    rate = heads_bc[:, L, 8 * d:8 * d + 8].unsqueeze(1).to_broadcast([P, NT, 8])
                    fma(dts[:, 3, d, :, :], dts[:, 0, d, :, :], -1.0, rate, ALU.mult, ALU.mult).then_inc(*does("la", L))

            def ssd(L):
                a = first(L)
                for f in range(KD + 1):
                    dve.wait_ge(*last_())
                    if f < KD:
                        key = (L, "xbc", f)
                        dve.wait_ge(*full(key))
                        if f >= 2:
                            dve.wait_ge(*when("conv_silu", (L, f - 2)))
                        if f == 1:
                            steps(L)
                        convolve(cacc[f % 2], lambda b, e: slot(key)[:, T0 + b:T0 + e],
                                 lambda k: par[:, L, R_CW + 8 * k + f:R_CW + 8 * k + f + 1], 5,
                                 par[:, L, R_CB + f:R_CB + f + 1], 0, lambda: frees(key))
                    if 1 <= f <= 6:
                        key = (L, "xT", f - 1)
                        dve.wait_ge(*full(key))
                        dst = xs_tok[:, :, (f - 1) * P:f * P] if f - 1 < 4 else b_tok[:, :, (f - 5) * P:(f - 4) * P]
                        dve.tensor_copy(dst, slot(key)[:, 0:TOK].rearrange("p (t c) -> p t c", t=NT)).then_inc(*frees(key))
                steps_end(L)

                def by_head(ap, n=64):
                    return ap.rearrange("p (h c) -> p h c", c=n)

                def wide(ap, n=64):
                    return ap.unsqueeze(2).to_broadcast([P, 8, n])

                for f in range(4):
                    dve.wait_ge(*read((L, "xT", f)))
                for c in range(a // P, NT):
                    mul(by_head(y_tok[:, c, :]), by_head(xs_tok[:, c, :]), wide(heads_bc[:, L, 32:40])).then_inc(*does("dve_step"))
                    dve.wait_ge(*last_())
                key = (L, "laT")
                dve.wait_ge(*full(key))
                for d in range(2):
                    rows = slice(64 * d, 64 * d + ROWS)
                    ins = dve.tensor_copy(laR[rows, :] if d == 0 else laR[rows, ::-1], slot(key)[rows, 0:P])
                    if d == 0:
                        ins.then_inc(*does("dve_step"))
                        dve.wait_ge(*last_())
                ins.then_inc(*frees(key))
                dve.wait_ge(*read(key))
                for d in range(2):
                    rows = slice(64 * d, 64 * d + ROWS)
                    o = diff[rows, 0, :]
                    keep = cst[rows, C_KEEP:C_KEEP + P]
                    dve.tensor_tensor_scan(o, keep, laR[rows, :], 0.0, ALU.mult, ALU.add).then_inc(*does("dve_step"))
                    dve.wait_ge(*last_())
                    ends = diff[rows, 0, SUM_BLOCK - 1:P:SUM_BLOCK]
                    dve.tensor_tensor_scan(blkR[rows, :], ones[rows, 0, 0:P // SUM_BLOCK], ends, 0.0,
                                                ALU.mult, ALU.add).then_inc(*does("dve_step"))
                    dve.wait_ge(*last_())
                    dve.tensor_tensor(diff[rows, 0, SUM_BLOCK:P].rearrange("p (b i) -> p b i", i=SUM_BLOCK),
                                           diff[rows, 0, SUM_BLOCK:P].rearrange("p (b i) -> p b i", i=SUM_BLOCK),
                                           blkR[rows, 0:P // SUM_BLOCK - 1].unsqueeze(2).to_broadcast(
                                               [ROWS, P // SUM_BLOCK - 1, SUM_BLOCK]), ALU.add).then_inc(*does("dve_step"))
                    dve.wait_ge(*last_())
                    dve.tensor_copy(cumR[rows, :], o if d == 0 else diff[rows, 0, ::-1]).then_inc(*does("cum_rows", L))
                key = (L, "cum")
                dve.wait_ge(*full(key))
                sums = [exin[:, i, :, :, :].rearrange("p d t h -> p (d t h)") for i in range(3)]
                dve.tensor_copy(sums[0].rearrange("p (d r) -> p d r", d=2),
                                     slot(key).rearrange("p (d c) -> p d c", d=2)[:, :, 0:ROWS]).then_inc(*frees(key))
                dve.wait_ge(*read(key))
                key = (L, "tot")
                dve.wait_ge(*full(key))
                dve.tensor_copy(sums[2], slot(key)[:, 0:2 * ROWS]).then_inc(*does("dve_step"))
                dve.wait_ge(*last_())
                dve.tensor_tensor(sums[1], slot(key)[:, 0:2 * ROWS], sums[0], ALU.subtract).then_inc(*frees(key))
                dve.wait_ge(*when("decays", L))
                mul(dterm[:, :, :, :].rearrange("p d t h -> p (d t h)"),
                         dts[:, 0, :, :, :].rearrange("p d t h -> p (d t h)"),
                         ex[:, 1, :, :, :].rearrange("p d t h -> p (d t h)")).then_inc(*does("dve_step"))
                dve.wait_ge(*last_())
                items = ssd_items(L)
                prev_seg, prev_state = [None], [None]

                def prepare(n):
                    d, c, want, has, gives = items[n]
                    dve.wait_ge(*last_())
                    if want:
                        key = (L, "cb", d, c)
                        mask = cst[:, (C_U, C_L)[d]:(C_U, C_L)[d] + P].unsqueeze(1).to_broadcast([P, 2, P])
                        dve.wait_ge(*full(key))
                        mul(cbm[:, n % 2, :, :], slot(key)[:, 0:256].rearrange("p (g i) -> p g i", g=2), mask).then_inc(*frees(key))
                        if prev_seg[0]:
                            dve.wait_ge(*when("seg_exp", prev_seg[0]))
                        key = (L, "seg", d, c)
                        dve.wait_ge(*full(key))
                        dve.tensor_tensor(diff[:, :, :], slot(key).rearrange("p (h i) -> p h i", h=8),
                                               wide(exin[:, 0, d, c, :], P), ALU.subtract).then_inc(*frees(key))
                        dve.wait_ge(*read(key))
                        dve.tensor_scalar(diff[:, :, :], diff[:, :, :], 0.0, None, ALU.min).then_inc(*does("diff", (L, d, c)))
                        prev_seg[0] = (L, d, c)
                    if gives:
                        if prev_state[0]:
                            dve.wait_ge(*full(prev_state[0]))
                        mul(by_head(xr[:, :]), by_head(xs_tok[:, c, :]), wide(dterm[:, d, c, :])).then_inc(*does("xr", (L, d, c)))
                        prev_state[0] = (L, "state", d, c)

                prepare(0)
                for n, (d, c, want, has, gives) in enumerate(items):
                    if n + 1 < len(items):
                        prepare(n + 1)
                    if want:
                        mul(by_head(xd[:, :]), by_head(xs_tok[:, c, :]), wide(dts[:, 0, d, c, :])).then_inc(*does("dve_step"))
                        dve.wait_ge(*last_())
                        dve.wait_ge(*when("seg_exp", (L, d, c)))
                        for g in range(2):
                            mul(seg[:, 4 * g:4 * g + 4, :], seg[:, 4 * g:4 * g + 4, :],
                                     cbm[:, n % 2, g:g + 1, :].to_broadcast([P, 4, P])).then_inc(*does("seg_masked", (L, d, c)))
                    dve.wait_ge(*last_())
                    if gives:
                        key = (L, "state", d, c)
                        dve.wait_ge(*full(key))
                        if has:
                            mul(by_head(decayed[:, :]), by_head(st[:, (n - 1) % 2, :]), wide(ex[:, 2, d, c, :])).then_inc(*does("dve_step"))
                            dve.wait_ge(*last_())
                            ins = dve.tensor_tensor(st[:, n % 2, :], slot(key)[:, 0:BW], decayed[:, :], ALU.add)
                        else:
                            ins = dve.tensor_copy(st[:, n % 2, :], slot(key)[:, 0:BW])
                        ins.then_inc(*frees(key))
                        dve.wait_ge(*read(key))
                    if want:
                        key = (L, "y", d, c)
                        dve.wait_ge(*last_())
                        dve.wait_ge(*full(key))
                        if has:
                            mul(by_head(yo[:, :]), by_head(slot(key)[:, HALF:2 * HALF]), wide(ex[:, 0, d, c, :])).then_inc(*does("dve_step"))
                            dve.wait_ge(*last_())
                            dve.tensor_tensor(y_tok[:, c, :], y_tok[:, c, :], yo[:, :], ALU.add).then_inc(*does("dve_step"))
                            dve.wait_ge(*last_())
                        dve.tensor_tensor(y_tok[:, c, :], slot(key)[:, 0:BW], y_tok[:, c, :], ALU.add).then_inc(*frees(key))
                for f in range(KB):
                    dve.wait_ge(*read((L, "z", f)))
                for c in range(a // P, NT):
                    key = (L, "yT", c)
                    dve.wait_ge(*full(key))
                    mul(zs[:, :, c * P:(c + 1) * P], slot(key)[:, 0:BW].rearrange("p (f t) -> p f t", f=KB),
                             zs[:, :, c * P:(c + 1) * P]).then_inc(*frees(key))
                for g in range(2):
                    dve.wait_ge(*last_())
                    dve.wait_ge(*read((L, "yms", g)))
                    dve.reciprocal(rstd[:, a:TOK], sdev[:, a:TOK]).then_inc(*does("dve_step"))
                    dve.wait_ge(*last_())
                    for f in range(2 * g, 2 * g + 2):
                        fma(zs[:, f, a:TOK], zs[:, f, a:TOK], par[:, L, R_SN + f:R_SN + f + 1], rstd[:, a:TOK],
                                 ALU.mult, ALU.mult).then_inc(*does("branch", (L, 3, f)))
                    for f in range(2 * g, 2 * g + 2):
                        branch_lo(L, 3, f, zs[:, f, :])

            def residual(L, key, f, gate, a):
                dve.wait_ge(*last_())
                dve.wait_ge(*full(key))
                for b, e, v in kinds(a):
                    ins = fma(x[:, f, b:e], slot(key)[:, T0 + b:T0 + e], mods[:, L, gate + f, v:v + 1], x[:, f, b:e])
                    if e < TOK:
                        ins.then_inc(*does("dve_step"))
                        dve.wait_ge(*last_())
                ins.then_inc(*frees(key))

            for L in range(DEPTH):
                a = first(L)
                ada(L)
                norm(L, 1, 0)
                latent(L)
                attention(L)
                merge(L, 0)
                short_conv(L)
                merge(L, 1)
                fourier(L)
                merge(L, 2)
                ssd(L)
                merge(L, 3)
                for k in range(KD):
                    dve.wait_ge(*when("merged_hi", (L, k)))
                    lo(h_lo[:, k, a:TOK], merged[:, k, a:TOK], h_hi[:, k, a:TOK]).then_inc(*does("merged_lo", (L, k)))
                dve.wait_ge(*when("x_back", L))
                for f in range(KD):
                    residual(L, (L, "out", f), f, 16, a)
                norm(L, 2, a)
                for c in range(4):
                    for f in range(KD + 1):
                        dve.wait_ge(*last_())
                        if f < KD:
                            n = c * KD + f
                            key = (L, "w1", c, f)
                            dve.wait_ge(*when("relu", (L, n)))
                            mul(act_f[n % 2][:, a:TOK], cols(key, a), act_r[:, n % 2, a:TOK]).then_inc(*frees(key))
                        if f:
                            m = c * KD + f - 1
                            dve.wait_ge(*when("f_hi", (L, m)))
                            lo(f_lo[:, f - 1, a:TOK], act_f[m % 2][:, a:TOK], f_hi[:, f - 1, a:TOK]).then_inc(*does("f_lo", (L, c, f - 1)))
                    for f in range(KD):
                        residual(L, (L, "w2", c, f), f, 40, a)
            norm(DEPTH, 1, CTX)
        return counts.table


_NAMES = ["x", "c", "ctx", "c_ctx", "ada_w", "ada_b", "norm1_g", "norm2_g", "w_in", "ssm_conv_w", "ssm_conv_b",
          "ssm_a_log", "ssm_dt_bias", "ssm_d", "ssm_norm_g", "sc_conv_w", "mla_qa_g", "mla_wqb", "mla_kva_g",
          "mla_wkvb", "w_branch", "w_out", "mlp_w1", "mlp_w2", "final_norm_g"]


def kernel(**inputs):
    import numpy as _np
    import concourse.bacc as _bacc
    from concourse.bass_utils import run_bass_kernel_spmd as _run

    tables, dft = constant_tables()
    given = {n: _np.ascontiguousarray(inputs[n]) for n in _NAMES}
    given["tables"], given["dft"] = tables, dft
    counts = None
    for _ in range(2):
        nc = _bacc.Bacc("TRN2", target_bir_lowering=False, num_devices=1)
        aps = {n: nc.dram_tensor(f"in_{n}_dram", a.shape, F32, kind="ExternalInput").ap() for n, a in given.items()}
        out = nc.dram_tensor("out_0_dram", (1, LAT, D), F32, kind="ExternalOutput").ap()
        counts = backbone(nc, aps, out, counts)
    r = _run(nc, [{f"in_{n}_dram": a for n, a in given.items()}], core_ids=[0])
    return r.results[0]["out_0_dram"]
```

```python
from contextlib import ExitStack

import numpy as np

import concourse.bass as bass
from concourse import mybir

P = 128
D = 1024
CTX = 256
LAT = 512
TOK = CTX + LAT
NT = TOK // P
GRID_W = 64
DEPTH = 2
DFF = 4 * D
EPS = 1e-6
BW = D // 2
KD = D // P
KB = BW // P
HEADS = 8
SSM_HD = 64
STATE = 128
NOPE, ROPE, VD = 64, 32, 64
QR, KVR = 384, 256
QH = NOPE + ROPE
SCALE = float(QH) ** -0.5
Z0 = 0
XBC0 = Z0 + BW
DT0 = XBC0 + 1024
SC0 = DT0 + 16
QA0 = SC0 + 3 * BW
KVA0 = QA0 + QR
KR0 = KVA0 + KVR
FN0 = KR0 + ROPE
GT0 = FN0 + BW
WT = 1024
NRAW = 4
NSLOT = 4
HALF = 512
T0 = HALF - CTX

F32 = mybir.dt.float32
F32R = mybir.dt.float32r
ALU = mybir.AluOpType
ACT = mybir.ActivationFunctionType
AX = mybir.AxisListType

SUM_BLOCK = 16
ROWS = NT * 8
C_ID, C_U, C_L, C_KEEP, C_ROT, C_CHAN = 0, 128, 256, 384, 512, 640
C_COS = C_CHAN + 256
C_SIN = C_COS + TOK
C_ALL = C_SIN + TOK
R_CW, R_CB, R_N1, R_N2, R_SN, R_SW, R_QG, R_KG, R_FG, R_C, R_CC, R_END = 0, 40, 48, 56, 64, 68, 80, 83, 85, 93, 101, 109


def constant_tables():
    t = np.zeros((P, C_ALL), np.float32)
    i = np.arange(P)
    t[:, C_ID:C_ID + P] = np.eye(P)
    t[:, C_U:C_U + P] = i[:, None] <= i[None, :]
    t[:, C_L:C_L + P] = i[:, None] >= i[None, :]
    t[:, C_KEEP:C_KEEP + P] = i[None, :] % SUM_BLOCK != 0
    nf = ROPE // 4
    for half in range(2):
        for f in range(nf):
            a = NOPE + 2 * nf * half + f
            t[a + nf, C_ROT + a] = -1.0
            t[a, C_ROT + a + nf] = 1.0
    w = 2 * np.pi * np.outer(i, i) / P
    t[:, C_CHAN:C_CHAN + P] = np.cos(w)
    t[:, C_CHAN + P:C_CHAN + 2 * P] = np.sin(w)
    tok = np.arange(LAT)
    inv = 10000.0 ** (-np.arange(nf) / nf)
    for half, pos in enumerate((tok // GRID_W, tok % GRID_W)):
        ang = inv[:, None] * pos[None, :]
        for part in range(2):
            a = NOPE + 2 * nf * half + nf * part
            t[a:a + nf, C_COS + CTX:C_COS + TOK] = np.cos(ang)
            t[a:a + nf, C_SIN + CTX:C_SIN + TOK] = np.sin(ang)
    t[NOPE:QH, C_COS:C_COS + CTX] = 1.0
    j = np.arange(LAT)
    w = 2 * np.pi * ((j[:, None] * j[None, :]) % LAT) / LAT
    dft = np.stack([np.cos(w), -np.sin(w)]).astype(np.float32)
    return t, dft


class Counts:

    def __init__(self, nc, ctx, known):
        self.nc, self.ctx, self.known, self.now, self.sems = nc, ctx, known or {}, {}, {}
        self.table, self.last = {}, None

    def sem(self, name):
        if name not in self.sems:
            self.sems[name] = self.ctx.enter_context(self.nc.semaphore(name))
            self.now[name] = 0
        return self.sems[name]

    def does(self, name, key=None, by=1):
        sem = self.sem(name)
        self.now[name] += by
        self.table[name, key] = self.now[name]
        self.last = sem, self.now[name]
        return sem, by

    def when(self, name, key):
        at = self.table.get((name, key)) or self.known.get((name, key))
        assert at or not self.known, (name, key)
        return self.sem(name), at or 1

    def mine(self):
        return self.last


def backbone(nc, A, out, known):
    ctx = ExitStack()
    with ctx:
        counts = Counts(nc, ctx, known)
        when, does, last_ = counts.when, counts.does, counts.mine

        def sb(name, shape, dt=F32, scope=ctx):
            return scope.enter_context(nc.sbuf_tensor(name, shape, dt))

        cst = sb("cst", [P, C_ALL])
        par = sb("par", [P, DEPTH, P])
        adab = sb("adab", [P, DEPTH, 48])
        mods = sb("mods", [P, DEPTH, 48, 2])
        gsc = sb("gsc", [P, 8, 2])
        heads_bc = sb("heads_bc", [P, DEPTH, 40])
        ones = sb("ones", [P, 4, P])
        epsc = sb("epsc", [P, 1])
        silc = sb("silc", [P, KD, 2])
        ksum = sb("ksum", [P, 2, 2, P])
        raw = sb("raw", [P, NRAW, WT])
        w_hi = sb("w_hi", [P, 2, WT], F32R)
        w_lo = sb("w_lo", [P, 2, WT], F32R)
        h_hi = sb("h_hi", [P, KD, TOK], F32R)
        h_lo = sb("h_lo", [P, KD, TOK], F32R)
        rstd = sb("rstd", [P, TOK])
        sdev = sb("sdev", [P, TOK])
        rmax = sb("rmax", [P, 2])
        rsum = sb("rsum", [P, 2])
        rrec = sb("rrec", [P, 2])
        psum = [ctx.enter_context(nc.psum_tensor(f"slot{i}", [P, 2 * HALF], F32)) for i in range(NSLOT)]

        with ExitStack() as m:
            br_hi = sb("br_hi", [P, KB, TOK], F32R, m)
            br_lo = sb("br_lo", [P, KB, TOK], F32R, m)
            with ExitStack() as q:
                kT = sb("kT", [P, HEADS, TOK], F32, q)
                vt = sb("vt", [P, NT, BW], F32, q)
                qT = sb("qT", [P, HEADS, TOK], F32, q)
                with ExitStack() as r:
                    ln_hi = sb("ln_hi", [P, 3, TOK], F32R, r)
                    ln_lo = sb("ln_lo", [P, 3, TOK], F32R, r)
                with ExitStack() as r:
                    pT = sb("pT", [P, NT, TOK], F32, r)
            sigm = sb("sigm", [P, 2, TOK], F32, m)
            gated = sb("gated", [P, TOK], F32, m)
            merged = sb("merged", [P, KD, TOK], F32, m)
            with ExitStack() as q:
                q.enter_context(nc.sbuf_tensor("past_mlp", [P, KD, TOK], F32))
                prod = sb("prod", [P, KD, P], F32, q)
            with ExitStack() as q:
                cgs = sb("cgs", [P, 2, TOK], F32, q)
                cgx = sb("cgx", [P, 2, TOK], F32, q)
                cvo = sb("cvo", [P, 2, TOK], F32, q)
            with ExitStack() as q:
                dft = sb("dft", [P, 2, 4, LAT], F32, q)
                ch_hi = sb("ch_hi", [P, 256], F32R, q)
                ch_lo = sb("ch_lo", [P, 256], F32R, q)
                fn_hi = sb("fn_hi", [P, TOK], F32R, q)
                fn_lo = sb("fn_lo", [P, TOK], F32R, q)
                fy = sb("fy", [P, NT, 256], F32, q)
            with ExitStack() as q:
                dts = sb("dts", [P, 6, 2, NT, 8], F32, q)
                ex = sb("ex", [P, 3, 2, NT, 8], F32, q)
                dterm = sb("dterm", [P, 2, NT, 8], F32, q)
                laR = sb("laR", [P, P], F32, q)
                cumR = sb("cumR", [P, P], F32, q)
                blkR = sb("blkR", [P, 8], F32, q)
                exin = sb("exin", [P, 3, 2, NT, 8], F32, q)
                xs_tok = sb("xs_tok", [P, NT, BW], F32, q)
                b_tok = sb("b_tok", [P, NT, 256], F32, q)
                y_tok = sb("y_tok", [P, NT, BW], F32, q)
                with ExitStack() as r:
                    bc = sb("bc", [P, 4, TOK], F32, r)
                with ExitStack() as r:
                    zs = sb("zs", [P, KB, TOK], F32, r)
        with ExitStack() as m:
            with ExitStack() as q:
                lraw = sb("lraw", [P, 5, TOK], F32, q)
                sql = sb("sql", [P, 3, TOK], F32, q)
            with ExitStack() as q:
                diff = sb("diff", [P, 8, P], F32, q)
                seg = sb("seg", [P, 8, P], F32, q)
                cbm = sb("cbm", [P, 2, 2, P], F32, q)
                xd = sb("xd", [P, 2, BW], F32, q)
                xr = sb("xr", [P, BW], F32, q)
                st = sb("st", [P, 2, BW], F32, q)
                yo = sb("yo", [P, BW], F32, q)
                decayed = sb("decayed", [P, BW], F32, q)
        with ExitStack() as m:
            x = sb("x", [P, KD, TOK], F32, m)
            with ExitStack() as q:
                sqx = sb("sqx", [P, KD, TOK], F32, q)
                parr = sb("parr", [P, DEPTH + 1, P], F32, q)
            with ExitStack() as q:
                xin = sb("xin", [P, 2, D], F32, q)
            with ExitStack() as q:
                f_hi = sb("f_hi", [P, KD, TOK], F32R, q)
                f_lo = sb("f_lo", [P, KD, TOK], F32R, q)
                act_r = sb("act_r", [P, 2, TOK], F32, q)
            with ExitStack() as q:
                yout = sb("yout", [P, 2, D], F32, q)
                xf = sb("xf", [P, KD, TOK], F32, q)
        y_sq = xs_tok[:, :, :].rearrange("p t c -> p (t c)").rearrange("p (k t) -> p k t", k=KB)
        act_f = [rstd, sdev]
        probs = [rstd, sdev]
        cacc = [gated, rstd]
        conv = sigm[:, 0, :]
        dtT = y_tok[:, :, :].rearrange("p t c -> p (t c)")[0:32, 0:TOK]

        x_spill = nc.dram_tensor("x_spill", (P, KD * TOK), F32, kind="Internal").ap()

        ADA_FIRST = range(0, 2 * KD, 2)
        ADA_LATER = [(0, f) for f in range(2 * KD, 6 * KD)] + [(1, f) for f in range(6 * KD)]
        ada_after = {}
        for k in range(4):
            for f in range(KD):
                ada_after[0, "gate", k, f] = len(ada_after)
        for c in range(4):
            for f in range(KD):
                ada_after[0, "w1", c, f] = len(ada_after)
            for f in range(0, KD, 2):
                ada_after[0, "w2", c, f] = len(ada_after)
        assert len(ada_after) == len(ADA_LATER)

        tiles, tile_of = [], {}

        def tile(key, src, k0, kt, c0, cols, pitch=0):
            tile_of[key] = len(tiles)
            tiles.append((src[k0 * P:(k0 + kt) * P, c0:c0 + cols].rearrange("(k p) c -> p k c", p=P), kt, cols,
                          pitch or cols))

        def ada_tile(n):
            if n < len(ADA_LATER):
                L, f = ADA_LATER[n]
                tile((L, "ada", f), A["ada_w"][L], 0, KD, P * f, P)

        def ada_tile_after(after):
            if after in ada_after:
                ada_tile(ada_after[after] + 1)

        def merge_tiles(L, k, branch):
            for j in range(4):
                for f in (2 * j, 2 * j + 1):
                    tile((L, "gate", k, f), A["w_in"][L], 0, KD, GT0 + D * branch + P * f, P)
                    ada_tile_after((L, "gate", k, f))
                tile((L, "proj", k, j), A["w_branch"][L, branch], 0, KB, 256 * j, 256)

        for L in range(DEPTH):
            win = A["w_in"][L]
            if L == 0:
                for f in range(2 * KD):
                    tile((L, "ada", f), A["ada_w"][L], 0, KD, P * f, P)
            for f in range(2):
                tile((L, "kva", f), win, 0, KD, KVA0 + P * f, P)
            tile((L, "kr"), win, 0, KD, KR0 - NOPE, P)
            for f in range(3):
                tile((L, "qa", f), win, 0, KD, QA0 + P * f, P)
            for i in range(2):
                tile((L, "wkv", i), A["mla_wkvb"][L], 0, 2, 512 * i, 512)
            for i in range(3):
                tile((L, "wq", i), A["mla_wqb"][L], 0, 3, 3 * QH * i, min(320, HEADS * QH - 3 * QH * i), 320)
            if L == 0:
                ada_tile(0)
            merge_tiles(L, 0, 2)
            for f in range(KB):
                tile((L, "cg", f), win, 0, KD, SC0 + BW + P * f, P)
                tile((L, "xin", f), win, 0, KD, SC0 + 2 * BW + P * f, P)
                tile((L, "bg", f), win, 0, KD, SC0 + P * f, P)
            merge_tiles(L, 1, 1)
            for f in range(KB):
                tile((L, "fn", f), win, 0, KD, FN0 + P * f, P)
            merge_tiles(L, 2, 3)
            tile((L, "dt"), win, 0, KD, DT0, P)
            for f in range(KD):
                tile((L, "xbc", f), win, 0, KD, XBC0 + P * f, P)
            for f in range(KB):
                tile((L, "z", f), win, 0, KD, Z0 + P * f, P)
            merge_tiles(L, 3, 0)
            for f in range(KD):
                tile((L, "out", f), A["w_out"][L], 0, KD, P * f, P)
            for c in range(4):
                for f in range(KD):
                    tile((L, "w1", c, f), A["mlp_w1"][L], 0, KD, D * c + P * f, P)
                    ada_tile_after((L, "w1", c, f))
                for f in range(KD):
                    tile((L, "w2", c, f), A["mlp_w2"][L], KD * c, KD, P * f, P)
                    ada_tile_after((L, "w2", c, f))
        whole = {s for key, s in tile_of.items() if key[1] == "ada"}
        split = [s for s in range(len(tiles)) if s not in whole]
        place = {s: n for n, s in enumerate(split)}

        ALL = [(T0, 0, CTX), (HALF, CTX, LAT)]
        LATS = ALL[1:]

        def spans(L):
            return ALL if L < DEPTH - 1 else LATS

        def first(L):
            return 0 if L < DEPTH - 1 else CTX

        def kinds(a):
            return ([(0, CTX, 1)] if a == 0 else []) + [(CTX, TOK, 0)]

        order, last_use = {}, {}

        def slot(key):
            return psum[order[key] % NSLOT][:, :]

        def cols(key, a, p0=0, p1=P):
            return slot(key)[p0:p1, T0 + a:T0 + TOK]

        slot_full = counts.sem("slot_full")
        slot_read = [counts.sem(f"slot{i}_read") for i in range(NSLOT)]

        def full(key):
            return slot_full, order[key] + 1

        def frees(key):
            counts.last = slot_read[order[key] % NSLOT], order[key] // NSLOT + 1
            return slot_read[order[key] % NSLOT], 1

        def read(key):
            return slot_read[order[key] % NSLOT], order[key] // NSLOT + 1

        block = ctx.enter_context(nc.Block())

        def att_items(L):
            return [(h, qt) for h in range(HEADS) for qt in range(first(L) // P, NT)]

        def ssd_items(L):
            return [(d, c, c * P >= first(L), n > 0, n < NT - 1)
                    for d, chunks in enumerate(((0, 1, 2, 3, 4, 5), (1, 0, 5, 4, 3, 2))) for n, c in enumerate(chunks)]

        def fourier_parts(L):
            parts = [(0, 2, 0, CTX, 2, (CTX * P) ** -0.5), (2, 4, CTX, LAT, 1, (LAT * P) ** -0.5)]
            return parts[first(L) // CTX:]

        @block.tensor
        def _(pe):
            ident = cst[:, C_ID:C_ID + P]

            def take(key):
                order[key] = len(order)
                if order[key] >= NSLOT:
                    pe.wait_ge(slot_read[order[key] % NSLOT], order[key] // NSLOT)
                return slot(key)

            def weights(wkey, key):
                s = tile_of[wkey]
                pe.wait_ge(*when("w_lo", s))
                last_use[s] = order[key]
                _, kt, _, pitch = tiles[s]
                return [w[:, place[s] % 2, 0:kt * pitch].rearrange("p (k c) -> p k c", k=kt) for w in (w_hi, w_lo)]

            def product(key, wkey, kts, col, a_hi, a_lo, sp, ready=None, backwards=False):
                o = take(key)
                wh, wl = weights(wkey, key)
                rows = range(kts)[::-1 if backwards else 1]
                for k in rows:
                    if ready:
                        ready(k)
                    for n, (w, a) in enumerate(((wh, a_hi), (wh, a_lo), (wl, a_hi))):
                        for c0, t0, nt in sp:
                            last = pe.matmul(o[:, c0:c0 + nt], w[:, k, col:col + P], a[:, k, t0:t0 + nt],
                                             start=(k == rows[0] and n == 0), stop=(k == rows[-1] and n == 2))
                last.then_inc(slot_full, 1)

            def mean_square(key, src, k0, k1, mat, sp, name, tag):
                o = take(key)
                for k in range(k0, k1):
                    pe.wait_ge(*when(name, (tag, k)))
                    for c0, t0, nt in sp:
                        last = pe.matmul(o[:, c0:c0 + nt], ones[:, mat, :], src[:, k, t0:t0 + nt],
                                         start=(k == k0), stop=(k == k1 - 1))
                last.then_inc(slot_full, 1)

            def turn(key, blocks, to=P):
                o = take(key)
                for n, b in enumerate(blocks):
                    last = pe.transpose(o[:, n * to:(n + 1) * to], b, ident if to == P else cst[0:to, C_ID:C_ID + to])
                last.then_inc(slot_full, 1)

            def ada_first():
                pe.wait_ge(*when("silu_c", 0))
                for f in ADA_FIRST:
                    o = take((0, "ada", f))
                    for i in range(2):
                        s = tile_of[0, "ada", f + i]
                        last_use[s] = order[0, "ada", f]
                        pe.wait_ge(counts.sem(f"raw{s % NRAW}_loaded"), 16 * (s // NRAW + 1))
                        w = raw[:, s % NRAW, :].rearrange("p (k c) -> p k c", k=KD)
                        for k in range(KD):
                            last = pe.matmul(o[:, 2 * i:2 * i + 2], w[:, k, :], silc[:, k, :],
                                             start=(k == 0), stop=(k == KD - 1))
                    last.then_inc(slot_full, 1)

            def ada_sum(after):
                if after not in ada_after:
                    return
                n = ada_after[after]
                if n == 0:
                    last_use[tile_of[(0, "ada", ADA_LATER[0][1])]] = order[0, "o", HEADS - 1]
                pe.wait_ge(*when("ada_ksum", n))
                o = take(("ada", n))
                for v in range(2):
                    last = pe.matmul(o[:, v:v + 1], ksum[:, n % 2, v, :], ones[:, 0, 0:1], start=True, stop=True)
                last.then_inc(slot_full, 1)
                if n + 1 < len(ADA_LATER):
                    L, f = ADA_LATER[n + 1]
                    last_use[tile_of[L, "ada", f]] = order["ada", n]

            def rotated(key, src, h, sp):
                o = take(key)
                for c0, t0, nt in sp:
                    last = pe.matmul(o[:, c0:c0 + nt], cst[NOPE:QH, C_ROT:C_ROT + P], src[NOPE:QH, h, t0:t0 + nt],
                                     start=True, stop=True)
                last.then_inc(slot_full, 1)

            def latent(L):
                sp = spans(L)
                for f in range(2):
                    product((L, "kva", f), (L, "kva", f), KD, 0, h_hi, h_lo, ALL,
                            (lambda k: pe.wait_ge(*when("h_lo", (L, 1, k)))) if f == 0 else None)
                product((L, "kr"), (L, "kr"), KD, 0, h_hi, h_lo, ALL)
                mean_square((L, "kvms"), sql, 0, 2, 3, ALL, "kv_squared", L)
                pe.wait_ge(*when("kr_copied", L))
                rotated((L, "krot"), kT, 0, ALL)
                for f in range(3):
                    product((L, "qa", f), (L, "qa", f), KD, 0, h_hi, h_lo, sp)
                for i in range(2):
                    for h in range(4 * i, 4 * i + 4):
                        product((L, "k", h), (L, "wkv", i), 2, P * (h % 4), ln_hi, ln_lo, ALL,
                                (lambda k: pe.wait_ge(*when("kvn_lo", (L, k)))) if h == 0 else None)
                    if i == 0:
                        mean_square((L, "qms"), sql, 0, 3, 2, sp, "q_squared", L)
                    for tp in range(NT // 2):
                        o = take((L, "v", i, tp))
                        wh, wl = [w.rearrange("p k (h c) -> p k h c", h=4)
                                  for w in weights((L, "wkv", i), (L, "v", i, tp))]
                        for u in range(2):
                            t = 2 * tp + u
                            for k in range(2):
                                for n, (a, w) in enumerate(((ln_hi, wh), (ln_hi, wl), (ln_lo, wh))):
                                    last = pe.matmul(o[:, HALF * u:HALF * u + 256], a[:, k, t * P:(t + 1) * P],
                                                     w[:, k, :, NOPE:NOPE + VD], start=(k == 0 and n == 0),
                                                     stop=(k == 1 and n == 2))
                        last.then_inc(slot_full, 1)
                for h in range(HEADS + 1):
                    if h < HEADS:
                        product((L, "q", h), (L, "wq", h // 3), 3, QH * (h % 3), ln_hi, ln_lo, sp,
                                (lambda k: pe.wait_ge(*when("qn_lo", (L, k)))) if h == 0 else None)
                    if h >= 1:
                        pe.wait_ge(*when("q_copied", (L, h - 1)))
                        rotated((L, "qrot", h - 1), qT, h - 1, sp)

            def attention(L):
                items = att_items(L)

                def scores(h, qt):
                    if (h, qt) == items[0]:
                        pe.wait_ge(*when("k_rotated", L))
                    if qt == items[0][1]:
                        pe.wait_ge(*when("q_rotated", (L, h)))
                        pe.wait_ge(*read((L, "k", h)))
                    o = take((L, "s", h, qt))
                    for c0, t0, nt in ALL[:1] if qt < 2 else ALL:
                        last = pe.matmul(o[:, c0:c0 + nt], qT[0:QH, h, qt * P:(qt + 1) * P],
                                         kT[0:QH, h, t0:t0 + nt], start=True, stop=True)
                    last.then_inc(slot_full, 1)

                def values(h):
                    o = take((L, "o", h))
                    for qt in range(items[0][1], NT):
                        pe.wait_ge(*read((L, "pT", h, qt)))
                    lo = (h % 2) * VD
                    for c0, q0, nq in spans(L):
                        kts = NT if q0 else 2
                        for k in range(kts):
                            if h == 0:
                                pe.wait_ge(*read((L, "v", 0, k // 2)))
                            if h == 4:
                                pe.wait_ge(*read((L, "v", 1, k // 2)))
                            last = pe.matmul(o[lo:lo + VD, c0:c0 + nq], vt[:, k, h * VD:(h + 1) * VD],
                                             pT[:, k, q0:q0 + nq], start=(k == 0), stop=(k == kts - 1))
                    last.then_inc(slot_full, 1)

                for n in range(len(items) + 3):
                    if n < len(items):
                        scores(*items[n])
                    if n >= 3 and items[n - 3][1] == NT - 1:
                        values(items[n - 3][0])
                    if 2 <= n < len(items) + 2:
                        h, qt = items[n - 2]
                        pe.wait_ge(*when("probs", (L, h, qt)))
                        turn((L, "pT", h, qt), [probs[n % 2][:, k * P:(k + 1) * P] for k in range(2 if qt < 2 else NT)])

            def branch_ready(L, k, i):
                if k == 0:
                    pe.wait_ge(*read((L, "o", 2 * i)))
                    pe.wait_ge(*read((L, "o", 2 * i + 1)))
                elif k == 2:
                    pe.wait_ge(*read((L, "fo", i)))
                else:
                    pe.wait_ge(*when("branch_lo", (L, k, i)))

            def merge(L, k):
                sp = spans(L)
                for j in range(4):
                    for f in (2 * j, 2 * j + 1):
                        product((L, "gate", k, f), (L, "gate", k, f), KD, 0, h_hi, h_lo, sp)
                        ada_sum((L, "gate", k, f))
                    for f in (2 * j, 2 * j + 1):
                        product((L, "proj", k, f), (L, "proj", k, j), KB, P * (f % 2), br_hi, br_lo, sp,
                                (lambda i: branch_ready(L, k, i)) if f == 0 else None)

            def short_conv(L):
                for f in range(KB):
                    for what in ("cg", "xin", "bg"):
                        product((L, what, f), (L, what, f), KD, 0, h_hi, h_lo, spans(L))

            def fourier(L):
                pairs = range(first(L) // CTX, NT // 2)
                product((L, "fn", 0), (L, "fn", 0), KD, 0, h_hi, h_lo, spans(L))
                pe.wait_ge(*when("channel_dft", L))
                for g in range(4):
                    pe.wait_ge(*read((L, "fn", g)))
                    for tp in pairs:
                        o = take((L, "fy", g, tp))
                        for u in range(2):
                            t = 2 * tp + u
                            for n, (a, b) in enumerate(((fn_hi, ch_hi), (fn_hi, ch_lo), (fn_lo, ch_hi))):
                                last = pe.matmul(o[:, HALF * u:HALF * u + 256], a[:, t * P:(t + 1) * P], b[:, :],
                                                 start=(n == 0), stop=(n == 2))
                        last.then_inc(slot_full, 1)
                    if g < 3:
                        product((L, "fn", g + 1), (L, "fn", g + 1), KD, 0, h_hi, h_lo, spans(L))
                    else:
                        pe.wait_ge(*when("dft_loaded", L))
                    if g == 0:
                        pe.wait_ge(*when("dft_loaded", L))
                    for tp in pairs:
                        pe.wait_ge(*read((L, "fy", g, tp)))
                    o = take((L, "fo", g))
                    for tile0, n_t, t0, nt, step, _ in fourier_parts(L):
                        for j in range(n_t):
                            for part in range(2):
                                last = pe.matmul(o[:, T0 + t0:T0 + t0 + nt], fy[:, tile0 + j, part * P:(part + 1) * P],
                                                 dft[:, part, j, 0:LAT:step], start=(j == 0 and part == 0),
                                                 stop=(j == n_t - 1 and part == 1))
                    last.then_inc(slot_full, 1)

            def cum_turned(L):
                pe.wait_ge(*when("cum_rows", L))
                o = take((L, "cum"))
                for d in range(2):
                    last = pe.matmul(o[:, HALF * d:HALF * d + ROWS], cumR[64 * d:64 * d + ROWS, :],
                                     cst[64 * d:64 * d + ROWS, C_ID + 64 * d:C_ID + 64 * d + ROWS],
                                     start=True, stop=True)
                last.then_inc(slot_full, 1)

            def ssd(L):
                product((L, "dt"), (L, "dt"), KD, 0, h_hi, h_lo, ALL, backwards=True)
                for f in range(KD):
                    product((L, "xbc", f), (L, "xbc", f), KD, 0, h_hi, h_lo, ALL)
                    if f == 0:
                        pe.wait_ge(*read((L, "dt")))
                        turn((L, "dtT"), [dtT[0:32, t * P:(t + 1) * P] for t in range(NT)], 32)
                    if 1 <= f <= 6:
                        pe.wait_ge(*when("conv_silu", (L, f - 1)))
                        src = conv if f - 1 < 4 else bc[:, f - 5, :]
                        turn((L, "xT", f - 1), [src[:, t * P:(t + 1) * P] for t in range(NT)])
                    if f == 5:
                        pe.wait_ge(*when("la", L))
                        o = take((L, "laT"))
                        la = dts[:, 3, :, :, :].rearrange("p d t h -> p d (t h)")
                        for d in range(2):
                            last = pe.matmul(o[64 * d:64 * d + ROWS, 0:P], la[:, d, :], ident, start=True, stop=True)
                        last.then_inc(slot_full, 1)
                    if f == 6:
                        cum_turned(L)
                pe.wait_ge(*read((L, "cum")))
                o = take((L, "tot"))
                for d, end in enumerate((P - 1, 0)):
                    last = pe.matmul(o[:, ROWS * d:ROWS * d + ROWS],
                                     cst[:, C_ID + end:C_ID + end + 1].to_broadcast([P, P]),
                                     exin[:, 0, d, :, :].rearrange("p t h -> p (t h)"), start=True, stop=True)
                last.then_inc(slot_full, 1)
                items = ssd_items(L)

                def within(n):
                    d, c, want, has, gives = items[n]
                    tk = slice(c * P, (c + 1) * P)
                    if gives:
                        pe.wait_ge(*when("xr", (L, d, c)))
                        o = take((L, "state", d, c))
                        for g in range(2):
                            last = pe.matmul(o[:, g * 256:(g + 1) * 256], b_tok[:, c, g * P:(g + 1) * P],
                                             xr[:, g * 256:(g + 1) * 256], start=True, stop=True)
                        last.then_inc(slot_full, 1)
                    if want:
                        o = take((L, "cb", d, c))
                        pe.wait_ge(*when("conv_silu", (L, 7)))
                        for g in range(2):
                            last = pe.matmul(o[:, g * P:(g + 1) * P], bc[:, g, tk], bc[:, 2 + g, tk],
                                             start=True, stop=True)
                        last.then_inc(slot_full, 1)
                        o = take((L, "seg", d, c))
                        rows = slice(64 * d, 64 * d + ROWS)
                        for h in range(8):
                            r = C_ID + 64 * d + 8 * c + h
                            last = pe.matmul(o[:, h * P:(h + 1) * P], cst[rows, r:r + 1].to_broadcast([ROWS, P]),
                                             cumR[rows, :], start=True, stop=True)
                        last.then_inc(slot_full, 1)

                def outputs(n):
                    d, c, want, has, gives = items[n]
                    if not want:
                        return
                    tk = slice(c * P, (c + 1) * P)
                    o = take((L, "y", d, c))
                    if has:
                        pe.wait_ge(*read((L, "state") + items[n - 1][0:2]))
                        for g in range(2):
                            pe.matmul(o[:, HALF + g * 256:HALF + (g + 1) * 256], bc[:, 2 + g, tk],
                                      st[:, (n - 1) % 2, g * 256:(g + 1) * 256], start=True, stop=True)
                    pe.wait_ge(*when("seg_masked", (L, d, c)))
                    pe.wait_ge(*when("xd", (L, d, c)))
                    for h in range(8):
                        last = pe.matmul(o[:, h * 64:(h + 1) * 64], seg[:, h, :], xd[:, n % 2, h * 64:(h + 1) * 64],
                                         start=True, stop=True)
                    last.then_inc(slot_full, 1)

                pe.wait_ge(*read((L, "xT", 5)))
                within(0)
                for n in range(len(items)):
                    if n + 1 < len(items):
                        within(n + 1)
                    outputs(n)
                for f in range(KB):
                    product((L, "z", f), (L, "z", f), KD, 0, h_hi, h_lo, spans(L))
                pe.wait_ge(*read((L, "y") + items[-1][0:2]))
                for c in range(first(L) // P, NT):
                    turn((L, "yT", c), [y_tok[:, c, f * P:(f + 1) * P] for f in range(KB)])
                for g in range(2):
                    mean_square((L, "yms", g), y_sq, 2 * g, 2 * g + 2, 3, spans(L), "y_squared", L)

            pe.wait_ge(*when("loaded", "params"))
            turn("params", [parr[:, i, :] for i in range(DEPTH + 1)])
            for t in range(NT):
                pe.wait_ge(*when(f"x_in{t % 2}", t))
                turn(("x", t), [xin[:, t % 2, k * P:(k + 1) * P] for k in range(KD)])
            for L in range(DEPTH):
                mean_square((L, "ms", 1), sqx, 0, KD, 1, ALL, "x_squared", (L, 1))
                if L == 0:
                    ada_first()
                latent(L)
                attention(L)
                merge(L, 0)
                short_conv(L)
                merge(L, 1)
                fourier(L)
                merge(L, 2)
                ssd(L)
                merge(L, 3)
                for f in range(KD):
                    product((L, "out", f), (L, "out", f), KD, 0, h_hi, h_lo, spans(L),
                            (lambda k: pe.wait_ge(*when("merged_lo", (L, k)))) if f == 0 else None)
                mean_square((L, "ms", 2), sqx, 0, KD, 1, spans(L), "x_squared", (L, 2))
                for c in range(4):
                    for f in range(KD):
                        product((L, "w1", c, f), (L, "w1", c, f), KD, 0, h_hi, h_lo, spans(L),
                                (lambda k: pe.wait_ge(*when("h_lo", (L, 2, k)))) if c == f == 0 else None)
                        ada_sum((L, "w1", c, f))
                    for f in range(KD):
                        product((L, "w2", c, f), (L, "w2", c, f), KD, 0, f_hi, f_lo, spans(L),
                                (lambda k: pe.wait_ge(*when("f_lo", (L, c, k)))) if f == 0 else None)
                        ada_sum((L, "w2", c, f))
            mean_square((DEPTH, "ms", 1), sqx, 0, KD, 1, LATS, "x_squared", (DEPTH, 1))
            pe.wait_ge(*when("x_scaled", KD - 1))
            for t in range(CTX // P, NT):
                turn(("y", t), [xf[:, k, t * P:(t + 1) * P] for k in range(KD)])

        @block.sync
        def _(sp_):
            for s, (src, kt, ncol, pitch) in enumerate(tiles):
                if s >= NRAW:
                    if s - NRAW in split:
                        sp_.wait_ge(*when("w_lo", s - NRAW))
                    elif s - NRAW < 2 * KD:
                        sp_.wait_ge(slot_full, last_use[s - NRAW] + 1)
                    else:
                        sp_.wait_ge(*when("ada_used", s - NRAW))
                dst = raw[:, s % NRAW, 0:kt * pitch].rearrange("p (k c) -> p k c", k=kt)[:, :, 0:ncol]
                sp_.dma_start(dst, src).then_inc(counts.sem(f"raw{s % NRAW}_loaded"), 16)

        @block.gpsimd
        def _(pool):
            def by_head(ap):
                return ap.rearrange("p (h c) -> p h c", c=64)

            def scaled(o, a, per_head):
                return pool.tensor_tensor(by_head(o), by_head(a), per_head.unsqueeze(2).to_broadcast([P, 8, 64]),
                                          ALU.mult)

            def ssd(L):
                for f in range(4):
                    pool.wait_ge(*read((L, "xT", f)))
                pool.wait_ge(*when("dterm", L))
                items = ssd_items(L)
                states, outs = [], []
                for n, (d, c, want, has, gives) in enumerate(items):
                    if gives:
                        if states:
                            pool.wait_ge(*full(states[-1]))
                        scaled(xr[:, :], xs_tok[:, c, :], dterm[:, d, c, :]).then_inc(*does("xr", (L, d, c)))
                        states.append((L, "state", d, c))
                    if want:
                        if [m for m in outs if m <= n - 2]:
                            m = [m for m in outs if m <= n - 2][-1]
                            pool.wait_ge(*full((L, "y") + items[m][0:2]))
                        scaled(xd[:, n % 2, :], xs_tok[:, c, :], dts[:, 0, d, c, :]).then_inc(*does("xd", (L, d, c)))
                        outs.append(n)
                        if d == 0:
                            scaled(y_tok[:, c, :], xs_tok[:, c, :], heads_bc[:, L, 32:40]).then_inc(
                                *does("skip", (L, c)))
                    if gives and has:
                        pool.wait_ge(*read((L, "state") + items[n - 1][0:2]))
                        scaled(decayed[:, :], st[:, (n - 1) % 2, :], ex[:, 2, d, c, :]).then_inc(
                            *does("decayed", (L, d, c)))

            for s in split:
                for L in range(DEPTH):
                    if s == tile_of[L, "z", 2]:
                        ssd(L)
                pool.wait_ge(*when("w_hi", s))
                pool.tensor_tensor(w_lo[:, place[s] % 2, :], raw[:, s % NRAW, :],
                                   w_hi[:, place[s] % 2, :].bitcast(F32), ALU.subtract).then_inc(*does("w_lo", s))

        @block.scalar
        def _(act):
            A_ = nc.scalar.activation
            fed = [0]

            def round_weights(limit):
                while fed[0] < len(split):
                    s = split[fed[0]]
                    needs = [last_use[split[fed[0] - 2]]] if fed[0] >= 2 else []
                    needs += [last_use.get(t, len(order)) for t in range(max(0, s - 2 * NRAW), s - NRAW + 1)
                              if t in whole]
                    if needs and max(needs) > limit:
                        break
                    act.wait_ge(counts.sem(f"raw{s % NRAW}_loaded"), 16 * (s // NRAW + 1))
                    if fed[0] >= 2:
                        act.wait_ge(slot_full, last_use[split[fed[0] - 2]] + 1)
                    A_(w_hi[:, fed[0] % 2, :], raw[:, s % NRAW, :], ACT.Copy).then_inc(*does("w_hi", s))
                    fed[0] += 1

            act.dma_start(cst[:, :], A["tables"]).then_inc(*does("loaded", "tables", 16))
            act.wait_ge(*when("cleared", 0))
            for L in range(DEPTH):
                vec = "(t c) -> t c"
                for r0, src, n in ((R_CW, A["ssm_conv_w"][L].rearrange("k (t c) -> (k t) c", c=P), 40),
                                   (R_CB, A["ssm_conv_b"][L].rearrange(vec, c=P), 8),
                                   (R_N1, A["norm1_g"][L].rearrange(vec, c=P), 8),
                                   (R_N2, A["norm2_g"][L].rearrange(vec, c=P), 8),
                                   (R_SN, A["ssm_norm_g"][L].rearrange(vec, c=P), 4),
                                   (R_SW, A["sc_conv_w"][L].rearrange("k (t c) -> (k t) c", c=P), 12),
                                   (R_QG, A["mla_qa_g"][L].rearrange(vec, c=P), 3),
                                   (R_KG, A["mla_kva_g"][L].rearrange(vec, c=P), 2),
                                   (R_FG, A["final_norm_g"].rearrange(vec, c=P), 8),
                                   (R_C, A["c"][0].rearrange(vec, c=P), 8),
                                   (R_CC, A["c_ctx"].rearrange(vec, c=P), 8)):
                    act.dma_start(parr[r0:r0 + n, L, :], src).then_inc(*does("loaded", (L, r0), 16))
                act.dma_start(parr[48 * L:48 * L + 48, DEPTH, :], A["ada_b"][L].rearrange(vec, c=P)).then_inc(*does("loaded", (L, "ada"), 16))
                for o, src, n in ((0, A["ssm_a_log"][L].rearrange("a b -> (a b)"), 16),
                                  (16, A["ssm_dt_bias"][L].rearrange("a b -> (a b)"), 16), (32, A["ssm_d"][L], 8)):
                    act.dma_start(heads_bc[:, L, o:o + n], src.partition_broadcast(P)).then_inc(*does("loaded", (L, "h", o), 16))
            counts.table["loaded", "params"] = counts.now["loaded"]
            for t in range(NT):
                if t >= 2:
                    act.wait_ge(*full(("x", t - 2)))
                act.dma_start(xin[:, t % 2, :], A["ctx"][0, t * P:(t + 1) * P, :] if t < 2 else A["x"][0, (t - 2) * P:(t - 1) * P, :]).then_inc(*does(f"x_in{t % 2}", t, 16))
            act.wait_ge(*read("params"))
            A_(silc[:, :, 0], par[:, 0, R_C:R_C + 8], ACT.Silu)
            A_(silc[:, :, 1], par[:, 0, R_CC:R_CC + 8], ACT.Silu).then_inc(*does("silu_c", 0))
            round_weights(-1)

            def norm(L, which, a):
                for k in range(KD):
                    if which == 2:
                        round_weights(order[(L, "out", k)] - 1)
                        act.wait_ge(*read((L, "out", k)))
                    elif L:
                        if k == 0:
                            round_weights(order[L - 1, "w2", 3, KD - 1] - 1)
                            act.wait_ge(*full((L - 1, "w2", 3, KD - 1)))
                        round_weights(order[(L - 1, "w2", 3, k)] - 1)
                        act.wait_ge(*read((L - 1, "w2", 3, k)))
                    elif k == 0:
                        for t in range(NT):
                            round_weights(order[("x", t)] - 1)
                            act.wait_ge(*read(("x", t)))
                    A_(sqx[:, k, a:TOK], x[:, k, a:TOK], ACT.Square).then_inc(*does("x_squared", ((L, which), k)))
                key = (L, "ms", which)
                round_weights(order[key] - 1)
                act.wait_ge(*full(key))
                A_(sdev[:, a:TOK], cols(key, a), ACT.Sqrt, bias=epsc[:, :]).then_inc(*frees(key))
                if L < DEPTH:
                    for k in range(KD):
                        act.wait_ge(*when("h", (L, which, k)))
                        A_(h_hi[:, k, a:TOK], sqx[:, k, a:TOK], ACT.Copy).then_inc(*does("h_hi", (L, which, k)))

            def latent(L):
                a = first(L)
                act.wait_ge(*when("x_stored", L))
                for f in range(2):
                    key = (L, "kva", f)
                    round_weights(order[key] - 1)
                    act.wait_ge(*full(key))
                    A_(sql[:, f, :], cols(key, 0), ACT.Square).then_inc(*does("kv_squared", (L, f)))
                    A_(lraw[:, f, :], cols(key, 0), ACT.Copy).then_inc(*frees(key))
                key = (L, "kr")
                round_weights(order[key] - 1)
                act.wait_ge(*full(key))
                A_(kT[NOPE:QH, 0, :], cols(key, 0, NOPE, QH), ACT.Copy).then_inc(*does("kr_copied", L))
                A_(kT[NOPE:QH, 1, :], cols(key, 0, NOPE, QH), ACT.Copy).then_inc(*frees(key))
                key = (L, "kvms")
                round_weights(order[key] - 1)
                act.wait_ge(*full(key))
                A_(sdev[:, :], cols(key, 0), ACT.Sqrt, bias=epsc[:, :]).then_inc(*frees(key))
                for f in range(3):
                    key = (L, "qa", f)
                    round_weights(order[key] - 1)
                    act.wait_ge(*full(key))
                    A_(lraw[:, 2 + f, a:TOK], cols(key, a), ACT.Copy).then_inc(*frees(key))
                    if f < 2:
                        act.wait_ge(*when("kvn", (L, f)))
                        A_(ln_hi[:, f, :], lraw[:, f, :], ACT.Copy).then_inc(*does("kvn_hi", (L, f)))
                act.wait_ge(*read((L, "qa", 2)))
                for f in range(3):
                    A_(sql[:, f, a:TOK], lraw[:, 2 + f, a:TOK], ACT.Square).then_inc(*does("q_squared", (L, f)))
                for h in range(HEADS):
                    key = (L, "k", h)
                    round_weights(order[key] - 1)
                    act.wait_ge(*full(key))
                    A_(kT[0:NOPE, h, :], cols(key, 0, 0, NOPE), ACT.Copy).then_inc(*frees(key))
                    if h == 3:
                        key = (L, "qms")
                        round_weights(order[key] - 1)
                        act.wait_ge(*full(key))
                        A_(sdev[:, a:TOK], cols(key, a), ACT.Sqrt, bias=epsc[:, :]).then_inc(*frees(key))
                key = (L, "v", 1, NT // 2 - 1)
                round_weights(order[key] - 1)
                act.wait_ge(*full(key))
                for f in range(3):
                    act.wait_ge(*when("qn", (L, f)))
                    A_(ln_hi[:, f, a:TOK], lraw[:, 2 + f, a:TOK], ACT.Copy).then_inc(*does("qn_hi", (L, f)))
                for h in range(HEADS):
                    key = (L, "q", h)
                    round_weights(order[key] - 1)
                    act.wait_ge(*full(key))
                    A_(qT[0:QH, h, a:TOK], cols(key, a, 0, QH), ACT.Copy, scale=SCALE).then_inc(*does("q_copied", (L, h)))

            def attention(L):
                items = att_items(L)
                for n in range(len(items) + 3):
                    if n < len(items):
                        h, qt = items[n]
                        key = (L, "s", h, qt)
                        end = CTX if qt < 2 else TOK
                        act.wait_ge(*when("row_max", (L, h, qt)))
                        if n >= 2:
                            act.wait_ge(*full((L, "pT") + items[n - 2]))
                        A_(probs[n % 2][:, 0:end], slot(key)[:, T0:T0 + end], ACT.Exp, bias=rmax[:, n % 2:n % 2 + 1],
                           accum_out=rsum[:, n % 2:n % 2 + 1]).then_inc(*frees(key))
                    if n >= 3 and items[n - 3][1] == NT - 1:
                        h = items[n - 3][0]
                        lo = (h % 2) * VD
                        round_weights(order[L, "o", h] - 1)
                        act.wait_ge(*full((L, "o", h)))
                        A_(br_hi[lo:lo + VD, h // 2, first(L):TOK], cols((L, "o", h), first(L), lo, lo + VD),
                           ACT.Copy).then_inc(*does("values_hi", (L, h)))
                    if 2 <= n < len(items) + 2:
                        h, qt = items[n - 2]
                        key = (L, "pT", h, qt)
                        act.wait_ge(*full(key))
                        nk = 2 if qt < 2 else NT
                        A_(pT[:, 0:nk, qt * P:(qt + 1) * P],
                           slot(key)[:, 0:nk * P].rearrange("p (k q) -> p k q", k=nk), ACT.Copy).then_inc(*frees(key))

            def branch_hi(L, k, f, src):
                A_(br_hi[:, f, first(L):TOK], src[:, first(L):TOK], ACT.Copy).then_inc(*does("branch_hi", (L, k, f)))

            def merge(L, k):
                a = first(L)
                for f in range(KD):
                    key = (L, "gate", k, f)
                    round_weights(order[key] - 1)
                    act.wait_ge(*full(key))
                    if f >= 2:
                        round_weights(order[(L, "proj", k, f - 2)] - 1)
                        act.wait_ge(*read((L, "proj", k, f - 2)))
                    elif k:
                        round_weights(order[(L, "proj", k - 1, f + 6)] - 1)
                        act.wait_ge(*read((L, "proj", k - 1, f + 6)))
                    A_(sigm[:, f % 2, a:TOK], cols(key, a), ACT.Sigmoid).then_inc(*frees(key))

            def short_conv(L):
                a = first(L)
                for f in range(KB + 1):
                    if f < KB:
                        key = (L, "cg", f)
                        round_weights(order[key] - 1)
                        act.wait_ge(*full(key))
                        if f >= 2:
                            round_weights(order[(L, "xin", f - 2)] - 1)
                            act.wait_ge(*read((L, "xin", f - 2)))
                        A_(cgs[:, f % 2, a:TOK], cols(key, a), ACT.Copy).then_inc(*frees(key))
                    if f >= 1:
                        round_weights(order[(L, "bg", f - 1)] - 1)
                        act.wait_ge(*read((L, "bg", f - 1)))
                        branch_hi(L, 1, f - 1, cvo[:, (f - 1) % 2, :])

            def ada_place_free(L, k):
                if L == 0:
                    act.wait_ge(*when("ada_ksum", ada_after[0, "gate", k, KD - 1] + 1))

            def fourier(L):
                a = first(L)
                round_weights(order[L, "proj", 1, KD - 1])
                act.wait_ge(*full((L, "proj", 1, KD - 1)))
                ada_place_free(L, 1)
                act.dma_start(dft.rearrange("p a j t -> p a (j t)"), A["dft"].rearrange("a (j p) t -> p a j t", p=P).rearrange("p a j t -> p a j t")).then_inc(*does("dft_loaded", L, 16))
                A_(ch_hi[:, :], cst[:, C_CHAN:C_CHAN + 256], ACT.Copy).then_inc(*does("channel_hi", L))

                def out_hi(g):
                    key = (L, "fo", g)
                    round_weights(order[key] - 1)
                    act.wait_ge(*full(key))
                    for _, _, t0, nt, _, scale in fourier_parts(L):
                        ins = A_(br_hi[:, g, t0:t0 + nt], slot(key)[:, T0 + t0:T0 + t0 + nt], ACT.Copy, scale=scale)
                    ins.then_inc(*does("fourier_hi", (L, g)))

                for g in range(4):
                    if g == 0:
                        round_weights(order[L, "fn", 0] - 1)
                        act.wait_ge(*full((L, "fn", 0)))
                    A_(fn_hi[:, a:TOK], cols((L, "fn", g), a), ACT.Copy).then_inc(*does("fn_hi", (L, g)))
                    if g >= 1:
                        out_hi(g - 1)
                    for tp in range(a // CTX, NT // 2):
                        key = (L, "fy", g, tp)
                        round_weights(order[key] - 1)
                        act.wait_ge(*full(key))
                        A_(fy[:, 2 * tp:2 * tp + 2, :],
                                slot(key).rearrange("p (a b) -> p a b", b=HALF)[:, :, 0:256], ACT.Copy).then_inc(*frees(key))
                    if g < 3:
                        round_weights(order[L, "fn", g + 1] - 1)
                        act.wait_ge(*full((L, "fn", g + 1)))
                out_hi(3)

            def ssd(L):
                a = first(L)
                key = (L, "dt")
                round_weights(order[key] - 1)
                ada_place_free(L, 2)
                act.wait_ge(*full(key))
                A_(dtT, cols(key, 0, 0, 32), ACT.Copy).then_inc(*frees(key))
                for f in range(KD):
                    if 1 <= f <= 4:
                        round_weights(order[L, "xT", f - 1] - 1)
                        act.wait_ge(*full((L, "xT", f - 1)))
                    round_weights(order[(L, "xbc", f)] - 1)
                    act.wait_ge(*read((L, "xbc", f)))
                    A_(conv if f < 4 else bc[:, f - 4, :], cacc[f % 2][:, :], ACT.Silu).then_inc(*does("conv_silu", (L, f)))
                    if f == 1:
                        act.wait_ge(*when("dt_abs", L))
                        A_(dts[:, 1, :, :, :], dts[:, 1, :, :, :], ACT.Exp, scale=-1.0).then_inc(*does("dt_exp", L))
                        A_(heads_bc[:, L, 0:16], heads_bc[:, L, 0:16], ACT.Exp).then_inc(*does("rates", L))
                    if f == 2:
                        act.wait_ge(*when("dt_one", L))
                        A_(dts[:, 4, :, :, :], dts[:, 2, :, :, :], ACT.Ln).then_inc(*does("dt_ln", L))
                round_weights(order[(L, "tot")] - 1)
                act.wait_ge(*read((L, "tot")))
                A_(ex[:, :, :, :, :].rearrange("p a d t h -> p (a d t h)"),
                        exin[:, :, :, :, :].rearrange("p a d t h -> p (a d t h)"), ACT.Exp).then_inc(*does("decays", L))
                prev = None
                for d, c, want, has, gives in ssd_items(L):
                    if want:
                        round_weights(order[L, "seg", d, c] - 1)
                        act.wait_ge(*read((L, "seg", d, c)))
                        A_(diff.rearrange("p h i -> p (h i)"), diff.rearrange("p h i -> p (h i)"), ACT.Relu,
                           scale=-1.0).then_inc(*does("diff_cut", (L, d, c)))
                        act.wait_ge(*when("diff_cut", (L, d, c)))
                        if prev:
                            act.wait_ge(*full((L, "y") + prev))
                        A_(seg.rearrange("p h i -> p (h i)"), diff.rearrange("p h i -> p (h i)"), ACT.Exp, scale=-1.0).then_inc(*does("seg_exp", (L, d, c)))
                        prev = (d, c)
                for f in range(KB):
                    key = (L, "z", f)
                    round_weights(order[key] - 1)
                    act.wait_ge(*full(key))
                    A_(zs[:, f, a:TOK], cols(key, a), ACT.Silu).then_inc(*frees(key))
                round_weights(order[(L, "yT", NT - 1)] - 1)
                act.wait_ge(*read((L, "yT", NT - 1)))
                for f in range(KB):
                    A_(y_sq[:, f, a:TOK], zs[:, f, a:TOK], ACT.Square).then_inc(*does("y_squared", (L, f)))
                for g in range(2):
                    key = (L, "yms", g)
                    round_weights(order[key] - 1)
                    act.wait_ge(*full(key))
                    A_(sdev[:, a:TOK], cols(key, a), ACT.Sqrt, bias=epsc[:, :]).then_inc(*frees(key))
                    for f in range(2 * g, 2 * g + 2):
                        act.wait_ge(*when("branch", (L, 3, f)))
                        branch_hi(L, 3, f, zs[:, f, :])

            for L in range(DEPTH):
                a = first(L)
                norm(L, 1, 0)
                act.dma_start(x_spill, x.rearrange("p k t -> p (k t)")).then_inc(*does("x_stored", L, 16))
                latent(L)
                attention(L)
                merge(L, 0)
                short_conv(L)
                merge(L, 1)
                fourier(L)
                merge(L, 2)
                ssd(L)
                merge(L, 3)
                round_weights(order[L, "proj", 3, KD - 1] - 1)
                act.wait_ge(*full((L, "proj", 3, KD - 1)))
                act.dma_start(x.rearrange("p k t -> p (k t)"), x_spill).then_inc(*does("x_back", L, 16))
                for k in range(KD):
                    act.wait_ge(*when("merged", (L, 3, k)))
                    A_(h_hi[:, k, a:TOK], merged[:, k, a:TOK], ACT.Copy).then_inc(*does("merged_hi", (L, k)))
                norm(L, 2, a)
                for n in range(4 * KD):
                    c, f = divmod(n, KD)
                    key = (L, "w1", c, f)
                    round_weights(order[key] - 1)
                    act.wait_ge(*full(key))
                    if n >= 2:
                        act.wait_ge(*read((L, "w1") + divmod(n - 2, KD)))
                    A_(act_r[:, n % 2, a:TOK], cols(key, a), ACT.Relu).then_inc(*does("relu", (L, n)))
                    for m in [n - 1] * (f > 0) + [n] * (f == KD - 1):
                        round_weights(order[(L, "w1") + divmod(m, KD)] - 1)
                        act.wait_ge(*read((L, "w1") + divmod(m, KD)))
                        A_(f_hi[:, m % KD, a:TOK], act_f[m % 2][:, a:TOK], ACT.Copy).then_inc(*does("f_hi", (L, m)))
            norm(DEPTH, 1, CTX)
            for t in range(CTX // P, NT):
                key = ("y", t)
                round_weights(order[key] - 1)
                act.wait_ge(*full(key))
                if t >= 4:
                    act.wait_ge(*when(f"y_out{t % 2}", t - 2))
                A_(yout[:, t % 2, :], slot(key), ACT.Copy).then_inc(*frees(key))
                act.wait_ge(*read(key))
                act.dma_start(out[0, t * P - CTX:(t + 1) * P - CTX, :], yout[:, t % 2, :]).then_inc(*does(f"y_out{t % 2}", t, 16))
            for t in (NT - 2, NT - 1):
                act.wait_ge(*when(f"y_out{t % 2}", t))

        @block.vector
        def _(dve):
            def mul(o, a, b):
                return dve.tensor_tensor(o, a, b, ALU.mult)

            def lo(o, whole, hi):
                return dve.tensor_tensor(o, whole, hi.bitcast(F32), ALU.subtract)

            def fma(o, a, s, b, op0=ALU.mult, op1=ALU.add):
                return dve.scalar_tensor_tensor(o, a, s, b, op0, op1)

            dve.memset(parr[:, :, :], 0.0)
            dve.memset(epsc[:, :], EPS).then_inc(*does("cleared", 0))
            for i, v in enumerate((1.0, 1.0 / D, 1.0 / QR, 1.0 / KVR)):
                dve.memset(ones[:, i, :], v).then_inc(*does("dve_step"))
                dve.wait_ge(*last_())
            dve.wait_ge(*full("params"))
            dve.tensor_copy(adab.rearrange("p l f -> p (l f)"), slot("params")[:, DEPTH * P:DEPTH * P + 96]).then_inc(*does("dve_step"))
            dve.wait_ge(*last_())
            dve.tensor_copy(par.rearrange("p l f -> p (l f)"), slot("params")[:, 0:DEPTH * P]).then_inc(*frees("params"))
            for t in range(NT):
                key = ("x", t)
                dve.wait_ge(*full(key))
                dve.tensor_copy(x[:, :, t * P:(t + 1) * P], slot(key).rearrange("p (k t) -> p k t", k=KD)).then_inc(*frees(key))
            def ada_first(f):
                dve.wait_ge(*full((0, "ada", f)))
                dve.tensor_tensor(mods[:, 0, f:f + 2, :],
                                  slot((0, "ada", f))[:, 0:4].rearrange("p (f v) -> p f v", v=2),
                                  adab[:, 0, f:f + 2].unsqueeze(2).to_broadcast([P, 2, 2]),
                                  ALU.add).then_inc(*frees((0, "ada", f)))

            def ada_ksum(n):
                if n == len(ADA_LATER):
                    return
                L, f = ADA_LATER[n]
                s = tile_of[L, "ada", f]
                w = raw[:, s % NRAW, :].rearrange("p (k c) -> p k c", k=KD)
                dve.wait_ge(counts.sem(f"raw{s % NRAW}_loaded"), 16 * (s // NRAW + 1))
                if n >= 2:
                    dve.wait_ge(*full(("ada", n - 2)))
                for v in range(2):
                    mul(prod[:, :, :], w, silc[:, :, v:v + 1].to_broadcast([P, KD, P])).then_inc(
                        *does(*(("dve_step",) if v == 0 else ("ada_used", s))))
                    dve.wait_ge(*last_())
                    dve.reduce_sum(ksum[:, n % 2, v, :], prod.rearrange("p k c -> p c k"), AX.X).then_inc(
                        *does(*(("dve_step",) if v == 0 else ("ada_ksum", n))))
                    dve.wait_ge(*last_())

            def ada(after):
                if after in ada_after:
                    n = ada_after[after]
                    L, f = ADA_LATER[n]
                    dve.wait_ge(*full(("ada", n)))
                    dve.tensor_scalar(mods[:, L, f, :], slot(("ada", n))[:, 0:2], adab[:, L, f:f + 1], None,
                                      ALU.add).then_inc(*frees(("ada", n)))
                    ada_ksum(n + 1)

            def norm(L, which, a):
                key = (L, "ms", which)
                dve.wait_ge(*last_())
                dve.wait_ge(*read(key))
                dve.reciprocal(rstd[:, a:TOK], sdev[:, a:TOK]).then_inc(*does("dve_step"))
                dve.wait_ge(*last_())
                if L == DEPTH:
                    for k in range(KD):
                        fma(xf[:, k, a:TOK], x[:, k, a:TOK], par[:, 0, R_FG + k:R_FG + k + 1], rstd[:, a:TOK],
                            ALU.mult, ALU.mult).then_inc(*does("x_scaled", k))
                    return
                start = (L, which) == (0, 1)
                if start:
                    for k in range(KD):
                        mul(sqx[:, k, :], x[:, k, :], rstd[:, :]).then_inc(*does("dve_step"))
                        ada_first(2 * k)
                    dve.wait_ge(*last_())
                sh0, sc0, g0 = ((0, 8, R_N1), (24, 32, R_N2))[which - 1]
                fma(gsc[:, :, :], mods[:, L, sc0:sc0 + 8, :], 1.0,
                    par[:, L, g0:g0 + 8].unsqueeze(2).to_broadcast([P, 8, 2]), ALU.add,
                    ALU.mult).then_inc(*does("dve_step"))
                for k in range(KD + 1):
                    dve.wait_ge(*last_())
                    if k < KD:
                        if not start:
                            mul(sqx[:, k, a:TOK], x[:, k, a:TOK], rstd[:, a:TOK]).then_inc(*does("dve_step"))
                            dve.wait_ge(*last_())
                        for b, e, v in kinds(a):
                            ins = dve.tensor_scalar(sqx[:, k, b:e], sqx[:, k, b:e], gsc[:, k, v:v + 1],
                                                    mods[:, L, sh0 + k, v:v + 1], ALU.mult, ALU.add)
                            if e == TOK:
                                ins.then_inc(*does("h", (L, which, k)))
                            else:
                                ins.then_inc(*does("dve_step"))
                                dve.wait_ge(*last_())
                    if k:
                        dve.wait_ge(*when("h_hi", (L, which, k - 1)))
                        lo(h_lo[:, k - 1, a:TOK], sqx[:, k - 1, a:TOK],
                           h_hi[:, k - 1, a:TOK]).then_inc(*does("h_lo", (L, which, k - 1)))

            def latent_norm(L, key, tiles_, g0, a, name):
                dve.wait_ge(*last_())
                dve.wait_ge(*read(key))
                dve.reciprocal(rstd[:, a:TOK], sdev[:, a:TOK]).then_inc(*does("dve_step"))
                dve.wait_ge(*last_())
                for f, src in enumerate(tiles_):
                    fma(lraw[:, src, a:TOK], lraw[:, src, a:TOK], par[:, L, g0 + f:g0 + f + 1], rstd[:, a:TOK],
                        ALU.mult, ALU.mult).then_inc(*does(name + "n", (L, f)))

            def latent_lo(L, tiles_, a, name):
                for f, src in enumerate(tiles_):
                    dve.wait_ge(*when(name + "n_hi", (L, f)))
                    lo(ln_lo[:, f, a:TOK], lraw[:, src, a:TOK],
                       ln_hi[:, f, a:TOK]).then_inc(*does(name + "n_lo", (L, f)))

            def latent(L):
                a = first(L)
                cos, sin = cst[NOPE:QH, C_COS:C_COS + TOK], cst[NOPE:QH, C_SIN:C_SIN + TOK]
                latent_norm(L, (L, "kvms"), (0, 1), R_KG, 0, "kv")
                latent_lo(L, (0, 1), 0, "kv")
                key = (L, "krot")
                dve.wait_ge(*full(key))
                dve.wait_ge(*read((L, "kr")))
                mul(kT[NOPE:QH, 2, :], cols(key, 0, NOPE, QH), sin).then_inc(*frees(key))
                mul(kT[NOPE:QH, 1, :], kT[NOPE:QH, 1, :], cos).then_inc(*does("dve_step"))
                dve.wait_ge(*last_())
                dve.tensor_tensor(kT[NOPE:QH, 3, :], kT[NOPE:QH, 1, :], kT[NOPE:QH, 2, :], ALU.add).then_inc(*does("dve_step"))
                dve.wait_ge(*last_())
                for h0, h1 in ((0, 3), (4, HEADS)):
                    ins = dve.tensor_copy(kT[NOPE:QH, h0:h1, :],
                                          kT[NOPE:QH, 3:4, :].to_broadcast([ROPE, h1 - h0, TOK]))
                    ins.then_inc(*does("k_rotated", L))
                for i in range(2):
                    if i == 1:
                        latent_norm(L, (L, "qms"), (2, 3, 4), R_QG, a, "q")
                    for tp in range(NT // 2):
                        key = (L, "v", i, tp)
                        dve.wait_ge(*full(key))
                        dve.tensor_copy(vt[:, 2 * tp:2 * tp + 2, 256 * i:256 * i + 256],
                                             slot(key).rearrange("p (a b) -> p a b", b=HALF)[:, :, 0:256]).then_inc(*frees(key))
                latent_lo(L, (2, 3, 4), a, "q")
                for h in range(HEADS):
                    dve.wait_ge(*last_())
                    dve.wait_ge(*when("q_copied", (L, h)))
                    ins = dve.tensor_copy(rrec[0:1, 0:1], slot((L, "q", h))[0:1, 0:1])
                    ins.then_inc(*frees((L, "q", h)))
                    key = (L, "qrot", h)
                    dve.wait_ge(*full(key))
                    mul(lraw[NOPE:QH, 0, a:TOK], cols(key, a, NOPE, QH), sin[:, a:TOK]).then_inc(*frees(key))
                    mul(qT[NOPE:QH, h, a:TOK], qT[NOPE:QH, h, a:TOK], cos[:, a:TOK]).then_inc(*does("dve_step"))
                    dve.wait_ge(*last_())
                    dve.tensor_tensor(qT[NOPE:QH, h, a:TOK], qT[NOPE:QH, h, a:TOK], lraw[NOPE:QH, 0, a:TOK],
                                           ALU.add).then_inc(*does("q_rotated", (L, h)))

            def attention(L):
                items = att_items(L)
                for n in range(len(items) + 3):
                    dve.wait_ge(*last_())
                    if n < len(items):
                        h, qt = items[n]
                        key = (L, "s", h, qt)
                        end = CTX if qt < 2 else TOK
                        dve.wait_ge(*full(key))
                        if n >= 2:
                            dve.wait_ge(*read((L, "s") + items[n - 2]))
                        dve.reduce_max(rmax[:, n % 2:n % 2 + 1], slot(key)[:, T0:T0 + end], AX.X, negate=True).then_inc(*does("row_max", (L, h, qt)))
                    if 1 <= n <= len(items):
                        h, qt = items[n - 1]
                        i = (n - 1) % 2
                        end = CTX if qt < 2 else TOK
                        dve.wait_ge(*read((L, "s", h, qt)))
                        dve.reciprocal(rrec[:, i:i + 1], rsum[:, i:i + 1]).then_inc(*does("dve_step"))
                        dve.wait_ge(*last_())
                        dve.tensor_scalar(probs[i][:, 0:end], probs[i][:, 0:end], rrec[:, i:i + 1], None, ALU.mult).then_inc(*does("probs", (L, h, qt)))
                    if n >= 3 and items[n - 3][1] == NT - 1:
                        h = items[n - 3][0]
                        p = (h % 2) * VD
                        dve.wait_ge(*when("values_hi", (L, h)))
                        lo(br_lo[p:p + VD, h // 2, first(L):TOK], cols((L, "o", h), first(L), p, p + VD),
                                br_hi[p:p + VD, h // 2, first(L):TOK]).then_inc(*frees((L, "o", h)))

            def branch_lo(L, k, f, src):
                a = first(L)
                dve.wait_ge(*when("branch_hi", (L, k, f)))
                lo(br_lo[:, f, a:TOK], src[:, a:TOK], br_hi[:, f, a:TOK]).then_inc(*does("branch_lo", (L, k, f)))

            def merge(L, k):
                a = first(L)
                if (L, k) == (0, 0):
                    dve.wait_ge(*last_())
                    ada_ksum(0)
                for f in range(KD):
                    if f % 2 == 0:
                        ada((L, "gate", k, f))
                        ada((L, "gate", k, f + 1))
                    key = (L, "proj", k, f)
                    dve.wait_ge(*last_())
                    dve.wait_ge(*full(key))
                    dve.wait_ge(*read((L, "gate", k, f)))
                    if k == 0:
                        mul(merged[:, f, a:TOK], cols(key, a), sigm[:, f % 2, a:TOK]).then_inc(*frees(key))
                    else:
                        mul(gated[:, a:TOK], cols(key, a), sigm[:, f % 2, a:TOK]).then_inc(*frees(key))
                        dve.wait_ge(*read(key))
                        dve.tensor_tensor(merged[:, f, a:TOK], merged[:, f, a:TOK], gated[:, a:TOK], ALU.add).then_inc(*does("merged", (L, k, f)))

            def convolve(o, src, taps, width, bias, a, signal):
                mid = width // 2
                steps = []
                if bias is None:
                    dve.tensor_scalar(o[:, a:TOK], src(a, TOK), taps(mid), None, ALU.mult).then_inc(*does("dve_step"))
                    dve.wait_ge(*last_())
                else:
                    dve.tensor_scalar(o[:, a:TOK], src(a, TOK), taps(mid), bias, ALU.mult, ALU.add).then_inc(*does("dve_step"))
                    dve.wait_ge(*last_())
                for k in [k for k in range(width) if k != mid]:
                    s = k - mid
                    for b, e, _ in kinds(a):
                        steps.append((b + max(0, -s), e - max(0, s), s, k))
                for n, (b, e, s, k) in enumerate(steps):
                    ins = fma(o[:, b:e], src(b + s, e + s), taps(k), o[:, b:e])
                    if n < len(steps) - 1:
                        ins.then_inc(*does("dve_step"))
                        dve.wait_ge(*last_())
                ins.then_inc(*signal())

            def short_conv(L):
                a = first(L)
                for f in range(KB):
                    key = (L, "xin", f)
                    dve.wait_ge(*last_())
                    dve.wait_ge(*full(key))
                    dve.wait_ge(*read((L, "cg", f)))
                    g, o = cgx[:, f % 2, :], cvo[:, f % 2, :]
                    mul(g[:, a:TOK], cols(key, a), cgs[:, f % 2, a:TOK]).then_inc(*frees(key))
                    dve.wait_ge(*read(key))
                    convolve(o, lambda b, e: g[:, b:e], lambda k: par[:, L, R_SW + 4 * k + f:R_SW + 4 * k + f + 1], 3,
                             None, a, lambda: does("dve_step"))
                    dve.wait_ge(*last_())
                    key = (L, "bg", f)
                    dve.wait_ge(*full(key))
                    mul(o[:, a:TOK], cols(key, a), o[:, a:TOK]).then_inc(*frees(key))
                    branch_lo(L, 1, f, o)

            def fourier(L):
                a = first(L)
                dve.wait_ge(*when("channel_hi", L))
                lo(ch_lo[:, :], cst[:, C_CHAN:C_CHAN + 256], ch_hi[:, :]).then_inc(*does("channel_dft", L))
                for g in range(5):
                    dve.wait_ge(*last_())
                    if g < 4:
                        key = (L, "fn", g)
                        dve.wait_ge(*when("fn_hi", (L, g)))
                        lo(fn_lo[:, a:TOK], cols(key, a), fn_hi[:, a:TOK]).then_inc(*frees(key))
                    if g >= 1:
                        key = (L, "fo", g - 1)
                        dve.wait_ge(*when("fourier_hi", (L, g - 1)))
                        parts = fourier_parts(L)
                        for n, (_, _, t0, nt, _, scale) in enumerate(parts):
                            ins = fma(br_lo[:, g - 1, t0:t0 + nt], slot(key)[:, T0 + t0:T0 + t0 + nt], scale,
                                      br_hi[:, g - 1, t0:t0 + nt].bitcast(F32), ALU.mult, ALU.subtract)
                            if n < len(parts) - 1:
                                ins.then_inc(*does("dve_step"))
                                dve.wait_ge(*last_())
                        ins.then_inc(*frees(key))

            def steps(L):
                key = (L, "dtT")
                dve.wait_ge(*last_())
                dve.wait_ge(*full(key))
                raw_ = slot(key)[:, 0:32 * NT].rearrange("p (t c) -> p t c", c=32)
                for d in range(2):
                    bias = heads_bc[:, L, 16 + 8 * d:24 + 8 * d].unsqueeze(1).to_broadcast([P, NT, 8])
                    ins = dve.tensor_tensor(dts[:, 0, d, :, :], raw_[:, :, 8 * d:8 * d + 8], bias, ALU.add)
                    if d == 0:
                        ins.then_inc(*does("dve_step"))
                        dve.wait_ge(*last_())
                ins.then_inc(*frees(key))
                dve.wait_ge(*read(key))
                v = [dts[:, i, :, :, :].rearrange("p d t h -> p (d t h)") for i in range(6)]
                fma(v[1], v[0], -1.0, v[0], ALU.mult, ALU.max).then_inc(*does("dt_abs", L))

            def steps_one(L):
                v = [dts[:, i, :, :, :].rearrange("p d t h -> p (d t h)") for i in range(6)]
                dve.wait_ge(*when("dt_exp", L))
                dve.tensor_scalar(v[2], v[1], 1.0, None, ALU.add).then_inc(*does("dt_one", L))
                dve.wait_ge(*when("dt_one", L))
                dve.tensor_scalar(v[3], v[2], -1.0, None, ALU.add).then_inc(*does("dve_step"))
                dve.wait_ge(*last_())
                dve.tensor_scalar(v[5], v[3], 0.0, None, ALU.is_equal).then_inc(*does("dve_step"))

            def steps_end(L):
                v = [dts[:, i, :, :, :].rearrange("p d t h -> p (d t h)") for i in range(6)]
                dve.wait_ge(*when("dt_ln", L))
                dve.tensor_tensor(v[4], v[4], v[5], ALU.add).then_inc(*does("dve_step"))
                dve.wait_ge(*last_())
                mul(v[4], v[4], v[1]).then_inc(*does("dve_step"))
                dve.wait_ge(*last_())
                dve.tensor_tensor(v[3], v[3], v[5], ALU.add).then_inc(*does("dve_step"))
                dve.wait_ge(*last_())
                dve.reciprocal(v[2], v[3]).then_inc(*does("dve_step"))
                dve.wait_ge(*last_())
                mul(v[4], v[4], v[2]).then_inc(*does("dve_step"))
                dve.wait_ge(*last_())
                fma(v[0], v[0], 0.0, v[4], ALU.max, ALU.add).then_inc(*does("dve_step"))
                dve.wait_ge(*last_())
                for d in range(2):
                    rate = heads_bc[:, L, 8 * d:8 * d + 8].unsqueeze(1).to_broadcast([P, NT, 8])
                    fma(dts[:, 3, d, :, :], dts[:, 0, d, :, :], -1.0, rate, ALU.mult, ALU.mult).then_inc(*does("la", L))

            def running_sums(L):
                key = (L, "laT")
                dve.wait_ge(*full(key))
                for d in range(2):
                    rows = slice(64 * d, 64 * d + ROWS)
                    ins = dve.tensor_copy(laR[rows, :] if d == 0 else laR[rows, ::-1], slot(key)[rows, 0:P])
                    if d == 0:
                        ins.then_inc(*does("dve_step"))
                        dve.wait_ge(*last_())
                ins.then_inc(*frees(key))
                dve.wait_ge(*read(key))
                for d in range(2):
                    rows = slice(64 * d, 64 * d + ROWS)
                    o = diff[rows, 0, :]
                    keep = cst[rows, C_KEEP:C_KEEP + P]
                    dve.tensor_tensor_scan(o, keep, laR[rows, :], 0.0, ALU.mult, ALU.add).then_inc(*does("dve_step"))
                    dve.wait_ge(*last_())
                    ends = diff[rows, 0, SUM_BLOCK - 1:P:SUM_BLOCK]
                    dve.tensor_tensor_scan(blkR[rows, :], ones[rows, 0, 0:P // SUM_BLOCK], ends, 0.0,
                                                ALU.mult, ALU.add).then_inc(*does("dve_step"))
                    dve.wait_ge(*last_())
                    dve.tensor_tensor(diff[rows, 0, SUM_BLOCK:P].rearrange("p (b i) -> p b i", i=SUM_BLOCK),
                                           diff[rows, 0, SUM_BLOCK:P].rearrange("p (b i) -> p b i", i=SUM_BLOCK),
                                           blkR[rows, 0:P // SUM_BLOCK - 1].unsqueeze(2).to_broadcast(
                                               [ROWS, P // SUM_BLOCK - 1, SUM_BLOCK]), ALU.add).then_inc(*does("dve_step"))
                    dve.wait_ge(*last_())
                    dve.tensor_copy(cumR[rows, :], o if d == 0 else diff[rows, 0, ::-1]).then_inc(*does("cum_rows", L))
                dve.wait_ge(*last_())

            def ssd(L):
                a = first(L)
                for f in range(KD + 1):
                    dve.wait_ge(*last_())
                    if f < KD:
                        key = (L, "xbc", f)
                        dve.wait_ge(*full(key))
                        if f >= 2:
                            dve.wait_ge(*when("conv_silu", (L, f - 2)))
                        if f == 1:
                            steps(L)
                        if f == 2:
                            steps_one(L)
                        if f == 4:
                            steps_end(L)
                        if f == 6:
                            running_sums(L)
                        if f == 7:
                            key = (L, "cum")
                            dve.wait_ge(*full(key))
                            dve.tensor_copy(exin[:, 0, :, :, :].rearrange("p d t h -> p d (t h)"),
                                            slot(key).rearrange("p (d c) -> p d c", d=2)[:, :, 0:ROWS]).then_inc(
                                                *frees(key))
                            dve.wait_ge(*last_())
                        key = (L, "xbc", f)
                        convolve(cacc[f % 2], lambda b, e: slot(key)[:, T0 + b:T0 + e],
                                 lambda k: par[:, L, R_CW + 8 * k + f:R_CW + 8 * k + f + 1], 5,
                                 par[:, L, R_CB + f:R_CB + f + 1], 0, lambda: frees(key))
                    if 1 <= f <= 6:
                        key = (L, "xT", f - 1)
                        dve.wait_ge(*full(key))
                        dst = xs_tok[:, :, (f - 1) * P:f * P] if f - 1 < 4 else b_tok[:, :, (f - 5) * P:(f - 4) * P]
                        dve.tensor_copy(dst, slot(key)[:, 0:TOK].rearrange("p (t c) -> p t c", t=NT)).then_inc(*frees(key))
                def by_head(ap, n=64):
                    return ap.rearrange("p (h c) -> p h c", c=n)

                def wide(ap, n=64):
                    return ap.unsqueeze(2).to_broadcast([P, 8, n])

                sums = [exin[:, i, :, :, :].rearrange("p d t h -> p (d t h)") for i in range(3)]
                key = (L, "tot")
                dve.wait_ge(*full(key))
                dve.tensor_copy(sums[2], slot(key)[:, 0:2 * ROWS]).then_inc(*does("dve_step"))
                dve.wait_ge(*last_())
                dve.tensor_tensor(sums[1], slot(key)[:, 0:2 * ROWS], sums[0], ALU.subtract).then_inc(*frees(key))
                dve.wait_ge(*when("decays", L))
                mul(dterm[:, :, :, :].rearrange("p d t h -> p (d t h)"),
                         dts[:, 0, :, :, :].rearrange("p d t h -> p (d t h)"),
                         ex[:, 1, :, :, :].rearrange("p d t h -> p (d t h)")).then_inc(*does("dterm", L))
                dve.wait_ge(*last_())
                items = ssd_items(L)

                def prepare(n):
                    d, c, want, has, gives = items[n]
                    if not want:
                        return
                    key = (L, "cb", d, c)
                    mask = cst[:, (C_U, C_L)[d]:(C_U, C_L)[d] + P].unsqueeze(1).to_broadcast([P, 2, P])
                    dve.wait_ge(*full(key))
                    mul(cbm[:, n % 2, :, :], slot(key)[:, 0:256].rearrange("p (g i) -> p g i", g=2),
                        mask).then_inc(*frees(key))
                    before = [i for i in items[:n] if i[2]]
                    if before:
                        dve.wait_ge(*when("seg_exp", (L,) + before[-1][0:2]))
                    key = (L, "seg", d, c)
                    dve.wait_ge(*full(key))
                    dve.tensor_tensor(diff[:, :, :], slot(key).rearrange("p (h i) -> p h i", h=8),
                                      wide(exin[:, 0, d, c, :], P), ALU.subtract).then_inc(*frees(key))

                def state(n):
                    d, c, want, has, gives = items[n]
                    if not gives:
                        return
                    key = (L, "state", d, c)
                    dve.wait_ge(*full(key))
                    if has:
                        dve.wait_ge(*when("decayed", (L, d, c)))
                        dve.tensor_tensor(st[:, n % 2, :], slot(key)[:, 0:BW], decayed[:, :],
                                          ALU.add).then_inc(*frees(key))
                    else:
                        dve.tensor_copy(st[:, n % 2, :], slot(key)[:, 0:BW]).then_inc(*frees(key))

                prepare(0)
                state(0)
                for n, (d, c, want, has, gives) in enumerate(items):
                    dve.wait_ge(*last_())
                    if want:
                        dve.wait_ge(*when("seg_exp", (L, d, c)))
                        for g in range(2):
                            mul(seg[:, 4 * g:4 * g + 4, :], seg[:, 4 * g:4 * g + 4, :],
                                cbm[:, n % 2, g:g + 1, :].to_broadcast([P, 4, P])).then_inc(
                                    *does("seg_masked", (L, d, c)))
                    if n + 1 < len(items):
                        prepare(n + 1)
                    key = (L, "y", d, c)
                    if want:
                        dve.wait_ge(*full(key))
                    if n + 1 < len(items):
                        state(n + 1)
                    if want:
                        dve.wait_ge(*when("skip", (L, c)))
                        dve.wait_ge(*last_())
                        if has:
                            mul(by_head(yo[:, :]), by_head(slot(key)[:, HALF:2 * HALF]),
                                wide(ex[:, 0, d, c, :])).then_inc(*does("dve_step"))
                            dve.wait_ge(*last_())
                            dve.tensor_tensor(y_tok[:, c, :], y_tok[:, c, :], yo[:, :],
                                              ALU.add).then_inc(*does("dve_step"))
                            dve.wait_ge(*last_())
                        dve.tensor_tensor(y_tok[:, c, :], slot(key)[:, 0:BW], y_tok[:, c, :],
                                          ALU.add).then_inc(*frees(key))
                for f in range(KB):
                    dve.wait_ge(*read((L, "z", f)))
                for c in range(a // P, NT):
                    key = (L, "yT", c)
                    dve.wait_ge(*full(key))
                    mul(zs[:, :, c * P:(c + 1) * P], slot(key)[:, 0:BW].rearrange("p (f t) -> p f t", f=KB),
                             zs[:, :, c * P:(c + 1) * P]).then_inc(*frees(key))
                for g in range(2):
                    dve.wait_ge(*last_())
                    dve.wait_ge(*read((L, "yms", g)))
                    dve.reciprocal(rstd[:, a:TOK], sdev[:, a:TOK]).then_inc(*does("dve_step"))
                    dve.wait_ge(*last_())
                    for f in range(2 * g, 2 * g + 2):
                        fma(zs[:, f, a:TOK], zs[:, f, a:TOK], par[:, L, R_SN + f:R_SN + f + 1], rstd[:, a:TOK],
                                 ALU.mult, ALU.mult).then_inc(*does("branch", (L, 3, f)))
                    for f in range(2 * g, 2 * g + 2):
                        branch_lo(L, 3, f, zs[:, f, :])

            def residual(L, key, f, gate, a):
                dve.wait_ge(*last_())
                dve.wait_ge(*full(key))
                for b, e, v in kinds(a):
                    ins = fma(x[:, f, b:e], slot(key)[:, T0 + b:T0 + e], mods[:, L, gate + f, v:v + 1], x[:, f, b:e])
                    if e < TOK:
                        ins.then_inc(*does("dve_step"))
                        dve.wait_ge(*last_())
                ins.then_inc(*frees(key))

            for L in range(DEPTH):
                a = first(L)
                norm(L, 1, 0)
                latent(L)
                attention(L)
                merge(L, 0)
                short_conv(L)
                merge(L, 1)
                fourier(L)
                merge(L, 2)
                ssd(L)
                merge(L, 3)
                for k in range(KD):
                    dve.wait_ge(*when("merged_hi", (L, k)))
                    lo(h_lo[:, k, a:TOK], merged[:, k, a:TOK], h_hi[:, k, a:TOK]).then_inc(*does("merged_lo", (L, k)))
                dve.wait_ge(*when("x_back", L))
                for f in range(KD):
                    residual(L, (L, "out", f), f, 16, a)
                norm(L, 2, a)
                for c in range(4):
                    for f in range(KD + 1):
                        dve.wait_ge(*last_())
                        if f < KD:
                            n = c * KD + f
                            key = (L, "w1", c, f)
                            dve.wait_ge(*when("relu", (L, n)))
                            mul(act_f[n % 2][:, a:TOK], cols(key, a), act_r[:, n % 2, a:TOK]).then_inc(*frees(key))
                            ada(key)
                        if f:
                            m = c * KD + f - 1
                            dve.wait_ge(*when("f_hi", (L, m)))
                            lo(f_lo[:, f - 1, a:TOK], act_f[m % 2][:, a:TOK], f_hi[:, f - 1, a:TOK]).then_inc(*does("f_lo", (L, c, f - 1)))
                    for f in range(KD):
                        residual(L, (L, "w2", c, f), f, 40, a)
                        ada((L, "w2", c, f))
            norm(DEPTH, 1, CTX)
        return counts.table


_NAMES = ["x", "c", "ctx", "c_ctx", "ada_w", "ada_b", "norm1_g", "norm2_g", "w_in", "ssm_conv_w", "ssm_conv_b",
          "ssm_a_log", "ssm_dt_bias", "ssm_d", "ssm_norm_g", "sc_conv_w", "mla_qa_g", "mla_wqb", "mla_kva_g",
          "mla_wkvb", "w_branch", "w_out", "mlp_w1", "mlp_w2", "final_norm_g"]


def kernel(**inputs):
    import numpy as _np
    import concourse.bacc as _bacc
    from concourse.bass_utils import run_bass_kernel_spmd as _run

    tables, dft = constant_tables()
    given = {n: _np.ascontiguousarray(inputs[n]) for n in _NAMES}
    given["tables"], given["dft"] = tables, dft
    counts = None
    for _ in range(2):
        nc = _bacc.Bacc("TRN2", target_bir_lowering=False, num_devices=1)
        aps = {n: nc.dram_tensor(f"in_{n}_dram", a.shape, F32, kind="ExternalInput").ap() for n, a in given.items()}
        out = nc.dram_tensor("out_0_dram", (1, LAT, D), F32, kind="ExternalOutput").ap()
        counts = backbone(nc, aps, out, counts)
    r = _run(nc, [{f"in_{n}_dram": a for n, a in given.items()}], core_ids=[0])
    return r.results[0]["out_0_dram"]
```

```python
from contextlib import ExitStack

import numpy as np

import concourse.bass as bass
from concourse import mybir

P = 128
D = 1024
CTX = 256
LAT = 512
TOK = CTX + LAT
NT = TOK // P
GRID_W = 64
DEPTH = 2
DFF = 4 * D
EPS = 1e-6
BW = D // 2
KD = D // P
KB = BW // P
HEADS = 8
SSM_HD = 64
STATE = 128
NOPE, ROPE, VD = 64, 32, 64
QR, KVR = 384, 256
QH = NOPE + ROPE
SCALE = float(QH) ** -0.5
Z0 = 0
XBC0 = Z0 + BW
DT0 = XBC0 + 1024
SC0 = DT0 + 16
QA0 = SC0 + 3 * BW
KVA0 = QA0 + QR
KR0 = KVA0 + KVR
FN0 = KR0 + ROPE
GT0 = FN0 + BW
WT = 1024
NRAW = 4
NSLOT = 4
HALF = 512
T0 = HALF - CTX

F32 = mybir.dt.float32
F32R = mybir.dt.float32r
ALU = mybir.AluOpType
ACT = mybir.ActivationFunctionType
AX = mybir.AxisListType

SCALED_BY_POOL = (2, 4, 6)
SUM_BLOCK = 16
ROWS = NT * 8
C_ID, C_U, C_L, C_KEEP, C_ROT, C_CHAN = 0, 128, 256, 384, 512, 640
C_COS = C_CHAN + 256
C_SIN = C_COS + TOK
C_ALL = C_SIN + TOK
R_CW, R_CB, R_N1, R_N2, R_SN, R_SW, R_QG, R_KG, R_FG, R_C, R_CC, R_END = 0, 40, 48, 56, 64, 68, 80, 83, 85, 93, 101, 109


def constant_tables():
    t = np.zeros((P, C_ALL), np.float32)
    i = np.arange(P)
    t[:, C_ID:C_ID + P] = np.eye(P)
    t[:, C_U:C_U + P] = i[:, None] <= i[None, :]
    t[:, C_L:C_L + P] = i[:, None] >= i[None, :]
    t[:, C_KEEP:C_KEEP + P] = i[None, :] % SUM_BLOCK != 0
    nf = ROPE // 4
    for half in range(2):
        for f in range(nf):
            a = NOPE + 2 * nf * half + f
            t[a + nf, C_ROT + a] = -1.0
            t[a, C_ROT + a + nf] = 1.0
    w = 2 * np.pi * np.outer(i, i) / P
    t[:, C_CHAN:C_CHAN + P] = np.cos(w)
    t[:, C_CHAN + P:C_CHAN + 2 * P] = np.sin(w)
    tok = np.arange(LAT)
    inv = 10000.0 ** (-np.arange(nf) / nf)
    for half, pos in enumerate((tok // GRID_W, tok % GRID_W)):
        ang = inv[:, None] * pos[None, :]
        for part in range(2):
            a = NOPE + 2 * nf * half + nf * part
            t[a:a + nf, C_COS + CTX:C_COS + TOK] = np.cos(ang)
            t[a:a + nf, C_SIN + CTX:C_SIN + TOK] = np.sin(ang)
    t[NOPE:QH, C_COS:C_COS + CTX] = 1.0
    j = np.arange(LAT)
    w = 2 * np.pi * ((j[:, None] * j[None, :]) % LAT) / LAT
    dft = np.stack([np.cos(w), -np.sin(w)]).astype(np.float32)
    return t, dft


class Counts:

    def __init__(self, nc, ctx, known):
        self.nc, self.ctx, self.known, self.now, self.sems = nc, ctx, known or {}, {}, {}
        self.table, self.last = {}, None

    def sem(self, name):
        if name not in self.sems:
            self.sems[name] = self.ctx.enter_context(self.nc.semaphore(name))
            self.now[name] = 0
        return self.sems[name]

    def does(self, name, key=None, by=1):
        sem = self.sem(name)
        self.now[name] += by
        self.table[name, key] = self.now[name]
        self.last = sem, self.now[name]
        return sem, by

    def when(self, name, key):
        at = self.table.get((name, key)) or self.known.get((name, key))
        assert at or not self.known, (name, key)
        return self.sem(name), at or 1

    def mine(self):
        return self.last


def backbone(nc, A, out, known):
    ctx = ExitStack()
    with ctx:
        counts = Counts(nc, ctx, known)
        when, does, mine = counts.when, counts.does, counts.mine

        def sb(name, shape, dt=F32, scope=ctx):
            return scope.enter_context(nc.sbuf_tensor(name, shape, dt))

        cst = sb("cst", [P, C_ALL])
        par = sb("par", [P, DEPTH, P])
        adab = sb("adab", [P, DEPTH, 48])
        mods = sb("mods", [P, DEPTH, 48, 2])
        gsc = sb("gsc", [P, 8, 2])
        dt_raw = sb("dt_raw", [P, NT, 16])
        heads_bc = sb("heads_bc", [P, DEPTH, 40])
        ones = sb("ones", [P, 4, P])
        epsc = sb("epsc", [P, 1])
        silc = sb("silc", [P, KD, 2])
        ksum = sb("ksum", [P, 2, 2, P])
        raw = sb("raw", [P, NRAW, WT])
        w_hi = sb("w_hi", [P, 2, WT], F32R)
        w_lo = sb("w_lo", [P, 2, WT], F32R)
        h_hi = sb("h_hi", [P, KD, TOK], F32R)
        h_lo = sb("h_lo", [P, KD, TOK], F32R)
        rstd = sb("rstd", [P, TOK])
        sdev = sb("sdev", [P, TOK])
        rmax = sb("rmax", [P, 2])
        rsum = sb("rsum", [P, 2])
        rrec = sb("rrec", [P, 2])
        psum = [ctx.enter_context(nc.psum_tensor(f"slot{i}", [P, 2 * HALF], F32)) for i in range(NSLOT)]

        with ExitStack() as m:
            br_hi = sb("br_hi", [P, KB, TOK], F32R, m)
            br_lo = sb("br_lo", [P, KB, TOK], F32R, m)
            with ExitStack() as q:
                kT = sb("kT", [P, HEADS, TOK], F32, q)
                vt = sb("vt", [P, NT, BW], F32, q)
                qT = sb("qT", [P, HEADS, TOK], F32, q)
                with ExitStack() as r:
                    ln_hi = sb("ln_hi", [P, 3, TOK], F32R, r)
                    ln_lo = sb("ln_lo", [P, 3, TOK], F32R, r)
                with ExitStack() as r:
                    pT = sb("pT", [P, NT, TOK], F32, r)
            sigm = sb("sigm", [P, 2, TOK], F32, m)
            gated = sb("gated", [P, TOK], F32, m)
            merged = sb("merged", [P, KD, TOK], F32, m)
            with ExitStack() as q:
                q.enter_context(nc.sbuf_tensor("past_mlp", [P, KD, TOK], F32))
                prod = sb("prod", [P, KD, P], F32, q)
            with ExitStack() as q:
                cgs = sb("cgs", [P, 2, TOK], F32, q)
                cgx = sb("cgx", [P, 2, TOK], F32, q)
                cvo = sb("cvo", [P, 2, TOK], F32, q)
            with ExitStack() as q:
                dft = sb("dft", [P, 2, 4, LAT], F32, q)
                ch_hi = sb("ch_hi", [P, 256], F32R, q)
                ch_lo = sb("ch_lo", [P, 256], F32R, q)
                fn_hi = sb("fn_hi", [P, TOK], F32R, q)
                fn_lo = sb("fn_lo", [P, TOK], F32R, q)
                fy = sb("fy", [P, NT, 256], F32, q)
            with ExitStack() as q:
                dts = sb("dts", [P, 6, 2, NT, 8], F32, q)
                ex = sb("ex", [P, 3, 2, NT, 8], F32, q)
                dterm = sb("dterm", [P, 2, NT, 8], F32, q)
                laR = sb("laR", [P, P], F32, q)
                cumR = sb("cumR", [P, P], F32, q)
                blkR = sb("blkR", [P, 8], F32, q)
                exin = sb("exin", [P, 3, 2, NT, 8], F32, q)
                xs_tok = sb("xs_tok", [P, NT, BW], F32, q)
                b_tok = sb("b_tok", [P, NT, 256], F32, q)
                y_tok = sb("y_tok", [P, NT, BW], F32, q)
                with ExitStack() as r:
                    bc = sb("bc", [P, 4, TOK], F32, r)
                with ExitStack() as r:
                    zs = sb("zs", [P, KB, TOK], F32, r)
        with ExitStack() as m:
            with ExitStack() as q:
                lraw = sb("lraw", [P, 5, TOK], F32, q)
                sql = sb("sql", [P, 3, TOK], F32, q)
            with ExitStack() as q:
                diff = sb("diff", [P, 8, P], F32, q)
                seg = sb("seg", [P, 8, P], F32, q)
                cbm = sb("cbm", [P, 2, 2, P], F32, q)
                xd = sb("xd", [P, 2, BW], F32, q)
                xr = sb("xr", [P, BW], F32, q)
                st = sb("st", [P, 2, BW], F32, q)
                yo = sb("yo", [P, BW], F32, q)
                decayed = sb("decayed", [P, BW], F32, q)
        with ExitStack() as m:
            x = sb("x", [P, KD, TOK], F32, m)
            with ExitStack() as q:
                sqx = sb("sqx", [P, KD, TOK], F32, q)
                parr = sb("parr", [P, DEPTH + 1, P], F32, q)
            with ExitStack() as q:
                xin = sb("xin", [P, 2, D], F32, q)
            with ExitStack() as q:
                f_hi = sb("f_hi", [P, KD, TOK], F32R, q)
                f_lo = sb("f_lo", [P, KD, TOK], F32R, q)
                act_r = sb("act_r", [P, 2, TOK], F32, q)
            with ExitStack() as q:
                yout = sb("yout", [P, 2, D], F32, q)
                xf = sb("xf", [P, KD, TOK], F32, q)
        y_sq = xs_tok[:, :, :].rearrange("p t c -> p (t c)").rearrange("p (k t) -> p k t", k=KB)
        act_f = [rstd, sdev]
        probs = [rstd, sdev]
        cacc = [gated, rstd]
        conv = sigm[:, 0, :]
        dtT = sql[0:32, 2, :]

        x_spill = nc.dram_tensor("x_spill", (P, KD * TOK), F32, kind="Internal").ap()

        ADA_FIRST = range(0, 2 * KD, 2)
        ADA_LATER = [(0, f) for f in range(2 * KD, 6 * KD)] + [(1, f) for f in range(6 * KD)]
        ada_after = {}
        for k in range(4):
            for f in range(KD):
                ada_after[0, "gate", k, f] = len(ada_after)
        for c in range(4):
            for f in range(KD):
                ada_after[0, "w1", c, f] = len(ada_after)
            for f in range(0, KD, 2):
                ada_after[0, "w2", c, f] = len(ada_after)
        assert len(ada_after) == len(ADA_LATER)

        tiles, tile_of = [], {}

        def tile(key, src, k0, kt, c0, cols, pitch=0):
            tile_of[key] = len(tiles)
            tiles.append((src[k0 * P:(k0 + kt) * P, c0:c0 + cols].rearrange("(k p) c -> p k c", p=P), kt, cols,
                          pitch or cols))

        def ada_tile(n):
            if n < len(ADA_LATER):
                L, f = ADA_LATER[n]
                tile((L, "ada", f), A["ada_w"][L], 0, KD, P * f, P)

        def ada_tile_after(after):
            if after in ada_after:
                ada_tile(ada_after[after] + 1)

        def gate_tile(L, k, f, branch):
            tile((L, "gate", k, f), A["w_in"][L], 0, KD, GT0 + D * branch + P * f, P)
            ada_tile_after((L, "gate", k, f))

        def merge_tiles(L, k, branch):
            for j in range(4):
                for f in (2 * j, 2 * j + 1):
                    gate_tile(L, k, f, branch)
                tile((L, "proj", k, j), A["w_branch"][L, branch], 0, KB, 256 * j, 256)

        for L in range(DEPTH):
            win = A["w_in"][L]
            if L == 0:
                for f in range(2 * KD):
                    tile((L, "ada", f), A["ada_w"][L], 0, KD, P * f, P)
            for f in range(2):
                tile((L, "kva", f), win, 0, KD, KVA0 + P * f, P)
            tile_of[L, "kr"] = len(tiles)
            both = win[:, DT0:DT0 + 2 * (KR0 - DT0)].rearrange("(k p) (b s) -> p k b s", p=P, b=2)
            tiles.append((both[:, :, :, 0:64], KD, P, P))
            for f in range(3):
                tile((L, "qa", f), win, 0, KD, QA0 + P * f, P)
            for i in range(2):
                tile((L, "wkv", i), A["mla_wkvb"][L], 0, 2, 512 * i, 512)
            for i in range(3):
                tile((L, "wq", i), A["mla_wqb"][L], 0, 3, 3 * QH * i, min(320, HEADS * QH - 3 * QH * i), 320)
            if L == 0:
                ada_tile(0)
            merge_tiles(L, 0, 2)
            for f in range(KB):
                tile((L, "cg", f), win, 0, KD, SC0 + BW + P * f, P)
                tile((L, "xin", f), win, 0, KD, SC0 + 2 * BW + P * f, P)
                tile((L, "bg", f), win, 0, KD, SC0 + P * f, P)
            merge_tiles(L, 1, 1)
            for f in range(KB):
                tile((L, "fn", f), win, 0, KD, FN0 + P * f, P)
            merge_tiles(L, 2, 3)
            for f in range(KD):
                tile((L, "xbc", f), win, 0, KD, XBC0 + P * f, P)
            for f in range(KB):
                tile((L, "z", f), win, 0, KD, Z0 + P * f, P)
            merge_tiles(L, 3, 0)
            for f in range(KD):
                tile((L, "out", f), A["w_out"][L], 0, KD, P * f, P)
            for c in range(4):
                for f in range(KD):
                    tile((L, "w1", c, f), A["mlp_w1"][L], 0, KD, D * c + P * f, P)
                    ada_tile_after((L, "w1", c, f))
                for f in range(KD):
                    tile((L, "w2", c, f), A["mlp_w2"][L], KD * c, KD, P * f, P)
                    ada_tile_after((L, "w2", c, f))
        key_value_tiles = {s for key, s in tile_of.items() if key[1] == "wkv"}
        step_and_key_tiles = {s for key, s in tile_of.items() if key[1] == "kr"}
        whole = {s for key, s in tile_of.items() if key[1] == "ada"}
        split = [s for s in range(len(tiles)) if s not in whole]
        place = {s: n for n, s in enumerate(split)}

        ALL = [(T0, 0, CTX), (HALF, CTX, LAT)]
        LATS = ALL[1:]

        def spans(L):
            return ALL if L < DEPTH - 1 else LATS

        def first(L):
            return 0 if L < DEPTH - 1 else CTX

        def kinds(a):
            return ([(0, CTX, 1)] if a == 0 else []) + [(CTX, TOK, 0)]

        order, last_use = {}, {}

        def slot(key):
            return psum[order[key] % NSLOT][:, :]

        def cols(key, a, p0=0, p1=P):
            return slot(key)[p0:p1, T0 + a:T0 + TOK]

        slot_full = counts.sem("slot_full")
        slot_read = [counts.sem(f"slot{i}_read") for i in range(NSLOT)]

        def full(key):
            return slot_full, order[key] + 1

        def frees(key):
            counts.last = slot_read[order[key] % NSLOT], order[key] // NSLOT + 1
            return slot_read[order[key] % NSLOT], 1

        def read(key):
            return slot_read[order[key] % NSLOT], order[key] // NSLOT + 1

        block = ctx.enter_context(nc.Block())

        def att_items(L):
            return [(h, qt) for h in range(HEADS) for qt in range(first(L) // P, NT)]

        def ssd_items(L):
            return [(d, c, c * P >= first(L), n > 0, n < NT - 1)
                    for d, chunks in enumerate(((0, 1, 2, 3, 4, 5), (1, 0, 5, 4, 3, 2))) for n, c in enumerate(chunks)]

        def fourier_parts(L):
            parts = [(0, 2, 0, CTX, 2, (CTX * P) ** -0.5), (2, 4, CTX, LAT, 1, (LAT * P) ** -0.5)]
            return parts[first(L) // CTX:]

        @block.tensor
        def _(pe):
            ident = cst[:, C_ID:C_ID + P]

            def take(key):
                order[key] = len(order)
                if order[key] >= NSLOT:
                    pe.wait_ge(slot_read[order[key] % NSLOT], order[key] // NSLOT)
                return slot(key)

            def weights(wkey, key):
                s = tile_of[wkey]
                pe.wait_ge(*when("w_lo", s))
                last_use[s] = order[key]
                _, kt, _, pitch = tiles[s]
                return [w[:, place[s] % 2, 0:kt * pitch].rearrange("p (k c) -> p k c", k=kt) for w in (w_hi, w_lo)]

            def product(key, wkey, kts, col, a_hi, a_lo, sp, ready=None, backwards=False):
                o = take(key)
                wh, wl = weights(wkey, key)
                rows = range(kts)[::-1 if backwards else 1]
                for k in rows:
                    if ready:
                        ready(k)
                    for n, (w, a) in enumerate(((wh, a_hi), (wh, a_lo), (wl, a_hi))):
                        for c0, t0, nt in sp:
                            last = pe.matmul(o[:, c0:c0 + nt], w[:, k, col:col + P], a[:, k, t0:t0 + nt],
                                             start=(k == rows[0] and n == 0), stop=(k == rows[-1] and n == 2))
                last.then_inc(slot_full, 1)

            def mean_square(key, src, k0, k1, mat, sp, name, tag):
                o = take(key)
                for k in range(k0, k1):
                    pe.wait_ge(*when(name, (tag, k)))
                    for c0, t0, nt in sp:
                        last = pe.matmul(o[:, c0:c0 + nt], ones[:, mat, :], src[:, k, t0:t0 + nt],
                                         start=(k == k0), stop=(k == k1 - 1))
                last.then_inc(slot_full, 1)

            def mean_of_x(key, sp):
                o = take(key)
                pe.wait_ge(*when("square_added", ((key[0], key[2]), KD - 1)))
                for c0, t0, nt in sp:
                    last = pe.matmul(o[:, c0:c0 + nt], ones[:, 1, :], rstd[:, t0:t0 + nt], start=True, stop=True)
                last.then_inc(slot_full, 1)

            def turn(key, blocks, to=P):
                o = take(key)
                for n, b in enumerate(blocks):
                    last = pe.transpose(o[:, n * to:(n + 1) * to], b, ident if to == P else cst[0:to, C_ID:C_ID + to])
                last.then_inc(slot_full, 1)

            def ada_first():
                pe.wait_ge(*when("silu_c", 0))
                for f in ADA_FIRST:
                    o = take((0, "ada", f))
                    for i in range(2):
                        s = tile_of[0, "ada", f + i]
                        last_use[s] = order[0, "ada", f]
                        pe.wait_ge(*when(f"raw{s % NRAW}_loaded", s))
                        w = raw[:, s % NRAW, :].rearrange("p (k c) -> p k c", k=KD)
                        for k in range(KD):
                            last = pe.matmul(o[:, 2 * i:2 * i + 2], w[:, k, :], silc[:, k, :],
                                             start=(k == 0), stop=(k == KD - 1))
                    last.then_inc(slot_full, 1)

            def ada_sum(after):
                if after not in ada_after:
                    return
                n = ada_after[after]
                if n == 0:
                    last_use[tile_of[(0, "ada", ADA_LATER[0][1])]] = order[0, "o", HEADS - 1]
                pe.wait_ge(*when("ada_ksum", n))
                o = take(("ada", n))
                for v in range(2):
                    last = pe.matmul(o[:, v:v + 1], ksum[:, n % 2, v, :], ones[:, 0, 0:1], start=True, stop=True)
                last.then_inc(slot_full, 1)
                if n + 1 < len(ADA_LATER):
                    L, f = ADA_LATER[n + 1]
                    last_use[tile_of[L, "ada", f]] = order["ada", n]

            def rotated(key, src, h, sp):
                o = take(key)
                for c0, t0, nt in sp:
                    last = pe.matmul(o[:, c0:c0 + nt], cst[NOPE:QH, C_ROT:C_ROT + P], src[NOPE:QH, h, t0:t0 + nt],
                                     start=True, stop=True)
                last.then_inc(slot_full, 1)

            def key_pair(L, pair):
                o = take((L, "k", pair))
                col = P * (pair % 2)
                wh, wl = weights((L, "wkv", pair // 2), (L, "k", pair))
                for k in range(2):
                    if pair == 0:
                        pe.wait_ge(*when("kvn_lo", (L, k)))
                    for n, (w, b) in enumerate(((wh, ln_hi), (wh, ln_lo), (wl, ln_hi))):
                        for c0, t0, nt in ALL:
                            last = pe.matmul(o[:, c0:c0 + nt], w[:, k, col:col + P], b[:, k, t0:t0 + nt],
                                             start=(k == 0 and n == 0), stop=(k == 1 and n == 2))
                last.then_inc(slot_full, 1)

            def latent(L):
                sp = spans(L)
                for f in range(2):
                    product((L, "kva", f), (L, "kva", f), KD, 0, h_hi, h_lo, ALL,
                            (lambda k: pe.wait_ge(*when("h_lo", (L, 1, k)))) if f == 0 else None)
                product((L, "kr"), (L, "kr"), KD, 0, h_hi, h_lo, ALL, backwards=True)
                mean_square((L, "kvms"), sql, 0, 2, 3, ALL, "kv_squared", L)
                pe.wait_ge(*when("kr_copied", L))
                rotated((L, "krot"), kT, 0, ALL)
                turn((L, "dtT"), [dtT[:, t * P:(t + 1) * P] for t in range(NT)], 32)
                for f in range(3):
                    product((L, "qa", f), (L, "qa", f), KD, 0, h_hi, h_lo, sp)
                for i in range(2):
                    for pair in range(2 * i, 2 * i + 2):
                        key_pair(L, pair)
                    if i == 0:
                        mean_square((L, "qms"), sql, 0, 3, 2, sp, "q_squared", L)
                    for tp in range(NT // 2):
                        o = take((L, "v", i, tp))
                        wh, wl = weights((L, "wkv", i), (L, "v", i, tp))
                        for u in range(2):
                            t = 2 * tp + u
                            for k in range(2):
                                for n, (a, w) in enumerate(((ln_hi, wh), (ln_hi, wl), (ln_lo, wh))):
                                    last = pe.matmul(o[:, HALF * u:HALF * u + 256], a[:, k, t * P:(t + 1) * P],
                                                     w[:, k, 256:512], start=(k == 0 and n == 0),
                                                     stop=(k == 1 and n == 2))
                        last.then_inc(slot_full, 1)
                for h in range(HEADS + 1):
                    if h < HEADS:
                        product((L, "q", h), (L, "wq", h // 3), 3, QH * (h % 3), ln_hi, ln_lo, sp,
                                (lambda k: pe.wait_ge(*when("qn_lo", (L, k)))) if h == 0 else None)
                    if h >= 1:
                        pe.wait_ge(*when("q_copied", (L, h - 1)))
                        rotated((L, "qrot", h - 1), qT, h - 1, sp)

            def attention(L):
                items = att_items(L)

                def scores(h, qt):
                    if (h, qt) == items[0]:
                        pe.wait_ge(*when("k_rotated", L))
                    if qt == items[0][1]:
                        pe.wait_ge(*when("q_rotated", (L, h)))
                        pe.wait_ge(*read((L, "k", h // 2)))
                    o = take((L, "s", h, qt))
                    for c0, t0, nt in ALL[:1] if qt < 2 else ALL:
                        last = pe.matmul(o[:, c0:c0 + nt], qT[0:QH, h, qt * P:(qt + 1) * P],
                                         kT[0:QH, h, t0:t0 + nt], start=True, stop=True)
                    last.then_inc(slot_full, 1)

                def values(h):
                    o = take((L, "o", h))
                    for qt in range(items[0][1], NT):
                        pe.wait_ge(*read((L, "pT", h, qt)))
                    lo = (h % 2) * VD
                    for c0, q0, nq in spans(L):
                        kts = NT if q0 else 2
                        for k in range(kts):
                            if h == 0:
                                pe.wait_ge(*read((L, "v", 0, k // 2)))
                            if h == 4:
                                pe.wait_ge(*read((L, "v", 1, k // 2)))
                            last = pe.matmul(o[lo:lo + VD, c0:c0 + nq], vt[:, k, h * VD:(h + 1) * VD],
                                             pT[:, k, q0:q0 + nq], start=(k == 0), stop=(k == kts - 1))
                    last.then_inc(slot_full, 1)

                for n in range(len(items) + 3):
                    if n < len(items):
                        scores(*items[n])
                    if n >= 3 and items[n - 3][1] == NT - 1:
                        values(items[n - 3][0])
                    if 2 <= n < len(items) + 2:
                        h, qt = items[n - 2]
                        pe.wait_ge(*when("probs", (L, h, qt)))
                        turn((L, "pT", h, qt), [probs[n % 2][:, k * P:(k + 1) * P] for k in range(2 if qt < 2 else NT)])

            def branch_ready(L, k, i):
                if k == 0:
                    pe.wait_ge(*read((L, "o", 2 * i)))
                    pe.wait_ge(*read((L, "o", 2 * i + 1)))
                elif k == 2:
                    pe.wait_ge(*read((L, "fo", i)))
                else:
                    pe.wait_ge(*when("branch_lo", (L, k, i)))

            def merge(L, k):
                sp = spans(L)
                for j in range(4):
                    for f in (2 * j, 2 * j + 1):
                        product((L, "gate", k, f), (L, "gate", k, f), KD, 0, h_hi, h_lo, sp)
                        ada_sum((L, "gate", k, f))
                    for f in (2 * j, 2 * j + 1):
                        product((L, "proj", k, f), (L, "proj", k, j), KB, P * (f % 2), br_hi, br_lo, sp,
                                (lambda i: branch_ready(L, k, i)) if f == 0 else None)

            def short_conv(L):
                for f in range(KB):
                    for what in ("cg", "xin", "bg"):
                        product((L, what, f), (L, what, f), KD, 0, h_hi, h_lo, spans(L))

            def fourier(L):
                pairs = range(first(L) // CTX, NT // 2)
                product((L, "fn", 0), (L, "fn", 0), KD, 0, h_hi, h_lo, spans(L))
                pe.wait_ge(*when("channel_dft", L))
                for g in range(4):
                    pe.wait_ge(*read((L, "fn", g)))
                    for tp in pairs:
                        o = take((L, "fy", g, tp))
                        for u in range(2):
                            t = 2 * tp + u
                            for n, (a, b) in enumerate(((fn_hi, ch_hi), (fn_hi, ch_lo), (fn_lo, ch_hi))):
                                last = pe.matmul(o[:, HALF * u:HALF * u + 256], a[:, t * P:(t + 1) * P], b[:, :],
                                                 start=(n == 0), stop=(n == 2))
                        last.then_inc(slot_full, 1)
                    if g < 3:
                        product((L, "fn", g + 1), (L, "fn", g + 1), KD, 0, h_hi, h_lo, spans(L))
                    else:
                        pe.wait_ge(*when("dft_loaded", L))
                    if g == 0:
                        pe.wait_ge(*when("dft_loaded", L))
                    for tp in pairs:
                        pe.wait_ge(*read((L, "fy", g, tp)))
                    o = take((L, "fo", g))
                    for tile0, n_t, t0, nt, step, _ in fourier_parts(L):
                        for j in range(n_t):
                            for part in range(2):
                                last = pe.matmul(o[:, T0 + t0:T0 + t0 + nt], fy[:, tile0 + j, part * P:(part + 1) * P],
                                                 dft[:, part, j, 0:LAT:step], start=(j == 0 and part == 0),
                                                 stop=(j == n_t - 1 and part == 1))
                    last.then_inc(slot_full, 1)

            def cum_turned(L):
                pe.wait_ge(*when("cum_rows", L))
                o = take((L, "cum"))
                for d in range(2):
                    last = pe.matmul(o[:, HALF * d:HALF * d + ROWS], cumR[64 * d:64 * d + ROWS, :],
                                     cst[64 * d:64 * d + ROWS, C_ID + 64 * d:C_ID + 64 * d + ROWS],
                                     start=True, stop=True)
                last.then_inc(slot_full, 1)

            def ssd(L):
                for f in range(KD):
                    product((L, "xbc", f), (L, "xbc", f), KD, 0, h_hi, h_lo, ALL)
                    if 1 <= f <= 6:
                        pe.wait_ge(*when("conv_silu", (L, f - 1)))
                        src = conv if f - 1 < 4 else bc[:, f - 5, :]
                        turn((L, "xT", f - 1), [src[:, t * P:(t + 1) * P] for t in range(NT)])
                    if f == 5:
                        pe.wait_ge(*when("la", L))
                        o = take((L, "laT"))
                        la = dts[:, 3, :, :, :].rearrange("p d t h -> p d (t h)")
                        for d in range(2):
                            last = pe.matmul(o[64 * d:64 * d + ROWS, 0:P], la[:, d, :], ident, start=True, stop=True)
                        last.then_inc(slot_full, 1)
                    if f == 6:
                        cum_turned(L)
                pe.wait_ge(*read((L, "cum")))
                o = take((L, "tot"))
                for d, end in enumerate((P - 1, 0)):
                    last = pe.matmul(o[:, ROWS * d:ROWS * d + ROWS],
                                     cst[:, C_ID + end:C_ID + end + 1].to_broadcast([P, P]),
                                     exin[:, 0, d, :, :].rearrange("p t h -> p (t h)"), start=True, stop=True)
                last.then_inc(slot_full, 1)
                for f in range(2):
                    product((L, "z", f), (L, "z", f), KD, 0, h_hi, h_lo, spans(L))
                items = ssd_items(L)

                def within(n):
                    d, c, want, has, gives = items[n]
                    tk = slice(c * P, (c + 1) * P)
                    if want:
                        o = take((L, "cb", d, c))
                        pe.wait_ge(*when("conv_silu", (L, 7)))
                        for g in range(2):
                            last = pe.matmul(o[:, g * P:(g + 1) * P], bc[:, g, tk], bc[:, 2 + g, tk],
                                             start=True, stop=True)
                        last.then_inc(slot_full, 1)
                        o = take((L, "seg", d, c))
                        rows = slice(64 * d, 64 * d + ROWS)
                        for h in range(8):
                            r = C_ID + 64 * d + 8 * c + h
                            last = pe.matmul(o[:, h * P:(h + 1) * P], cst[rows, r:r + 1].to_broadcast([ROWS, P]),
                                             cumR[rows, :], start=True, stop=True)
                        last.then_inc(slot_full, 1)
                    if gives:
                        pe.wait_ge(*when("xr", (L, d, c)))
                        o = take((L, "state", d, c))
                        for g in range(2):
                            last = pe.matmul(o[:, g * 256:(g + 1) * 256], b_tok[:, c, g * P:(g + 1) * P],
                                             xr[:, g * 256:(g + 1) * 256], start=True, stop=True)
                        last.then_inc(slot_full, 1)

                def outputs(n):
                    d, c, want, has, gives = items[n]
                    if not want:
                        return
                    tk = slice(c * P, (c + 1) * P)
                    o = take((L, "y", d, c))
                    if has:
                        pe.wait_ge(*read((L, "state") + items[n - 1][0:2]))
                        for g in range(2):
                            pe.matmul(o[:, HALF + g * 256:HALF + (g + 1) * 256], bc[:, 2 + g, tk],
                                      st[:, (n - 1) % 2, g * 256:(g + 1) * 256], start=True, stop=True)
                    pe.wait_ge(*when("seg_masked", (L, d, c)))
                    pe.wait_ge(*when("xd", (L, d, c)))
                    for h in range(8):
                        last = pe.matmul(o[:, h * 64:(h + 1) * 64], seg[:, h, :], xd[:, n % 2, h * 64:(h + 1) * 64],
                                         start=True, stop=True)
                    last.then_inc(slot_full, 1)

                pe.wait_ge(*read((L, "xT", 5)))
                within(0)
                for n in range(len(items)):
                    if n + 1 < len(items):
                        within(n + 1)
                    outputs(n)
                for f in range(2, KB):
                    product((L, "z", f), (L, "z", f), KD, 0, h_hi, h_lo, spans(L))
                pe.wait_ge(*read((L, "y") + items[-1][0:2]))
                for c in range(first(L) // P, NT):
                    turn((L, "yT", c), [y_tok[:, c, f * P:(f + 1) * P] for f in range(KB)])
                for g in range(2):
                    mean_square((L, "yms", g), y_sq, 2 * g, 2 * g + 2, 3, spans(L), "y_squared", L)

            pe.wait_ge(*when("loaded", "tables"))
            for t in range(NT):
                pe.wait_ge(*when(f"x_in{t % 2}", t))
                turn(("x", t), [xin[:, t % 2, k * P:(k + 1) * P] for k in range(KD)])
            for name in ("loaded0", "loaded1"):
                pe.wait_ge(*when(name, "all"))
            turn("params", [parr[:, i, :] for i in range(DEPTH + 1)])
            for L in range(DEPTH):
                mean_of_x((L, "ms", 1), ALL)
                if L == 0:
                    ada_first()
                latent(L)
                attention(L)
                merge(L, 0)
                short_conv(L)
                merge(L, 1)
                fourier(L)
                merge(L, 2)
                ssd(L)
                merge(L, 3)
                for f in range(KD):
                    product((L, "out", f), (L, "out", f), KD, 0, h_hi, h_lo, spans(L),
                            (lambda k: pe.wait_ge(*when("merged_lo", (L, k)))) if f == 0 else None)
                mean_of_x((L, "ms", 2), spans(L))
                for c in range(4):
                    for f in range(KD):
                        product((L, "w1", c, f), (L, "w1", c, f), KD, 0, h_hi, h_lo, spans(L),
                                (lambda k: pe.wait_ge(*when("h_lo", (L, 2, k)))) if c == f == 0 else None)
                        ada_sum((L, "w1", c, f))
                    for f in range(KD):
                        product((L, "w2", c, f), (L, "w2", c, f), KD, 0, f_hi, f_lo, spans(L),
                                (lambda k: pe.wait_ge(*when("f_lo", (L, c, k)))) if f == 0 else None)
                        ada_sum((L, "w2", c, f))
            mean_of_x((DEPTH, "ms", 1), LATS)
            for t in range(CTX // P, NT):
                o = take(("y", t))
                for k in range(KD):
                    if t == CTX // P:
                        pe.wait_ge(*when("x_scaled", k))
                    last = pe.transpose(o[:, k * P:(k + 1) * P], xf[:, k, t * P:(t + 1) * P], ident)
                last.then_inc(slot_full, 1)

        def load_parameters(queue, L, name):
            queue.wait_ge(*when("cleared", 0))
            vec = "(t c) -> t c"
            for r0, src, n in ((R_CW, A["ssm_conv_w"][L].rearrange("k (t c) -> (k t) c", c=P), 40),
                               (R_CB, A["ssm_conv_b"][L].rearrange(vec, c=P), 8),
                               (R_N1, A["norm1_g"][L].rearrange(vec, c=P), 8),
                               (R_N2, A["norm2_g"][L].rearrange(vec, c=P), 8),
                               (R_SN, A["ssm_norm_g"][L].rearrange(vec, c=P), 4),
                               (R_SW, A["sc_conv_w"][L].rearrange("k (t c) -> (k t) c", c=P), 12),
                               (R_QG, A["mla_qa_g"][L].rearrange(vec, c=P), 3),
                               (R_KG, A["mla_kva_g"][L].rearrange(vec, c=P), 2),
                               (R_FG, A["final_norm_g"].rearrange(vec, c=P), 8),
                               (R_C, A["c"][0].rearrange(vec, c=P), 8),
                               (R_CC, A["c_ctx"].rearrange(vec, c=P), 8)):
                queue.dma_start(parr[r0:r0 + n, L, :], src).then_inc(*does(name, r0, 16))
            queue.dma_start(parr[48 * L:48 * L + 48, DEPTH, :], A["ada_b"][L].rearrange(vec, c=P)).then_inc(
                *does(name, "ada", 16))
            for o, src, n in ((0, A["ssm_a_log"][L].rearrange("a b -> (a b)"), 16),
                              (16, A["ssm_dt_bias"][L].rearrange("a b -> (a b)"), 16), (32, A["ssm_d"][L], 8)):
                queue.dma_start(heads_bc[:, L, o:o + n], src.partition_broadcast(P)).then_inc(*does(name, "all", 16))

        @block.sync
        def _(sp_):
            load_parameters(sp_, 0, "loaded0")
            for s, (src, kt, ncol, pitch) in enumerate(tiles):
                if s >= NRAW:
                    if s - NRAW in split:
                        sp_.wait_ge(*when("w_lo", s - NRAW))
                    elif s - NRAW < 2 * KD:
                        sp_.wait_ge(slot_full, last_use[s - NRAW] + 1)
                    else:
                        sp_.wait_ge(*when("ada_used", s - NRAW))
                dst = raw[:, s % NRAW, 0:kt * pitch].rearrange("p (k c) -> p k c", k=kt)[:, :, 0:ncol]
                if s in key_value_tiles:
                    pieces = [(dst[:, k, 256 * t:256 * t + 256].rearrange("p (h c) -> p h c", h=4),
                               src[:, k, :].rearrange("p (h t c) -> p t h c", t=2, h=4)[:, t])
                              for k in range(kt) for t in range(2)]
                elif s in step_and_key_tiles:
                    pieces = [(dst[:, :, 64 * b:64 * b + 64], src[:, :, b, :]) for b in range(2)]
                else:
                    pieces = [(dst, src)]
                for to, piece in pieces:
                    sp_.dma_start(to, piece).then_inc(*does(f"raw{s % NRAW}_loaded", s, 16))

        @block.gpsimd
        def _(pool):
            load_parameters(pool, 1, "loaded1")

            def norm(L, which, a):
                pool.wait_ge(*when("rstd", (L, which)))
                for k in SCALED_BY_POOL:
                    pool.tensor_tensor(sqx[:, k, a:TOK], x[:, k, a:TOK], rstd[:, a:TOK],
                                       ALU.mult).then_inc(*does("x_by_rstd", (L, which, k)))

            def by_head(ap):
                return ap.rearrange("p (h c) -> p h c", c=64)

            def scaled(o, a, per_head):
                return pool.tensor_tensor(by_head(o), by_head(a), per_head.unsqueeze(2).to_broadcast([P, 8, 64]),
                                          ALU.mult)

            def ssd(L):
                for f in range(4):
                    pool.wait_ge(*read((L, "xT", f)))
                pool.wait_ge(*when("dterm", L))
                items = ssd_items(L)
                states, outs = [], []
                for n, (d, c, want, has, gives) in enumerate(items):
                    if gives:
                        if states:
                            pool.wait_ge(*full(states[-1]))
                        scaled(xr[:, :], xs_tok[:, c, :], dterm[:, d, c, :]).then_inc(*does("xr", (L, d, c)))
                        states.append((L, "state", d, c))
                    if want:
                        if [m for m in outs if m <= n - 2]:
                            m = [m for m in outs if m <= n - 2][-1]
                            pool.wait_ge(*full((L, "y") + items[m][0:2]))
                        scaled(xd[:, n % 2, :], xs_tok[:, c, :], dts[:, 0, d, c, :]).then_inc(*does("xd", (L, d, c)))
                        outs.append(n)
                        if d == 0:
                            scaled(y_tok[:, c, :], xs_tok[:, c, :], heads_bc[:, L, 32:40]).then_inc(
                                *does("skip", (L, c)))
                    if gives and has:
                        pool.wait_ge(*read((L, "state") + items[n - 1][0:2]))
                        scaled(decayed[:, :], st[:, (n - 1) % 2, :], ex[:, 2, d, c, :]).then_inc(
                            *does("decayed", (L, d, c)))

            for s in split:
                for L in range(DEPTH):
                    if L and s == tile_of[L, "kr"]:
                        norm(L, 1, 0)
                    if s == tile_of[L, "w1", 0, 2]:
                        norm(L, 2, first(L))
                    if s == tile_of[L, "z", 2]:
                        ssd(L)
                pool.wait_ge(*when("w_hi", s))
                pool.tensor_tensor(w_lo[:, place[s] % 2, :], raw[:, s % NRAW, :],
                                   w_hi[:, place[s] % 2, :].bitcast(F32), ALU.subtract).then_inc(*does("w_lo", s))

        @block.scalar
        def _(act):
            A_ = nc.scalar.activation
            fed = [0]

            def round_weights(limit):
                while fed[0] < len(split):
                    s = split[fed[0]]
                    needs = [last_use[split[fed[0] - 2]]] if fed[0] >= 2 else []
                    needs += [last_use.get(t, len(order)) for t in range(max(0, s - 2 * NRAW), s - NRAW + 1)
                              if t in whole]
                    if needs and max(needs) > limit:
                        break
                    act.wait_ge(*when(f"raw{s % NRAW}_loaded", s))
                    if fed[0] >= 2:
                        act.wait_ge(slot_full, last_use[split[fed[0] - 2]] + 1)
                    A_(w_hi[:, fed[0] % 2, :], raw[:, s % NRAW, :], ACT.Copy).then_inc(*does("w_hi", s))
                    fed[0] += 1

            act.dma_start(cst[:, :], A["tables"]).then_inc(*does("loaded", "tables", 16))
            for t in range(NT):
                if t >= 2:
                    act.wait_ge(*full(("x", t - 2)))
                src = A["ctx"][0, t * P:(t + 1) * P, :] if t < 2 else A["x"][0, (t - 2) * P:(t - 1) * P, :]
                act.dma_start(xin[:, t % 2, :], src).then_inc(
                    *does(f"x_in{t % 2}", t, 16))
            act.wait_ge(*read("params"))
            A_(silc[:, :, 0], par[:, 0, R_C:R_C + 8], ACT.Silu)
            A_(silc[:, :, 1], par[:, 0, R_CC:R_CC + 8], ACT.Silu).then_inc(*does("silu_c", 0))
            round_weights(-1)

            def norm(L, which, a):
                for k in range(KD):
                    if which == 2:
                        round_weights(order[(L, "out", k)])
                        act.wait_ge(*read((L, "out", k)))
                    elif L:
                        round_weights(order[(L - 1, "w2", 3, k)])
                        act.wait_ge(*read((L - 1, "w2", 3, k)))
                    elif k == 0:
                        for t in range(NT):
                            round_weights(order[("x", t)])
                            act.wait_ge(*read(("x", t)))
                    if k >= 2:
                        act.wait_ge(*when("square_added", ((L, which), max(1, k - 2))))
                    A_(act_r[:, k % 2, a:TOK], x[:, k, a:TOK], ACT.Square).then_inc(
                        *does("x_squared", ((L, which), k)))
                key = (L, "ms", which)
                round_weights(order[key] - 1)
                act.wait_ge(*full(key))
                A_(sdev[:, a:TOK], cols(key, a), ACT.Sqrt, bias=epsc[:, :]).then_inc(*frees(key))
                round_weights(order[key])
                if (L, which) == (0, 1):
                    round_weights(order[0, "ada", ADA_FIRST[-1]])
                if L < DEPTH:
                    for k in range(KD):
                        act.wait_ge(*when("h", (L, which, k)))
                        A_(h_hi[:, k, a:TOK], sqx[:, k, a:TOK], ACT.Copy).then_inc(*does("h_hi", (L, which, k)))

            def latent(L):
                a = first(L)
                round_weights(order[L, "kva", 0])
                act.wait_ge(*when("x_stored", L))
                for f in range(2):
                    key = (L, "kva", f)
                    round_weights(order[key] - 1)
                    act.wait_ge(*full(key))
                    A_(sql[:, f, :], cols(key, 0), ACT.Square).then_inc(*does("kv_squared", (L, f)))
                    A_(lraw[:, f, :], cols(key, 0), ACT.Copy).then_inc(*frees(key))
                    round_weights(order[key])
                key = (L, "kr")
                round_weights(order[key] - 1)
                act.wait_ge(*full(key))
                A_(dtT, cols(key, 0, 0, 32), ACT.Copy)
                A_(kT[NOPE:QH, 0, :], cols(key, 0, NOPE, QH), ACT.Copy).then_inc(*does("kr_copied", L))
                A_(kT[NOPE:QH, 1, :], cols(key, 0, NOPE, QH), ACT.Copy).then_inc(*frees(key))
                round_weights(order[key])
                key = (L, "kvms")
                round_weights(order[key] - 1)
                act.wait_ge(*full(key))
                A_(sdev[:, :], cols(key, 0), ACT.Sqrt, bias=epsc[:, :]).then_inc(*frees(key))
                round_weights(order[key])
                for f in range(3):
                    key = (L, "qa", f)
                    round_weights(order[key] - 1)
                    act.wait_ge(*full(key))
                    A_(lraw[:, 2 + f, a:TOK], cols(key, a), ACT.Copy).then_inc(*frees(key))
                    round_weights(order[key])
                    if f < 2:
                        act.wait_ge(*when("kvn", (L, f)))
                        A_(ln_hi[:, f, :], lraw[:, f, :], ACT.Copy).then_inc(*does("kvn_hi", (L, f)))
                act.wait_ge(*read((L, "qa", 2)))
                for f in range(3):
                    A_(sql[:, f, a:TOK], lraw[:, 2 + f, a:TOK], ACT.Square).then_inc(*does("q_squared", (L, f)))
                for pair in range(HEADS // 2):
                    key = (L, "k", pair)
                    round_weights(order[key] - 1)
                    act.wait_ge(*full(key))
                    A_(kT[0:NOPE, 2 * pair, :], cols(key, 0, 0, NOPE), ACT.Copy)
                    A_(kT[0:NOPE, 2 * pair + 1, :], cols(key, 0, NOPE, P), ACT.Copy).then_inc(*frees(key))
                    round_weights(order[key])
                    if pair == 1:
                        key = (L, "qms")
                        round_weights(order[key] - 1)
                        act.wait_ge(*full(key))
                        A_(sdev[:, a:TOK], cols(key, a), ACT.Sqrt, bias=epsc[:, :]).then_inc(*frees(key))
                        round_weights(order[key])
                key = (L, "v", 1, NT // 2 - 1)
                round_weights(order[key] - 1)
                act.wait_ge(*full(key))
                for f in range(3):
                    act.wait_ge(*when("qn", (L, f)))
                    A_(ln_hi[:, f, a:TOK], lraw[:, 2 + f, a:TOK], ACT.Copy).then_inc(*does("qn_hi", (L, f)))
                for h in range(HEADS):
                    key = (L, "q", h)
                    round_weights(order[key] - 1)
                    act.wait_ge(*full(key))
                    A_(qT[0:QH, h, a:TOK], cols(key, a, 0, QH), ACT.Copy, scale=SCALE).then_inc(
                        *does("q_copied", (L, h)))

            def attention(L):
                items = att_items(L)
                for n in range(len(items) + 3):
                    if n < len(items):
                        h, qt = items[n]
                        key = (L, "s", h, qt)
                        end = CTX if qt < 2 else TOK
                        act.wait_ge(*when("row_max", (L, h, qt)))
                        if n >= 2:
                            act.wait_ge(*full((L, "pT") + items[n - 2]))
                        A_(probs[n % 2][:, 0:end], slot(key)[:, T0:T0 + end], ACT.Exp, bias=rmax[:, n % 2:n % 2 + 1],
                           accum_out=rsum[:, n % 2:n % 2 + 1]).then_inc(*frees(key))
                        round_weights(order[key])
                    if n >= 3 and items[n - 3][1] == NT - 1:
                        h = items[n - 3][0]
                        lo = (h % 2) * VD
                        round_weights(order[L, "o", h] - 1)
                        act.wait_ge(*full((L, "o", h)))
                        A_(br_hi[lo:lo + VD, h // 2, first(L):TOK], cols((L, "o", h), first(L), lo, lo + VD),
                           ACT.Copy).then_inc(*does("values_hi", (L, h)))
                    if 2 <= n < len(items) + 2:
                        h, qt = items[n - 2]
                        key = (L, "pT", h, qt)
                        act.wait_ge(*full(key))
                        nk = 2 if qt < 2 else NT
                        A_(pT[:, 0:nk, qt * P:(qt + 1) * P],
                           slot(key)[:, 0:nk * P].rearrange("p (k q) -> p k q", k=nk), ACT.Copy).then_inc(*frees(key))
                        round_weights(order[key])

            def branch_hi(L, k, f, src):
                A_(br_hi[:, f, first(L):TOK], src[:, first(L):TOK], ACT.Copy).then_inc(*does("branch_hi", (L, k, f)))

            def gate(L, k, f, before):
                a = first(L)
                key = (L, "gate", k, f)
                round_weights(order[key] - 1)
                act.wait_ge(*full(key))
                if before:
                    round_weights(order[before])
                    act.wait_ge(*read(before))
                A_(sigm[:, f % 2, a:TOK], cols(key, a), ACT.Sigmoid).then_inc(*frees(key))
                round_weights(order[key])

            def merge(L, k):
                for f in range(KD):
                    if f >= 2:
                        gate(L, k, f, (L, "proj", k, f - 2))
                    elif k == 3:
                        gate(L, k, f, (L, "yT", NT - 1))
                    else:
                        gate(L, k, f, (L, "proj", k - 1, f + 6) if k else None)

            def short_conv(L):
                a = first(L)
                for f in range(KB + 1):
                    if f < KB:
                        key = (L, "cg", f)
                        round_weights(order[key] - 1)
                        act.wait_ge(*full(key))
                        if f >= 2:
                            round_weights(order[(L, "xin", f - 2)])
                            act.wait_ge(*read((L, "xin", f - 2)))
                        A_(cgs[:, f % 2, a:TOK], cols(key, a), ACT.Copy).then_inc(*frees(key))
                        round_weights(order[key])
                    if f >= 1:
                        round_weights(order[(L, "bg", f - 1)])
                        act.wait_ge(*read((L, "bg", f - 1)))
                        branch_hi(L, 1, f - 1, cvo[:, (f - 1) % 2, :])

            def ada_place_free(L, k):
                if L == 0:
                    act.wait_ge(*when("ada_ksum", ada_after[0, "gate", k, KD - 1] + 1))

            def fourier(L):
                a = first(L)
                round_weights(order[L, "proj", 1, KD - 1])
                act.wait_ge(*full((L, "proj", 1, KD - 1)))
                ada_place_free(L, 1)
                act.dma_start(dft.rearrange("p a j t -> p a (j t)"),
                              A["dft"].rearrange("a (j p) t -> p a j t", p=P)).then_inc(
                    *does("dft_loaded", L, 16))
                A_(ch_hi[:, :], cst[:, C_CHAN:C_CHAN + 256], ACT.Copy).then_inc(*does("channel_hi", L))

                def out_hi(g):
                    key = (L, "fo", g)
                    round_weights(order[key] - 1)
                    act.wait_ge(*full(key))
                    for _, _, t0, nt, _, scale in fourier_parts(L):
                        ins = A_(br_hi[:, g, t0:t0 + nt], slot(key)[:, T0 + t0:T0 + t0 + nt], ACT.Copy, scale=scale)
                    ins.then_inc(*does("fourier_hi", (L, g)))

                for g in range(4):
                    if g == 0:
                        round_weights(order[L, "fn", 0] - 1)
                        act.wait_ge(*full((L, "fn", 0)))
                    A_(fn_hi[:, a:TOK], cols((L, "fn", g), a), ACT.Copy).then_inc(*does("fn_hi", (L, g)))
                    if g >= 1:
                        out_hi(g - 1)
                    for tp in range(a // CTX, NT // 2):
                        key = (L, "fy", g, tp)
                        round_weights(order[key] - 1)
                        act.wait_ge(*full(key))
                        A_(fy[:, 2 * tp:2 * tp + 2, :],
                                slot(key).rearrange("p (a b) -> p a b", b=HALF)[:, :, 0:256], ACT.Copy).then_inc(
                                    *frees(key))
                        round_weights(order[key])
                    if g < 3:
                        round_weights(order[L, "fn", g + 1] - 1)
                        act.wait_ge(*full((L, "fn", g + 1)))
                out_hi(3)

            def ssd(L):
                a = first(L)
                for f in range(KD):
                    if 1 <= f <= 4:
                        round_weights(order[L, "xT", f - 1] - 1)
                        act.wait_ge(*full((L, "xT", f - 1)))
                    round_weights(order[(L, "xbc", f)])
                    act.wait_ge(*read((L, "xbc", f)))
                    A_(conv if f < 4 else bc[:, f - 4, :], cacc[f % 2][:, :], ACT.Silu).then_inc(
                        *does("conv_silu", (L, f)))
                    if f == 1:
                        act.wait_ge(*when("dt_abs", L))
                        A_(dts[:, 1, :, :, :], dts[:, 1, :, :, :], ACT.Exp, scale=-1.0).then_inc(*does("dt_exp", L))
                        A_(heads_bc[:, L, 0:16], heads_bc[:, L, 0:16], ACT.Exp).then_inc(*does("rates", L))
                    if f == 2:
                        act.wait_ge(*when("dt_one", L))
                        A_(dts[:, 4, :, :, :], dts[:, 2, :, :, :], ACT.Ln).then_inc(*does("dt_ln", L))
                round_weights(order[(L, "tot")])
                act.wait_ge(*read((L, "tot")))
                A_(ex[:, :, :, :, :].rearrange("p a d t h -> p (a d t h)"),
                        exin[:, :, :, :, :].rearrange("p a d t h -> p (a d t h)"), ACT.Exp).then_inc(*does("decays", L))
                for f in range(2):
                    key = (L, "z", f)
                    round_weights(order[key] - 1)
                    act.wait_ge(*full(key))
                    act.wait_ge(*read((L, "proj", 2, f + 6)))
                    A_(sigm[:, f, a:TOK], cols(key, a), ACT.Silu).then_inc(*frees(key))
                    round_weights(order[key])
                prev = None
                for d, c, want, has, gives in ssd_items(L):
                    if want:
                        round_weights(order[L, "seg", d, c])
                        act.wait_ge(*read((L, "seg", d, c)))
                        A_(diff.rearrange("p h i -> p (h i)"), diff.rearrange("p h i -> p (h i)"), ACT.Relu,
                           scale=-1.0).then_inc(*does("diff_cut", (L, d, c)))
                        act.wait_ge(*when("diff_cut", (L, d, c)))
                        if prev:
                            act.wait_ge(*full((L, "y") + prev))
                        A_(seg.rearrange("p h i -> p (h i)"), diff.rearrange("p h i -> p (h i)"), ACT.Exp,
                           scale=-1.0).then_inc(
                            *does("seg_exp", (L, d, c)))
                        prev = (d, c)
                for f in range(2, KB):
                    key = (L, "z", f)
                    round_weights(order[key] - 1)
                    act.wait_ge(*full(key))
                    A_(zs[:, f, a:TOK], cols(key, a), ACT.Silu).then_inc(*frees(key))
                    round_weights(order[key])
                round_weights(order[(L, "yT", NT - 1)])
                act.wait_ge(*read((L, "yT", NT - 1)))
                for f in range(KB):
                    A_(y_sq[:, f, a:TOK], zs[:, f, a:TOK], ACT.Square).then_inc(*does("y_squared", (L, f)))
                for g in range(2):
                    key = (L, "yms", g)
                    round_weights(order[key] - 1)
                    act.wait_ge(*full(key))
                    A_(sdev[:, a:TOK], cols(key, a), ACT.Sqrt, bias=epsc[:, :]).then_inc(*frees(key))
                    round_weights(order[key])
                    for f in range(2 * g, 2 * g + 2):
                        act.wait_ge(*when("branch", (L, 3, f)))
                        branch_hi(L, 3, f, zs[:, f, :])

            for L in range(DEPTH):
                a = first(L)
                norm(L, 1, 0)
                act.dma_start(x_spill, x.rearrange("p k t -> p (k t)")).then_inc(*does("x_stored", L, 16))
                latent(L)
                attention(L)
                merge(L, 0)
                short_conv(L)
                merge(L, 1)
                fourier(L)
                merge(L, 2)
                ssd(L)
                merge(L, 3)
                round_weights(order[L, "proj", 3, KD - 1] - 1)
                act.wait_ge(*full((L, "proj", 3, KD - 1)))
                act.dma_start(x.rearrange("p k t -> p (k t)"), x_spill).then_inc(*does("x_back", L, 16))
                for k in range(KD):
                    act.wait_ge(*when("merged", (L, 3, k)))
                    A_(h_hi[:, k, a:TOK], merged[:, k, a:TOK], ACT.Copy).then_inc(*does("merged_hi", (L, k)))
                norm(L, 2, a)
                for n in range(4 * KD):
                    c, f = divmod(n, KD)
                    key = (L, "w1", c, f)
                    round_weights(order[key] - 1)
                    act.wait_ge(*full(key))
                    if n >= 2:
                        act.wait_ge(*read((L, "w1") + divmod(n - 2, KD)))
                    A_(act_r[:, n % 2, a:TOK], cols(key, a), ACT.Relu).then_inc(*does("relu", (L, n)))
                    for m in [n - 1] * (f > 0) + [n] * (f == KD - 1):
                        round_weights(order[(L, "w1") + divmod(m, KD)])
                        act.wait_ge(*read((L, "w1") + divmod(m, KD)))
                        A_(f_hi[:, m % KD, a:TOK], act_f[m % 2][:, a:TOK], ACT.Copy).then_inc(*does("f_hi", (L, m)))
            norm(DEPTH, 1, CTX)
            for t in range(CTX // P, NT):
                key = ("y", t)
                round_weights(order[key] - 1)
                act.wait_ge(*full(key))
                if t >= 4:
                    act.wait_ge(*when(f"y_out{t % 2}", t - 2))
                A_(yout[:, t % 2, :], slot(key), ACT.Copy).then_inc(*frees(key))
                round_weights(order[key])
                act.wait_ge(*read(key))
                act.dma_start(out[0, t * P - CTX:(t + 1) * P - CTX, :], yout[:, t % 2, :]).then_inc(
                    *does(f"y_out{t % 2}", t, 16))
            for t in (NT - 2, NT - 1):
                act.wait_ge(*when(f"y_out{t % 2}", t))

        @block.vector
        def _(dve):
            def mul(o, a, b):
                return dve.tensor_tensor(o, a, b, ALU.mult)

            def lo(o, whole, hi):
                return dve.tensor_tensor(o, whole, hi.bitcast(F32), ALU.subtract)

            def fma(o, a, s, b, op0=ALU.mult, op1=ALU.add):
                return dve.scalar_tensor_tensor(o, a, s, b, op0, op1)

            dve.memset(parr[:, :, :], 0.0)
            dve.memset(epsc[:, :], EPS).then_inc(*does("cleared", 0))
            for i, v in enumerate((1.0, 1.0 / D, 1.0 / QR, 1.0 / KVR)):
                dve.memset(ones[:, i, :], v).then_inc(*does("dve_step"))
                dve.wait_ge(*mine())
            for t in range(NT):
                key = ("x", t)
                dve.wait_ge(*full(key))
                dve.tensor_copy(x[:, :, t * P:(t + 1) * P], slot(key).rearrange("p (k t) -> p k t", k=KD)).then_inc(
                    *frees(key))
            dve.wait_ge(*full("params"))
            dve.tensor_copy(adab.rearrange("p l f -> p (l f)"), slot("params")[:, DEPTH * P:DEPTH * P + 96]).then_inc(
                *does("dve_step"))
            dve.wait_ge(*mine())
            dve.tensor_copy(par.rearrange("p l f -> p (l f)"), slot("params")[:, 0:DEPTH * P]).then_inc(
                *frees("params"))
            def ada_first(f):
                dve.wait_ge(*full((0, "ada", f)))
                dve.tensor_tensor(mods[:, 0, f:f + 2, :],
                                  slot((0, "ada", f))[:, 0:4].rearrange("p (f v) -> p f v", v=2),
                                  adab[:, 0, f:f + 2].unsqueeze(2).to_broadcast([P, 2, 2]),
                                  ALU.add).then_inc(*frees((0, "ada", f)))

            def ada_ksum(n):
                if n == len(ADA_LATER):
                    return
                L, f = ADA_LATER[n]
                s = tile_of[L, "ada", f]
                w = raw[:, s % NRAW, :].rearrange("p (k c) -> p k c", k=KD)
                dve.wait_ge(*when(f"raw{s % NRAW}_loaded", s))
                if n >= 2:
                    dve.wait_ge(*full(("ada", n - 2)))
                for v in range(2):
                    mul(prod[:, :, :], w, silc[:, :, v:v + 1].to_broadcast([P, KD, P])).then_inc(
                        *does(*(("dve_step",) if v == 0 else ("ada_used", s))))
                    dve.wait_ge(*mine())
                    dve.reduce_sum(ksum[:, n % 2, v, :], prod.rearrange("p k c -> p c k"), AX.X).then_inc(
                        *does(*(("dve_step",) if v == 0 else ("ada_ksum", n))))
                    dve.wait_ge(*mine())

            def ada(after):
                if after in ada_after:
                    n = ada_after[after]
                    L, f = ADA_LATER[n]
                    dve.wait_ge(*full(("ada", n)))
                    dve.tensor_scalar(mods[:, L, f, :], slot(("ada", n))[:, 0:2], adab[:, L, f:f + 1], None,
                                      ALU.add).then_inc(*frees(("ada", n)))
                    ada_ksum(n + 1)

            def add_square(L, which, k, a):
                if k < 1:
                    return
                dve.wait_ge(*when("x_squared", ((L, which), k)))
                dve.wait_ge(*mine())
                before = act_r[:, 0, a:TOK] if k == 1 else rstd[:, a:TOK]
                dve.tensor_tensor(rstd[:, a:TOK], act_r[:, k % 2, a:TOK], before, ALU.add).then_inc(
                    *does("square_added", ((L, which), k)))

            def norm(L, which, a):
                key = (L, "ms", which)
                add_square(L, which, KD - 1, a)
                dve.wait_ge(*mine())
                dve.wait_ge(*read(key))
                dve.reciprocal(rstd[:, a:TOK], sdev[:, a:TOK]).then_inc(*does("rstd", (L, which)))
                dve.wait_ge(*mine())
                if L == DEPTH:
                    for k in range(KD):
                        fma(xf[:, k, a:TOK], x[:, k, a:TOK], par[:, 0, R_FG + k:R_FG + k + 1], rstd[:, a:TOK],
                            ALU.mult, ALU.mult).then_inc(*does("x_scaled", k))
                    return
                start = (L, which) == (0, 1)
                if start:
                    for k in range(KD):
                        mul(sqx[:, k, :], x[:, k, :], rstd[:, :]).then_inc(*does("dve_step"))
                        ada_first(2 * k)
                    dve.wait_ge(*mine())
                sh0, sc0, g0 = ((0, 8, R_N1), (24, 32, R_N2))[which - 1]
                fma(gsc[:, :, :], mods[:, L, sc0:sc0 + 8, :], 1.0,
                    par[:, L, g0:g0 + 8].unsqueeze(2).to_broadcast([P, 8, 2]), ALU.add,
                    ALU.mult).then_inc(*does("dve_step"))
                for k in range(KD + 1):
                    dve.wait_ge(*mine())
                    if k < KD:
                        if not start and k in SCALED_BY_POOL:
                            dve.wait_ge(*when("x_by_rstd", (L, which, k)))
                        elif not start:
                            mul(sqx[:, k, a:TOK], x[:, k, a:TOK], rstd[:, a:TOK]).then_inc(*does("dve_step"))
                            dve.wait_ge(*mine())
                        for b, e, v in kinds(a):
                            ins = dve.tensor_scalar(sqx[:, k, b:e], sqx[:, k, b:e], gsc[:, k, v:v + 1],
                                                    mods[:, L, sh0 + k, v:v + 1], ALU.mult, ALU.add)
                            if e == TOK:
                                ins.then_inc(*does("h", (L, which, k)))
                            else:
                                ins.then_inc(*does("dve_step"))
                                dve.wait_ge(*mine())
                    if k:
                        dve.wait_ge(*when("h_hi", (L, which, k - 1)))
                        lo(h_lo[:, k - 1, a:TOK], sqx[:, k - 1, a:TOK],
                           h_hi[:, k - 1, a:TOK]).then_inc(*does("h_lo", (L, which, k - 1)))

            def latent_norm(L, key, tiles_, g0, a, name):
                dve.wait_ge(*mine())
                dve.wait_ge(*read(key))
                dve.reciprocal(rstd[:, a:TOK], sdev[:, a:TOK]).then_inc(*does("dve_step"))
                dve.wait_ge(*mine())
                for f, src in enumerate(tiles_):
                    fma(lraw[:, src, a:TOK], lraw[:, src, a:TOK], par[:, L, g0 + f:g0 + f + 1], rstd[:, a:TOK],
                        ALU.mult, ALU.mult).then_inc(*does(name + "n", (L, f)))

            def latent_lo(L, tiles_, a, name):
                for f, src in enumerate(tiles_):
                    dve.wait_ge(*when(name + "n_hi", (L, f)))
                    lo(ln_lo[:, f, a:TOK], lraw[:, src, a:TOK],
                       ln_hi[:, f, a:TOK]).then_inc(*does(name + "n_lo", (L, f)))

            def latent(L):
                a = first(L)
                cos, sin = cst[NOPE:QH, C_COS:C_COS + TOK], cst[NOPE:QH, C_SIN:C_SIN + TOK]
                key = (L, "krot")
                dve.wait_ge(*full(key))
                dve.wait_ge(*read((L, "kr")))
                mul(kT[NOPE:QH, 2, :], cols(key, 0, NOPE, QH), sin).then_inc(*frees(key))
                mul(kT[NOPE:QH, 1, :], kT[NOPE:QH, 1, :], cos).then_inc(*does("dve_step"))
                dve.wait_ge(*mine())
                latent_norm(L, (L, "kvms"), (0, 1), R_KG, 0, "kv")
                latent_lo(L, (0, 1), 0, "kv")
                dve.tensor_tensor(kT[NOPE:QH, 3, :], kT[NOPE:QH, 1, :], kT[NOPE:QH, 2, :], ALU.add).then_inc(
                    *does("dve_step"))
                dve.wait_ge(*mine())
                key = (L, "dtT")
                dve.wait_ge(*full(key))
                dve.tensor_copy(dt_raw[:, :, :],
                                slot(key)[:, 0:32 * NT].rearrange("p (t c) -> p t c", c=32)[:, :, 0:16]).then_inc(
                                    *frees(key))
                for h0, h1 in ((0, 3), (4, HEADS)):
                    ins = dve.tensor_copy(kT[NOPE:QH, h0:h1, :],
                                          kT[NOPE:QH, 3:4, :].to_broadcast([ROPE, h1 - h0, TOK]))
                    ins.then_inc(*does("k_rotated", L))
                for i in range(2):
                    if i == 1:
                        latent_norm(L, (L, "qms"), (2, 3, 4), R_QG, a, "q")
                    for tp in range(NT // 2):
                        key = (L, "v", i, tp)
                        dve.wait_ge(*full(key))
                        dve.tensor_copy(vt[:, 2 * tp:2 * tp + 2, 256 * i:256 * i + 256],
                                             slot(key).rearrange("p (a b) -> p a b", b=HALF)[:, :, 0:256]).then_inc(
                                                 *frees(key))
                latent_lo(L, (2, 3, 4), a, "q")
                for h in range(HEADS):
                    dve.wait_ge(*mine())
                    dve.wait_ge(*when("q_copied", (L, h)))
                    ins = dve.tensor_copy(rrec[0:1, 0:1], slot((L, "q", h))[0:1, 0:1])
                    ins.then_inc(*frees((L, "q", h)))
                    key = (L, "qrot", h)
                    dve.wait_ge(*full(key))
                    mul(lraw[NOPE:QH, 0, a:TOK], cols(key, a, NOPE, QH), sin[:, a:TOK]).then_inc(*frees(key))
                    mul(qT[NOPE:QH, h, a:TOK], qT[NOPE:QH, h, a:TOK], cos[:, a:TOK]).then_inc(*does("dve_step"))
                    dve.wait_ge(*mine())
                    dve.tensor_tensor(qT[NOPE:QH, h, a:TOK], qT[NOPE:QH, h, a:TOK], lraw[NOPE:QH, 0, a:TOK],
                                           ALU.add).then_inc(*does("q_rotated", (L, h)))

            def attention(L):
                items = att_items(L)
                for n in range(len(items) + 3):
                    dve.wait_ge(*mine())
                    if n < len(items):
                        h, qt = items[n]
                        key = (L, "s", h, qt)
                        end = CTX if qt < 2 else TOK
                        dve.wait_ge(*full(key))
                        if n >= 2:
                            dve.wait_ge(*read((L, "s") + items[n - 2]))
                        dve.reduce_max(rmax[:, n % 2:n % 2 + 1], slot(key)[:, T0:T0 + end], AX.X, negate=True).then_inc(
                            *does("row_max", (L, h, qt)))
                    if 1 <= n <= len(items):
                        h, qt = items[n - 1]
                        i = (n - 1) % 2
                        end = CTX if qt < 2 else TOK
                        dve.wait_ge(*read((L, "s", h, qt)))
                        dve.reciprocal(rrec[:, i:i + 1], rsum[:, i:i + 1]).then_inc(*does("dve_step"))
                        dve.wait_ge(*mine())
                        dve.tensor_scalar(probs[i][:, 0:end], probs[i][:, 0:end], rrec[:, i:i + 1], None,
                                          ALU.mult).then_inc(
                            *does("probs", (L, h, qt)))
                    if n >= 3 and items[n - 3][1] == NT - 1:
                        h = items[n - 3][0]
                        p = (h % 2) * VD
                        dve.wait_ge(*when("values_hi", (L, h)))
                        lo(br_lo[p:p + VD, h // 2, first(L):TOK], cols((L, "o", h), first(L), p, p + VD),
                                br_hi[p:p + VD, h // 2, first(L):TOK]).then_inc(*frees((L, "o", h)))

            def branch_lo(L, k, f, src):
                a = first(L)
                dve.wait_ge(*when("branch_hi", (L, k, f)))
                lo(br_lo[:, f, a:TOK], src[:, a:TOK], br_hi[:, f, a:TOK]).then_inc(*does("branch_lo", (L, k, f)))

            def merge(L, k):
                a = first(L)
                if (L, k) == (0, 0):
                    dve.wait_ge(*mine())
                    ada_ksum(0)
                for f in range(KD):
                    if f % 2 == 0:
                        ada((L, "gate", k, f))
                        ada((L, "gate", k, f + 1))
                    key = (L, "proj", k, f)
                    dve.wait_ge(*mine())
                    dve.wait_ge(*full(key))
                    dve.wait_ge(*read((L, "gate", k, f)))
                    if k == 0:
                        mul(merged[:, f, a:TOK], cols(key, a), sigm[:, f % 2, a:TOK]).then_inc(*frees(key))
                    else:
                        mul(gated[:, a:TOK], cols(key, a), sigm[:, f % 2, a:TOK]).then_inc(*frees(key))
                        dve.wait_ge(*read(key))
                        dve.tensor_tensor(merged[:, f, a:TOK], merged[:, f, a:TOK], gated[:, a:TOK], ALU.add).then_inc(
                            *does("merged", (L, k, f)))

            def convolve(o, src, taps, width, bias, a, signal):
                mid = width // 2
                steps = []
                if bias is None:
                    dve.tensor_scalar(o[:, a:TOK], src(a, TOK), taps(mid), None, ALU.mult).then_inc(*does("dve_step"))
                    dve.wait_ge(*mine())
                else:
                    dve.tensor_scalar(o[:, a:TOK], src(a, TOK), taps(mid), bias, ALU.mult, ALU.add).then_inc(
                        *does("dve_step"))
                    dve.wait_ge(*mine())
                for k in [k for k in range(width) if k != mid]:
                    s = k - mid
                    for b, e, _ in kinds(a):
                        steps.append((b + max(0, -s), e - max(0, s), s, k))
                for n, (b, e, s, k) in enumerate(steps):
                    ins = fma(o[:, b:e], src(b + s, e + s), taps(k), o[:, b:e])
                    if n < len(steps) - 1:
                        ins.then_inc(*does("dve_step"))
                        dve.wait_ge(*mine())
                ins.then_inc(*signal())

            def short_conv(L):
                a = first(L)
                for f in range(KB):
                    key = (L, "xin", f)
                    dve.wait_ge(*mine())
                    dve.wait_ge(*full(key))
                    dve.wait_ge(*read((L, "cg", f)))
                    g, o = cgx[:, f % 2, :], cvo[:, f % 2, :]
                    mul(g[:, a:TOK], cols(key, a), cgs[:, f % 2, a:TOK]).then_inc(*frees(key))
                    dve.wait_ge(*read(key))
                    convolve(o, lambda b, e: g[:, b:e], lambda k: par[:, L, R_SW + 4 * k + f:R_SW + 4 * k + f + 1], 3,
                             None, a, lambda: does("dve_step"))
                    dve.wait_ge(*mine())
                    key = (L, "bg", f)
                    dve.wait_ge(*full(key))
                    mul(o[:, a:TOK], cols(key, a), o[:, a:TOK]).then_inc(*frees(key))
                    branch_lo(L, 1, f, o)

            def fourier(L):
                a = first(L)
                dve.wait_ge(*when("channel_hi", L))
                lo(ch_lo[:, :], cst[:, C_CHAN:C_CHAN + 256], ch_hi[:, :]).then_inc(*does("channel_dft", L))
                for g in range(5):
                    dve.wait_ge(*mine())
                    if g < 4:
                        key = (L, "fn", g)
                        dve.wait_ge(*when("fn_hi", (L, g)))
                        lo(fn_lo[:, a:TOK], cols(key, a), fn_hi[:, a:TOK]).then_inc(*frees(key))
                    if g >= 1:
                        key = (L, "fo", g - 1)
                        dve.wait_ge(*when("fourier_hi", (L, g - 1)))
                        parts = fourier_parts(L)
                        for n, (_, _, t0, nt, _, scale) in enumerate(parts):
                            ins = fma(br_lo[:, g - 1, t0:t0 + nt], slot(key)[:, T0 + t0:T0 + t0 + nt], scale,
                                      br_hi[:, g - 1, t0:t0 + nt].bitcast(F32), ALU.mult, ALU.subtract)
                            if n < len(parts) - 1:
                                ins.then_inc(*does("dve_step"))
                                dve.wait_ge(*mine())
                        ins.then_inc(*frees(key))

            def steps(L):
                for d in range(2):
                    bias = heads_bc[:, L, 16 + 8 * d:24 + 8 * d].unsqueeze(1).to_broadcast([P, NT, 8])
                    dve.tensor_tensor(dts[:, 0, d, :, :], dt_raw[:, :, 8 * d:8 * d + 8], bias,
                                      ALU.add).then_inc(*does("dve_step"))
                    dve.wait_ge(*mine())
                v = [dts[:, i, :, :, :].rearrange("p d t h -> p (d t h)") for i in range(6)]
                fma(v[1], v[0], -1.0, v[0], ALU.mult, ALU.max).then_inc(*does("dt_abs", L))

            def steps_one(L):
                v = [dts[:, i, :, :, :].rearrange("p d t h -> p (d t h)") for i in range(6)]
                dve.wait_ge(*when("dt_exp", L))
                dve.tensor_scalar(v[2], v[1], 1.0, None, ALU.add).then_inc(*does("dt_one", L))
                dve.wait_ge(*when("dt_one", L))
                dve.tensor_scalar(v[3], v[2], -1.0, None, ALU.add).then_inc(*does("dve_step"))
                dve.wait_ge(*mine())
                dve.tensor_scalar(v[5], v[3], 0.0, None, ALU.is_equal).then_inc(*does("dve_step"))

            def steps_end(L):
                v = [dts[:, i, :, :, :].rearrange("p d t h -> p (d t h)") for i in range(6)]
                dve.wait_ge(*when("dt_ln", L))
                dve.tensor_tensor(v[4], v[4], v[5], ALU.add).then_inc(*does("dve_step"))
                dve.wait_ge(*mine())
                mul(v[4], v[4], v[1]).then_inc(*does("dve_step"))
                dve.wait_ge(*mine())
                dve.tensor_tensor(v[3], v[3], v[5], ALU.add).then_inc(*does("dve_step"))
                dve.wait_ge(*mine())
                dve.reciprocal(v[2], v[3]).then_inc(*does("dve_step"))
                dve.wait_ge(*mine())
                mul(v[4], v[4], v[2]).then_inc(*does("dve_step"))
                dve.wait_ge(*mine())
                fma(v[0], v[0], 0.0, v[4], ALU.max, ALU.add).then_inc(*does("dve_step"))
                dve.wait_ge(*mine())
                for d in range(2):
                    rate = heads_bc[:, L, 8 * d:8 * d + 8].unsqueeze(1).to_broadcast([P, NT, 8])
                    fma(dts[:, 3, d, :, :], dts[:, 0, d, :, :], -1.0, rate, ALU.mult, ALU.mult).then_inc(*does("la", L))

            def running_sums(L):
                key = (L, "laT")
                dve.wait_ge(*full(key))
                for d in range(2):
                    rows = slice(64 * d, 64 * d + ROWS)
                    ins = dve.tensor_copy(laR[rows, :] if d == 0 else laR[rows, ::-1], slot(key)[rows, 0:P])
                    if d == 0:
                        ins.then_inc(*does("dve_step"))
                        dve.wait_ge(*mine())
                ins.then_inc(*frees(key))
                dve.wait_ge(*read(key))
                for d in range(2):
                    rows = slice(64 * d, 64 * d + ROWS)
                    o = diff[rows, 0, :]
                    keep = cst[rows, C_KEEP:C_KEEP + P]
                    dve.tensor_tensor_scan(o, keep, laR[rows, :], 0.0, ALU.mult, ALU.add).then_inc(*does("dve_step"))
                    dve.wait_ge(*mine())
                    ends = diff[rows, 0, SUM_BLOCK - 1:P:SUM_BLOCK]
                    dve.tensor_tensor_scan(blkR[rows, :], ones[rows, 0, 0:P // SUM_BLOCK], ends, 0.0,
                                                ALU.mult, ALU.add).then_inc(*does("dve_step"))
                    dve.wait_ge(*mine())
                    dve.tensor_tensor(diff[rows, 0, SUM_BLOCK:P].rearrange("p (b i) -> p b i", i=SUM_BLOCK),
                                           diff[rows, 0, SUM_BLOCK:P].rearrange("p (b i) -> p b i", i=SUM_BLOCK),
                                           blkR[rows, 0:P // SUM_BLOCK - 1].unsqueeze(2).to_broadcast(
                                               [ROWS, P // SUM_BLOCK - 1, SUM_BLOCK]), ALU.add).then_inc(
                                                   *does("dve_step"))
                    dve.wait_ge(*mine())
                    dve.tensor_copy(cumR[rows, :], o if d == 0 else diff[rows, 0, ::-1]).then_inc(*does("cum_rows", L))
                dve.wait_ge(*mine())

            def ssd(L):
                a = first(L)
                for f in range(KD + 1):
                    dve.wait_ge(*mine())
                    if f < KD:
                        key = (L, "xbc", f)
                        dve.wait_ge(*full(key))
                        if f >= 2:
                            dve.wait_ge(*when("conv_silu", (L, f - 2)))
                        if f == 1:
                            steps(L)
                        if f == 2:
                            steps_one(L)
                        if f == 4:
                            steps_end(L)
                        if f == 6:
                            running_sums(L)
                        if f == 7:
                            key = (L, "cum")
                            dve.wait_ge(*full(key))
                            dve.tensor_copy(exin[:, 0, :, :, :].rearrange("p d t h -> p d (t h)"),
                                            slot(key).rearrange("p (d c) -> p d c", d=2)[:, :, 0:ROWS]).then_inc(
                                                *frees(key))
                            dve.wait_ge(*mine())
                        key = (L, "xbc", f)
                        convolve(cacc[f % 2], lambda b, e: slot(key)[:, T0 + b:T0 + e],
                                 lambda k: par[:, L, R_CW + 8 * k + f:R_CW + 8 * k + f + 1], 5,
                                 par[:, L, R_CB + f:R_CB + f + 1], 0, lambda: frees(key))
                    if 1 <= f <= 6:
                        key = (L, "xT", f - 1)
                        dve.wait_ge(*full(key))
                        dst = xs_tok[:, :, (f - 1) * P:f * P] if f - 1 < 4 else b_tok[:, :, (f - 5) * P:(f - 4) * P]
                        dve.tensor_copy(dst, slot(key)[:, 0:TOK].rearrange("p (t c) -> p t c", t=NT)).then_inc(
                            *frees(key))
                def by_head(ap, n=64):
                    return ap.rearrange("p (h c) -> p h c", c=n)

                def wide(ap, n=64):
                    return ap.unsqueeze(2).to_broadcast([P, 8, n])

                sums = [exin[:, i, :, :, :].rearrange("p d t h -> p (d t h)") for i in range(3)]
                key = (L, "tot")
                dve.wait_ge(*full(key))
                dve.tensor_copy(sums[2], slot(key)[:, 0:2 * ROWS]).then_inc(*does("dve_step"))
                dve.wait_ge(*mine())
                dve.tensor_tensor(sums[1], slot(key)[:, 0:2 * ROWS], sums[0], ALU.subtract).then_inc(*frees(key))
                dve.wait_ge(*when("decays", L))
                mul(dterm[:, :, :, :].rearrange("p d t h -> p (d t h)"),
                         dts[:, 0, :, :, :].rearrange("p d t h -> p (d t h)"),
                         ex[:, 1, :, :, :].rearrange("p d t h -> p (d t h)")).then_inc(*does("dterm", L))
                dve.wait_ge(*mine())
                items = ssd_items(L)

                def prepare(n):
                    d, c, want, has, gives = items[n]
                    if not want:
                        return
                    key = (L, "cb", d, c)
                    mask = cst[:, (C_U, C_L)[d]:(C_U, C_L)[d] + P].unsqueeze(1).to_broadcast([P, 2, P])
                    dve.wait_ge(*full(key))
                    mul(cbm[:, n % 2, :, :], slot(key)[:, 0:256].rearrange("p (g i) -> p g i", g=2),
                        mask).then_inc(*frees(key))
                    before = [i for i in items[:n] if i[2]]
                    if before:
                        dve.wait_ge(*when("seg_exp", (L,) + before[-1][0:2]))
                    key = (L, "seg", d, c)
                    dve.wait_ge(*full(key))
                    dve.tensor_tensor(diff[:, :, :], slot(key).rearrange("p (h i) -> p h i", h=8),
                                      wide(exin[:, 0, d, c, :], P), ALU.subtract).then_inc(*frees(key))

                def state(n):
                    d, c, want, has, gives = items[n]
                    if not gives:
                        return
                    key = (L, "state", d, c)
                    dve.wait_ge(*full(key))
                    if has:
                        dve.wait_ge(*when("decayed", (L, d, c)))
                        dve.tensor_tensor(st[:, n % 2, :], slot(key)[:, 0:BW], decayed[:, :],
                                          ALU.add).then_inc(*frees(key))
                    else:
                        dve.tensor_copy(st[:, n % 2, :], slot(key)[:, 0:BW]).then_inc(*frees(key))

                prepare(0)
                state(0)
                for n, (d, c, want, has, gives) in enumerate(items):
                    dve.wait_ge(*mine())
                    if want:
                        dve.wait_ge(*when("seg_exp", (L, d, c)))
                        for g in range(2):
                            mul(seg[:, 4 * g:4 * g + 4, :], seg[:, 4 * g:4 * g + 4, :],
                                cbm[:, n % 2, g:g + 1, :].to_broadcast([P, 4, P])).then_inc(
                                    *does("seg_masked", (L, d, c)))
                    if n + 1 < len(items):
                        prepare(n + 1)
                    key = (L, "y", d, c)
                    if want:
                        dve.wait_ge(*full(key))
                    if n + 1 < len(items):
                        state(n + 1)
                    if want:
                        dve.wait_ge(*when("skip", (L, c)))
                        dve.wait_ge(*mine())
                        if has:
                            mul(by_head(yo[:, :]), by_head(slot(key)[:, HALF:2 * HALF]),
                                wide(ex[:, 0, d, c, :])).then_inc(*does("dve_step"))
                            dve.wait_ge(*mine())
                            dve.tensor_tensor(y_tok[:, c, :], y_tok[:, c, :], yo[:, :],
                                              ALU.add).then_inc(*does("dve_step"))
                            dve.wait_ge(*mine())
                        dve.tensor_tensor(y_tok[:, c, :], slot(key)[:, 0:BW], y_tok[:, c, :],
                                          ALU.add).then_inc(*frees(key))
                for f in range(KB):
                    dve.wait_ge(*read((L, "z", f)))
                for c in range(a // P, NT):
                    key = (L, "yT", c)
                    dve.wait_ge(*full(key))
                    y = slot(key)[:, 0:BW].rearrange("p (f t) -> p f t", f=KB)
                    mul(zs[:, 0:2, c * P:(c + 1) * P], y[:, 0:2, :],
                        sigm[:, :, c * P:(c + 1) * P]).then_inc(*does("dve_step"))
                    mul(zs[:, 2:4, c * P:(c + 1) * P], y[:, 2:4, :],
                        zs[:, 2:4, c * P:(c + 1) * P]).then_inc(*frees(key))
                for g in range(2):
                    dve.wait_ge(*mine())
                    dve.wait_ge(*read((L, "yms", g)))
                    dve.reciprocal(rstd[:, a:TOK], sdev[:, a:TOK]).then_inc(*does("dve_step"))
                    dve.wait_ge(*mine())
                    for f in range(2 * g, 2 * g + 2):
                        fma(zs[:, f, a:TOK], zs[:, f, a:TOK], par[:, L, R_SN + f:R_SN + f + 1], rstd[:, a:TOK],
                                 ALU.mult, ALU.mult).then_inc(*does("branch", (L, 3, f)))
                    for f in range(2 * g, 2 * g + 2):
                        branch_lo(L, 3, f, zs[:, f, :])

            def residual(L, key, f, gate, a):
                dve.wait_ge(*mine())
                dve.wait_ge(*full(key))
                for b, e, v in kinds(a):
                    ins = fma(x[:, f, b:e], slot(key)[:, T0 + b:T0 + e], mods[:, L, gate + f, v:v + 1], x[:, f, b:e])
                    if e < TOK:
                        ins.then_inc(*does("dve_step"))
                        dve.wait_ge(*mine())
                ins.then_inc(*frees(key))

            for L in range(DEPTH):
                a = first(L)
                if L == 0:
                    for k in range(KD - 1):
                        add_square(0, 1, k, 0)
                norm(L, 1, 0)
                latent(L)
                attention(L)
                merge(L, 0)
                short_conv(L)
                merge(L, 1)
                fourier(L)
                merge(L, 2)
                ssd(L)
                merge(L, 3)
                for k in range(KD):
                    dve.wait_ge(*when("merged_hi", (L, k)))
                    lo(h_lo[:, k, a:TOK], merged[:, k, a:TOK], h_hi[:, k, a:TOK]).then_inc(*does("merged_lo", (L, k)))
                dve.wait_ge(*when("x_back", L))
                for f in range(KD):
                    residual(L, (L, "out", f), f, 16, a)
                    add_square(L, 2, f - 1, a)
                norm(L, 2, a)
                for c in range(4):
                    for f in range(KD + 1):
                        dve.wait_ge(*mine())
                        if f < KD:
                            n = c * KD + f
                            key = (L, "w1", c, f)
                            dve.wait_ge(*when("relu", (L, n)))
                            mul(act_f[n % 2][:, a:TOK], cols(key, a), act_r[:, n % 2, a:TOK]).then_inc(*frees(key))
                            ada(key)
                        if f:
                            m = c * KD + f - 1
                            dve.wait_ge(*when("f_hi", (L, m)))
                            lo(f_lo[:, f - 1, a:TOK], act_f[m % 2][:, a:TOK], f_hi[:, f - 1, a:TOK]).then_inc(
                                *does("f_lo", (L, c, f - 1)))
                    for f in range(KD):
                        residual(L, (L, "w2", c, f), f, 40, a)
                        if c == 3:
                            add_square(L + 1, 1, f - 1, first(L) if L + 1 < DEPTH else CTX)
                        ada((L, "w2", c, f))
            norm(DEPTH, 1, CTX)
        return counts.table


_NAMES = ["x", "c", "ctx", "c_ctx", "ada_w", "ada_b", "norm1_g", "norm2_g", "w_in", "ssm_conv_w", "ssm_conv_b",
          "ssm_a_log", "ssm_dt_bias", "ssm_d", "ssm_norm_g", "sc_conv_w", "mla_qa_g", "mla_wqb", "mla_kva_g",
          "mla_wkvb", "w_branch", "w_out", "mlp_w1", "mlp_w2", "final_norm_g"]


def kernel(**inputs):
    import numpy as _np
    import concourse.bacc as _bacc
    from concourse.bass_utils import run_bass_kernel_spmd as _run

    tables, dft = constant_tables()
    given = {n: _np.ascontiguousarray(inputs[n]) for n in _NAMES}
    given["tables"], given["dft"] = tables, dft
    counts = None
    for _ in range(2):
        nc = _bacc.Bacc("TRN2", target_bir_lowering=False, num_devices=1)
        aps = {n: nc.dram_tensor(f"in_{n}_dram", a.shape, F32, kind="ExternalInput").ap() for n, a in given.items()}
        out = nc.dram_tensor("out_0_dram", (1, LAT, D), F32, kind="ExternalOutput").ap()
        counts = backbone(nc, aps, out, counts)
    r = _run(nc, [{f"in_{n}_dram": a for n, a in given.items()}], core_ids=[0])
    return r.results[0]["out_0_dram"]
```
